# Optimizing a Trainium2 kernel written in Bass

```python
import jax, jax.numpy as jnp
from jax import lax
import numpy as np
import math

D_MODEL = 1024
BATCH = 1
SEQ = 512
DEPTH = 1

MLA_HEADS = 8
MLA_NOPE = 64
MLA_ROPE = 32
MLA_QK = MLA_NOPE + MLA_ROPE
MLA_V = 64
MLA_W = MLA_HEADS * MLA_V
MLA_Q_RANK = 256
MLA_KV_RANK = 128
ROPE_THETA = 10000.0
Q_BLOCK = 128

RWKV_HEADS = 8
RWKV_N = 64
RWKV_W = RWKV_HEADS * RWKV_N
DECAY_LORA = 64
AAA_LORA = 64
GATE_LORA = 128

MIX_W = MLA_W + RWKV_W
MLA_IN = MLA_Q_RANK + MLA_KV_RANK + MLA_ROPE
RWKV_IN = 3 * RWKV_W + DECAY_LORA + AAA_LORA + GATE_LORA
IN_W = MLA_IN + RWKV_IN

N_GROUPS = 4
EXPERTS_PER_GROUP = 8
N_EXPERTS = N_GROUPS * EXPERTS_PER_GROUP
TOP_K = 2
D_EXPERT = 256

NORM_EPS = 1e-6
LNX_EPS = 64e-5


def rms_norm(x, g, eps=NORM_EPS):
    xf = x.astype(jnp.float32)
    y = xf * lax.rsqrt(jnp.mean(xf * xf, axis=-1, keepdims=True) + eps)
    return (y * g.astype(jnp.float32)).astype(x.dtype)

def rope_tables(positions):
    half = MLA_ROPE // 2
    inv_freq = 1.0 / (ROPE_THETA ** (jnp.arange(half, dtype=jnp.float32) / half))
    ang = positions.astype(jnp.float32)[..., None] * inv_freq
    return jnp.cos(ang)[:, :, None, :], jnp.sin(ang)[:, :, None, :]

def apply_rope(x, cos, sin):
    half = MLA_ROPE // 2
    xf = x.astype(jnp.float32)
    x1, x2 = xf[..., :half], xf[..., half:]
    return jnp.concatenate([x1 * cos - x2 * sin, x2 * cos + x1 * sin], axis=-1).astype(x.dtype)

def mla_group(c_q, c_kv, k_rope, positions, g_cq, w_uq, g_ckv, w_uk, w_uv, g_qn, g_kn):
    bsz, s, _ = c_q.shape
    q = jnp.einsum('bsr,rhd->bshd', rms_norm(c_q, g_cq), w_uq)
    ckv = rms_norm(c_kv, g_ckv)
    k_nope = jnp.einsum('bsr,rhd->bshd', ckv, w_uk)
    v = jnp.einsum('bsr,rhd->bshd', ckv, w_uv)
    k_rope_h = jnp.broadcast_to(k_rope[:, :, None, :], (bsz, s, MLA_HEADS, MLA_ROPE))
    k = jnp.concatenate([k_nope, k_rope_h], axis=-1)
    q = rms_norm(q, g_qn)
    k = rms_norm(k, g_kn)
    cos, sin = rope_tables(positions)
    q = jnp.concatenate([q[..., :MLA_NOPE], apply_rope(q[..., MLA_NOPE:], cos, sin)], axis=-1)
    k = jnp.concatenate([k[..., :MLA_NOPE], apply_rope(k[..., MLA_NOPE:], cos, sin)], axis=-1)
    scale = MLA_QK ** -0.5
    outs = []
    for blk in range(s // Q_BLOCK):
        q0 = blk * Q_BLOCK
        kend = q0 + Q_BLOCK
        scores = jnp.einsum('bqhd,bkhd->bhqk', q[:, q0:kend], k[:, :kend]).astype(jnp.float32) * scale
        causal = (q0 + jnp.arange(Q_BLOCK))[:, None] >= jnp.arange(kend)[None, :]
        scores = jnp.where(causal, scores, -jnp.inf)
        probs = jax.nn.softmax(scores, axis=-1).astype(v.dtype)
        outs.append(jnp.einsum('bhqk,bkhd->bqhd', probs, v[:, :kend]))
    return jnp.concatenate(outs, axis=1).reshape(bsz, s, MLA_W)

def rwkv7_group(feat, mu, w0, w2, a0, a2, g2, k_k, k_a, r_k, lnx_g, lnx_b):
    bsz, s, _ = feat.shape
    prev = jnp.pad(feat, ((0, 0), (1, 0), (0, 0)))[:, :-1]
    feat = feat + (prev - feat) * mu
    splits = np.cumsum([RWKV_W, RWKV_W, RWKV_W, DECAY_LORA, AAA_LORA]).tolist()
    r, k, v, wl, al, gl = jnp.split(feat, splits, axis=-1)
    w = -jax.nn.softplus(-(w0 + jnp.tanh(wl) @ w2)) - 0.5
    a = jax.nn.sigmoid(a0 + al @ a2)
    g = jax.nn.sigmoid(gl) @ g2
    heads = lambda t: t.reshape(bsz, s, RWKV_HEADS, RWKV_N).astype(jnp.float32)
    kk = heads(k * k_k)
    kk = kk * lax.rsqrt(jnp.sum(kk * kk, axis=-1, keepdims=True) + 1e-12)
    k = k * (1.0 + (a - 1.0) * k_a)
    rh, kh, vh, ah = heads(r), heads(k), heads(v), heads(a)
    decay = jnp.exp(-jnp.exp(heads(w)))

    def step(state, inp):
        r_t, k_t, v_t, kk_t, b_t, d_t = inp
        sa = jnp.einsum('bhvk,bhk->bhv', state, -kk_t)
        state = (state * d_t[:, :, None, :] + sa[..., None] * b_t[:, :, None, :]
                 + v_t[..., None] * k_t[:, :, None, :])
        return state, jnp.einsum('bhvk,bhk->bhv', state, r_t)

    tm = lambda t: jnp.swapaxes(t, 0, 1)
    state0 = jnp.zeros((bsz, RWKV_HEADS, RWKV_N, RWKV_N), jnp.float32)
    _, y = lax.scan(step, state0, (tm(rh), tm(kh), tm(vh), tm(kk), tm(kk * ah), tm(decay)))
    y = tm(y)
    mean = jnp.mean(y, axis=-1, keepdims=True)
    var = jnp.mean(jnp.square(y - mean), axis=-1, keepdims=True)
    y = ((y - mean) * lax.rsqrt(var + LNX_EPS)).reshape(bsz, s, RWKV_W)
    y = y * lnx_g.astype(jnp.float32) + lnx_b.astype(jnp.float32)
    bonus = jnp.sum(rh * kh * r_k.astype(jnp.float32), axis=-1, keepdims=True) * vh
    y = y + bonus.reshape(bsz, s, RWKV_W)
    return (y * g.astype(jnp.float32)).astype(feat.dtype)

def hier_moe(h, w_group, b_group, w_expert, b_expert, w_gate, w_up, w_down):
    bsz, s, d = h.shape
    t = h.reshape(bsz * s, d)
    n = t.shape[0]
    rows = jnp.arange(n)
    group_logits = (t @ w_group).astype(jnp.float32) + b_group.astype(jnp.float32)
    group_probs = jax.nn.softmax(group_logits, axis=-1)
    _, gsel = lax.top_k(group_logits, 1)
    gsel = gsel[:, 0]
    expert_logits = ((t @ w_expert).astype(jnp.float32) + b_expert.astype(jnp.float32)).reshape(
        n, N_GROUPS, EXPERTS_PER_GROUP)
    in_group = expert_logits[rows, gsel]
    top_vals, top_idx = lax.top_k(in_group, TOP_K)
    weights = jax.nn.softmax(top_vals, axis=-1) * group_probs[rows, gsel][:, None]
    expert_ids = gsel[:, None] * EXPERTS_PER_GROUP + top_idx
    combine = jnp.sum(jax.nn.one_hot(expert_ids, N_EXPERTS, dtype=jnp.float32) * weights[..., None],
                      axis=1).astype(t.dtype)
    y = jnp.zeros_like(t)
    for e in range(N_EXPERTS):
        hidden = jax.nn.silu(t @ w_gate[e]) * (t @ w_up[e])
        y = y + combine[:, e:e + 1] * (hidden @ w_down[e])
    return y.reshape(bsz, s, d)

def hybrid_layer(x, positions, g_mix, w_in, g_cq, w_uq, g_ckv, w_uk, w_uv, g_qn, g_kn, g_mla_out,
                 rw_mu, rw_w0, rw_w2, rw_a0, rw_a2, rw_g2, rw_k_k, rw_k_a, rw_r_k, rw_lnx_g, rw_lnx_b,
                 w_o, g_ffn, w_group, b_group, w_expert, b_expert, w_gate, w_up, w_down):
    h = rms_norm(x, g_mix)
    proj = h @ w_in
    c_q = proj[..., :MLA_Q_RANK]
    c_kv = proj[..., MLA_Q_RANK:MLA_Q_RANK + MLA_KV_RANK]
    k_rope = proj[..., MLA_Q_RANK + MLA_KV_RANK:MLA_IN]
    feat = proj[..., MLA_IN:]
    mla_out = rms_norm(mla_group(c_q, c_kv, k_rope, positions, g_cq, w_uq, g_ckv, w_uk, w_uv, g_qn, g_kn),
                       g_mla_out)
    rw_out = rwkv7_group(feat, rw_mu, rw_w0, rw_w2, rw_a0, rw_a2, rw_g2, rw_k_k, rw_k_a, rw_r_k,
                         rw_lnx_g, rw_lnx_b)
    x = x + jnp.concatenate([mla_out, rw_out], axis=-1) @ w_o
    x = x + hier_moe(rms_norm(x, g_ffn), w_group, b_group, w_expert, b_expert, w_gate, w_up, w_down)
    return x

def first_inputs(seed: int = 0) -> dict:
    key = jax.random.key(seed)
    ks = iter(jax.random.split(key, 40))
    L = DEPTH

    def nrm(shape, scale):
        return jax.random.normal(next(ks), shape, jnp.float32) * scale

    def gain(shape):
        return 1.0 + nrm(shape, 0.02)

    x = nrm((BATCH, SEQ, D_MODEL), 1.0)
    positions = (jnp.arange(SEQ, dtype=jnp.int32)[None, :]
                 + jax.random.randint(next(ks), (BATCH, 1), 0, 1024, jnp.int32))
    return {
        'x': x,
        'positions': positions,
        'g_mix': gain((L, D_MODEL)),
        'w_in': nrm((L, D_MODEL, IN_W), D_MODEL ** -0.5),
        'g_cq': gain((L, MLA_Q_RANK)),
        'w_uq': nrm((L, MLA_Q_RANK, MLA_HEADS, MLA_QK), MLA_Q_RANK ** -0.5),
        'g_ckv': gain((L, MLA_KV_RANK)),
        'w_uk': nrm((L, MLA_KV_RANK, MLA_HEADS, MLA_NOPE), MLA_KV_RANK ** -0.5),
        'w_uv': nrm((L, MLA_KV_RANK, MLA_HEADS, MLA_V), MLA_KV_RANK ** -0.5),
        'g_qn': gain((L, MLA_QK)),
        'g_kn': gain((L, MLA_QK)),
        'g_mla_out': gain((L, MLA_W)),
        'rw_mu': jax.random.uniform(next(ks), (L, RWKV_IN), jnp.float32, 0.0, 1.0),
        'rw_w0': jax.random.uniform(next(ks), (L, RWKV_W), jnp.float32, -4.0, 2.0),
        'rw_w2': nrm((L, DECAY_LORA, RWKV_W), 0.5 * DECAY_LORA ** -0.5),
        'rw_a0': nrm((L, RWKV_W), 0.1),
        'rw_a2': nrm((L, AAA_LORA, RWKV_W), 0.5 * AAA_LORA ** -0.5),
        'rw_g2': nrm((L, GATE_LORA, RWKV_W), GATE_LORA ** -0.5),
        'rw_k_k': 0.85 + nrm((L, RWKV_W), 0.02),
        'rw_k_a': 1.0 + nrm((L, RWKV_W), 0.02),
        'rw_r_k': nrm((L, RWKV_HEADS, RWKV_N), 0.1),
        'rw_lnx_g': gain((L, RWKV_W)),
        'rw_lnx_b': nrm((L, RWKV_W), 0.01),
        'w_o': nrm((L, MIX_W, D_MODEL), MIX_W ** -0.5),
        'g_ffn': gain((L, D_MODEL)),
        'w_group': nrm((L, D_MODEL, N_GROUPS), D_MODEL ** -0.5),
        'b_group': nrm((L, N_GROUPS), 0.01),
        'w_expert': nrm((L, D_MODEL, N_EXPERTS), D_MODEL ** -0.5),
        'b_expert': nrm((L, N_EXPERTS), 0.01),
        'w_gate': nrm((L, N_EXPERTS, D_MODEL, D_EXPERT), D_MODEL ** -0.5),
        'w_up': nrm((L, N_EXPERTS, D_MODEL, D_EXPERT), D_MODEL ** -0.5),
        'w_down': nrm((L, N_EXPERTS, D_EXPERT, D_MODEL), D_EXPERT ** -0.5),
    }

def first_block(x, positions, g_mix, w_in, g_cq, w_uq, g_ckv, w_uk, w_uv, g_qn, g_kn, g_mla_out,
              rw_mu, rw_w0, rw_w2, rw_a0, rw_a2, rw_g2, rw_k_k, rw_k_a, rw_r_k, rw_lnx_g, rw_lnx_b,
              w_o, g_ffn, w_group, b_group, w_expert, b_expert, w_gate, w_up, w_down):
    for l in range(DEPTH):
        x = hybrid_layer(x, positions, g_mix[l], w_in[l], g_cq[l], w_uq[l], g_ckv[l], w_uk[l], w_uv[l],
                         g_qn[l], g_kn[l], g_mla_out[l], rw_mu[l], rw_w0[l], rw_w2[l], rw_a0[l],
                         rw_a2[l], rw_g2[l], rw_k_k[l], rw_k_a[l], rw_r_k[l], rw_lnx_g[l], rw_lnx_b[l],
                         w_o[l], g_ffn[l], w_group[l], b_group[l], w_expert[l], b_expert[l],
                         w_gate[l], w_up[l], w_down[l])
    return x


DEPTH_2 = 2

DA_HEADS = 4
DA_QK_DIM = 64
DA_V_DIM = 2 * DA_QK_DIM
RET_HEADS = 4
RET_QK_DIM = 64
RET_V_DIM = 64
RET_CHUNK = 128
SC_WIDTH = 256
SC_GROUPS = 4
CONV_W = 3
D_FF = 2816
REL_BUCKETS = 32
REL_MAX_DIST = 128
EPS = 1e-6
N_BRANCH = 3

DA_QK_W = DA_HEADS * 2 * DA_QK_DIM
DA_V_W = DA_HEADS * DA_V_DIM
RET_QK_W = RET_HEADS * RET_QK_DIM
RET_V_W = RET_HEADS * RET_V_DIM
IN_SPLITS = (DA_QK_W, DA_QK_W, DA_V_W,
             RET_QK_W, RET_QK_W, RET_V_W, RET_V_W,
             SC_WIDTH, SC_WIDTH, SC_WIDTH,
             N_BRANCH * D_MODEL)
IN_WIDTH = 2 * DA_QK_W + DA_V_W + 2 * RET_QK_W + 2 * RET_V_W + 3 * SC_WIDTH + N_BRANCH * D_MODEL


def rmsnorm(x, g):
    xf = x.astype(jnp.float32)
    y = xf * lax.rsqrt(jnp.mean(xf * xf, axis=-1, keepdims=True) + EPS)
    return (y * g.astype(jnp.float32)).astype(x.dtype)

def causal_dwconv(x, w, b):
    S = x.shape[1]
    K = w.shape[0]
    xp = jnp.pad(x, ((0, 0), (K - 1, 0), (0, 0)))
    y = b + xp[:, 0:S] * w[0]
    for k in range(1, K):
        y = y + xp[:, k:k + S] * w[k]
    return y

def rel_bucket(n):
    max_exact = REL_BUCKETS // 2
    nf = jnp.maximum(n, 1).astype(jnp.float32)
    large = max_exact + (jnp.log(nf / max_exact) / math.log(REL_MAX_DIST / max_exact)
                         * (REL_BUCKETS - max_exact)).astype(jnp.int32)
    large = jnp.minimum(large, REL_BUCKETS - 1)
    return jnp.where(n < max_exact, n, large)

def rotary(x, pos):
    d = x.shape[-1]
    half = d // 2
    inv = ROPE_THETA ** (-jnp.arange(half, dtype=jnp.float32) / half)
    ang = pos.astype(jnp.float32)[:, None] * inv[None, :]
    cos = jnp.cos(ang)[None, :, None, :]
    sin = jnp.sin(ang)[None, :, None, :]
    xf = x.astype(jnp.float32)
    x1, x2 = xf[..., :half], xf[..., half:]
    return jnp.concatenate([x1 * cos - x2 * sin, x2 * cos + x1 * sin], axis=-1)

def diff_attention(q, k, v, lam, bias_dist):
    B, S, H = q.shape[0], q.shape[1], q.shape[2]
    qh = jnp.transpose(q, (0, 2, 3, 1, 4)).astype(jnp.float32)
    kh = jnp.transpose(k, (0, 2, 3, 1, 4)).astype(jnp.float32)
    vh = jnp.transpose(v, (0, 2, 1, 3)).astype(jnp.float32)
    kpos = jnp.arange(S)
    neg = jnp.finfo(jnp.float32).min

    def block(i):
        start = i * Q_BLOCK
        qb = lax.dynamic_slice_in_dim(qh, start, Q_BLOCK, axis=3)
        dist = (start + jnp.arange(Q_BLOCK))[:, None] - kpos[None, :]
        bias = jnp.transpose(bias_dist[jnp.maximum(dist, 0)], (2, 0, 1)).astype(jnp.float32)
        s = jnp.einsum('bhmqd,bhmkd->bhmqk', qb, kh) + bias[None, :, None]
        s = jnp.where(dist >= 0, s, neg)
        p = jax.nn.softmax(s, axis=-1)
        a = p[:, :, 0] - lam * p[:, :, 1]
        return jnp.einsum('bhqk,bhke->bhqe', a, vh)

    out = lax.map(block, jnp.arange(S // Q_BLOCK))
    return jnp.transpose(out, (1, 0, 3, 2, 4)).reshape(B, S, H, -1)

def retention(q, k, v):
    B, S, H, dk = q.shape
    dv = v.shape[-1]
    C = RET_CHUNK
    N = S // C
    lg = jnp.log(1.0 - 2.0 ** (-5.0 - jnp.arange(H, dtype=jnp.float32)))
    to_chunks = lambda t: jnp.transpose(t.astype(jnp.float32).reshape(B, N, C, H, t.shape[-1]), (0, 3, 1, 2, 4))
    qc, kc, vc = to_chunks(q), to_chunks(k), to_chunks(v)
    idx = jnp.arange(C, dtype=jnp.float32)
    diff = idx[:, None] - idx[None, :]
    d_intra = jnp.where(diff[None] >= 0, jnp.exp(lg[:, None, None] * jnp.maximum(diff, 0.0)[None]), 0.0)
    inner = jnp.einsum('bhncd,bhnjd->bhncj', qc, kc) * d_intra[None, :, None]
    inner = jnp.einsum('bhncj,bhnje->bhnce', inner, vc)
    k_dec = kc * jnp.exp(lg[:, None] * (C - 1 - idx)[None])[None, :, None, :, None]
    kv = jnp.einsum('bhncd,bhnce->nbhde', k_dec, vc)
    chunk_decay = jnp.exp(lg * C)[None, :, None, None]

    def step(R, kv_n):
        return R * chunk_decay + kv_n, R

    _, R_prev = lax.scan(step, jnp.zeros((B, H, dk, dv), jnp.float32), kv)
    q_dec = qc * jnp.exp(lg[:, None] * (idx + 1.0)[None])[None, :, None, :, None]
    cross = jnp.einsum('bhncd,nbhde->bhnce', q_dec, R_prev)
    o = inner + cross
    return jnp.transpose(o, (0, 2, 3, 1, 4)).reshape(B, S, H, dv)

def second_inputs(seed: int = 0) -> dict:
    key = jax.random.key(seed)
    ks = jax.random.split(key, 24)
    f32 = jnp.float32
    nrm = lambda k, shape, s: jax.random.normal(k, shape, f32) * s
    gain = lambda k, shape: 1.0 + 0.05 * jax.random.normal(k, shape, f32)
    return {
        "x": nrm(ks[0], (BATCH, SEQ, D_MODEL), 1.0),
        "rel_bias": nrm(ks[1], (REL_BUCKETS, DA_HEADS), 0.5),
        "norm_mix_g": gain(ks[2], (DEPTH_2, D_MODEL)),
        "w_in": nrm(ks[3], (DEPTH_2, D_MODEL, IN_WIDTH), D_MODEL ** -0.5),
        "b_gate": nrm(ks[4], (DEPTH_2, N_BRANCH * D_MODEL), 0.02),
        "da_q_norm_g": gain(ks[5], (DEPTH_2, DA_QK_DIM)),
        "da_k_norm_g": gain(ks[6], (DEPTH_2, DA_QK_DIM)),
        "da_lambda": nrm(ks[7], (DEPTH_2, 4, DA_QK_DIM), 0.1),
        "da_subln_g": gain(ks[8], (DEPTH_2, DA_V_DIM)),
        "ret_norm_g": gain(ks[9], (DEPTH_2, RET_V_DIM)),
        "sc_conv_w": nrm(ks[10], (DEPTH_2, CONV_W, SC_WIDTH), CONV_W ** -0.5),
        "sc_conv_b": nrm(ks[11], (DEPTH_2, SC_WIDTH), 0.02),
        "w_branch_da": nrm(ks[12], (DEPTH_2, DA_V_W, D_MODEL), DA_V_W ** -0.5),
        "w_branch_ret": nrm(ks[13], (DEPTH_2, RET_V_W, D_MODEL), RET_V_W ** -0.5),
        "w_branch_sc": nrm(ks[14], (DEPTH_2, SC_WIDTH, D_MODEL), SC_WIDTH ** -0.5),
        "w_out": nrm(ks[15], (DEPTH_2, D_MODEL, D_MODEL), 0.5 * D_MODEL ** -0.5),
        "norm_ffn_g": gain(ks[16], (DEPTH_2, D_MODEL)),
        "w_ffn_in": nrm(ks[17], (DEPTH_2, D_MODEL, 2 * D_FF), D_MODEL ** -0.5),
        "ffn_conv_w": nrm(ks[18], (DEPTH_2, CONV_W, D_FF), CONV_W ** -0.5),
        "ffn_conv_b": nrm(ks[19], (DEPTH_2, D_FF), 0.02),
        "w_ffn_out": nrm(ks[20], (DEPTH_2, D_FF, D_MODEL), 0.5 * D_FF ** -0.5),
    }

def second_block(x, rel_bias, norm_mix_g, w_in, b_gate, da_q_norm_g, da_k_norm_g, da_lambda,
              da_subln_g, ret_norm_g, sc_conv_w, sc_conv_b, w_branch_da, w_branch_ret,
              w_branch_sc, w_out, norm_ffn_g, w_ffn_in, ffn_conv_w, ffn_conv_b, w_ffn_out):
    B, S, D = x.shape
    pos = jnp.arange(S)
    bias_dist = rel_bias[rel_bucket(pos)]
    offs = np.cumsum(IN_SPLITS)[:-1].tolist()
    for l in range(DEPTH_2):
        h = rmsnorm(x, norm_mix_g[l])
        proj = jnp.einsum('bsd,de->bse', h, w_in[l])
        (da_q, da_k, da_v, r_q, r_k, r_v, r_g,
         sc_b, sc_c, sc_x, gate_pre) = jnp.split(proj, offs, axis=-1)

        lam_init = 0.8 - 0.6 * math.exp(-0.3 * l)
        lp = da_lambda[l].astype(jnp.float32)
        lam = jnp.exp(jnp.sum(lp[0] * lp[1])) - jnp.exp(jnp.sum(lp[2] * lp[3])) + lam_init
        q = rmsnorm(da_q.reshape(B, S, DA_HEADS, 2, DA_QK_DIM), da_q_norm_g[l]) * (DA_QK_DIM ** -0.5)
        k = rmsnorm(da_k.reshape(B, S, DA_HEADS, 2, DA_QK_DIM), da_k_norm_g[l])
        v = da_v.reshape(B, S, DA_HEADS, DA_V_DIM)
        o_da = diff_attention(q, k, v, lam, bias_dist)
        o_da = (rmsnorm(o_da, da_subln_g[l]) * (1.0 - lam_init)).astype(x.dtype).reshape(B, S, DA_V_W)

        rq = rotary(r_q.reshape(B, S, RET_HEADS, RET_QK_DIM), pos)
        rk = rotary(r_k.reshape(B, S, RET_HEADS, RET_QK_DIM), pos) * (RET_QK_DIM ** -0.5)
        rv = r_v.reshape(B, S, RET_HEADS, RET_V_DIM)
        o_ret = rmsnorm(retention(rq, rk, rv), ret_norm_g[l]).reshape(B, S, RET_V_W)
        o_ret = (o_ret * jax.nn.silu(r_g.astype(jnp.float32))).astype(x.dtype)

        o_sc = sc_b * causal_dwconv(sc_c * sc_x, sc_conv_w[l], sc_conv_b[l])

        gates = jax.nn.sigmoid((gate_pre + b_gate[l]).astype(jnp.float32)).astype(x.dtype)
        gates = gates.reshape(B, S, N_BRANCH, D)
        y = (gates[:, :, 0] * jnp.einsum('bse,ed->bsd', o_da, w_branch_da[l])
             + gates[:, :, 1] * jnp.einsum('bse,ed->bsd', o_ret, w_branch_ret[l])
             + gates[:, :, 2] * jnp.einsum('bse,ed->bsd', o_sc, w_branch_sc[l]))
        x = x + jnp.einsum('bsd,de->bse', y, w_out[l])

        h = rmsnorm(x, norm_ffn_g[l])
        gu = jnp.einsum('bsd,df->bsf', h, w_ffn_in[l])
        g_ff, u_ff = gu[..., :D_FF], gu[..., D_FF:]
        g_ff = causal_dwconv(g_ff, ffn_conv_w[l], ffn_conv_b[l])
        x = x + jnp.einsum('bsf,fd->bsd', jax.nn.silu(g_ff) * u_ff, w_ffn_out[l])
    return x


def setup_inputs(seed=0):
    out = dict(first_inputs(seed))
    for name, value in second_inputs(seed + 1).items():
        if name != "x":
            out[name + "_2"] = value
    return out


def reference(
    x, positions, g_mix, w_in, g_cq, w_uq, g_ckv, w_uk, w_uv, g_qn, g_kn, g_mla_out, rw_mu,
    rw_w0, rw_w2, rw_a0, rw_a2, rw_g2, rw_k_k, rw_k_a, rw_r_k, rw_lnx_g, rw_lnx_b, w_o, g_ffn,
    w_group, b_group, w_expert, b_expert, w_gate, w_up, w_down, rel_bias_2, norm_mix_g_2,
    w_in_2, b_gate_2, da_q_norm_g_2, da_k_norm_g_2, da_lambda_2, da_subln_g_2, ret_norm_g_2,
    sc_conv_w_2, sc_conv_b_2, w_branch_da_2, w_branch_ret_2, w_branch_sc_2, w_out_2,
    norm_ffn_g_2, w_ffn_in_2, ffn_conv_w_2, ffn_conv_b_2, w_ffn_out_2,
):
    x = first_block(
        x, positions, g_mix, w_in, g_cq, w_uq, g_ckv, w_uk, w_uv, g_qn, g_kn, g_mla_out, rw_mu,
        rw_w0, rw_w2, rw_a0, rw_a2, rw_g2, rw_k_k, rw_k_a, rw_r_k, rw_lnx_g, rw_lnx_b, w_o,
        g_ffn, w_group, b_group, w_expert, b_expert, w_gate, w_up, w_down,
    )
    return second_block(
        x, rel_bias_2, norm_mix_g_2, w_in_2, b_gate_2, da_q_norm_g_2, da_k_norm_g_2,
        da_lambda_2, da_subln_g_2, ret_norm_g_2, sc_conv_w_2, sc_conv_b_2, w_branch_da_2,
        w_branch_ret_2, w_branch_sc_2, w_out_2, norm_ffn_g_2, w_ffn_in_2, ffn_conv_w_2,
        ffn_conv_b_2, w_ffn_out_2,
    )


_drawn_inputs = setup_inputs


def setup_inputs(seed=0):
    import zlib

    import numpy as np

    out = dict(_drawn_inputs(seed))
    spreads = {}
    factors = {'g_cq': 2.941,
     'rw_w2': 2.778,
     'rw_k_k': 4.054,
     'rw_k_a': 4.206,
     'rw_lnx_g': 3.236,
     'rw_lnx_b': 3.528,
     'b_group': 4.934,
     'b_expert': 3.555,
     'b_gate_2': 8.0,
     'da_q_norm_g_2': 8.0,
     'da_k_norm_g_2': 8.0,
     'da_lambda_2': 3.966,
     'da_subln_g_2': 5.196,
     'ret_norm_g_2': 7.346,
     'sc_conv_b_2': 8.0,
     'ffn_conv_b_2': 8.0}
    for name, (base, spread) in spreads.items():
        noise = np.random.default_rng([zlib.crc32(name.encode()), seed]).standard_normal(out[name].shape)
        drawn = base * np.exp(spread * noise) if base else spread * noise
        out[name] = __import__('jax').numpy.asarray(drawn.astype(out[name].dtype))
    for name, factor in factors.items():
        out[name] = (out[name] * factor).astype(out[name].dtype)
    return out
```

```python
from contextlib import ExitStack

import numpy as np
import concourse.bass as bass
from concourse import mybir

F32 = mybir.dt.float32
I32 = mybir.dt.int32
ALU = mybir.AluOpType
ACT = mybir.ActivationFunctionType
AX = mybir.AxisListType

P = 128
T = 512
NT = T // P
D = 1024
KD = D // P
EPS = 1e-6
NEG = -1.0e30

HM, NOPE, ROPE = 8, 64, 32
QK = NOPE + ROPE
QR, KVR = 256, 128
HR, RN = 8, 64
RW = HR * RN
LNX_EPS = 64e-5
CH = 64
NCH = T // CH
EXP_NEG_HALF = 0.6065306597126334
NG, EG, NE, DE = 4, 8, 32, 256

L2 = 2
DH, DQ, DV = 4, 64, 128
RH, RQ = 4, 64
SCW = 256
DFF = 2816
KF = DFF // P
R = 6
ARENA = 55 * 512 + 40
TPS = 8

CONST_COLS = [("ident", 128), ("ones", 128), ("blk64", 128), ("perm64", 128), ("perm96", 128),
              ("upper", 128), ("upper_eq", 128), ("lower", 128), ("lev1", 128), ("lev1T", 128),
              ("lev2", 128), ("lev4", 128), ("lev8", 128), ("lev16", 128), ("lev32", 128),
              ("causal", 512), ("ret_decay", 4 * 512), ("ret_cos", 512), ("ret_sin", 512),
              ("scan_keep", 512), ("inv_freq", 1), ("iota32", 32), ("iota4", 4)]
P1_COLS = [("g_mix", 8), ("g_cq", 2), ("g_ckv", 1), ("g_qn", 1), ("g_kn", 1), ("g_mla_out", 4),
           ("mu", 14), ("w0", 4), ("a0", 4), ("k_k", 4), ("k_a", 4), ("r_k", 4), ("lnx_g", 4),
           ("lnx_b", 4), ("g_ffn", 8), ("b_route", 36), ("w_route", 8 * 36)]
W1_COLS = [("uq", 2 * 768), ("uk", 512), ("uv", 512), ("w2a2", 512), ("g2", 512)]
P2_COLS = [("g_mix", 8), ("b_gate", 24), ("gq", 1), ("gk", 1), ("subln", 1), ("retg", 1), ("scw", 6),
           ("scb", 2), ("g_ffn", 8), ("fcw", 66), ("fcb", 22), ("lam_init", 1), ("one_minus", 1),
           ("lam", 256)]


def offsets(cols):
    at, out = 0, {}
    for name, n in cols:
        out[name] = (at, n)
        at += n
    return out, at


def job_names():
    a = ["ssq1"]
    a += [f"win{m}" for m in range(18)]
    a += ["cqss", "ckvss"]
    a += [f"vm{i}" for i in range(NT)]
    for h in range(HM):
        a += [f"q{h}", f"k{h}", f"qss{h}", f"kss{h}", f"qp{h}", f"kp{h}"]
    units = [(h, i) for h in range(HM) for i in range(NT)]
    for n, (h, i) in enumerate(units):
        a.append(f"ms{h}_{i}")
        if n:
            ph, pi = units[n - 1]
            a.append(f"mt{ph}_{pi}")
            if pi == NT - 1 and ph % 2 == 1:
                a.append(f"mo{ph // 2}")
    a += [f"mt{HM - 1}_{NT - 1}", f"mo{HM // 2 - 1}", "moss"]
    for c in range(4):
        a += [f"ru{c}", f"ra{c}", f"rg{c}", f"rkk{c}", f"rb{c}"]
        a += [f"rt{c}_{x}" for x in "vbk"]
        for hh in range(2):
            a += [f"m{x}{c}_{hh}" for x in ("abT", "ab", "ak", "br", "kr")]
        for lev in (2, 4, 8, 16, 32):
            for hh in range(2):
                a.append(f"ix{c}_{lev}_{hh}")
            for hh in range(2):
                a.append(f"iy{c}_{lev}_{hh}")
                if lev != 32:
                    a.append(f"iz{c}_{lev}_{hh}")
        for n in range(NCH):
            a += [f"cw{c}_{n}", f"cu{c}_{n}", f"cy{c}_{n}"]
            if n < NCH - 1:
                a.append(f"cs{c}_{n}")
        a += [f"gm{c}", f"gv{c}"]
    a += [f"wo{m}" for m in range(8)]
    a += ["ssq2", "route", "combT"]
    m = ["mg0", "mu0", "mg1", "mu1"] + [f"md{m}" for m in range(8)]
    l = ["ssq3"] + [f"dav{i}" for i in range(NT)] + [f"rv{i}" for i in range(NT)]
    l += [f"{x}{c}" for x in ("rq", "rk") for c in range(2)]
    for h in range(DH):
        l += [f"dq{h}", f"dk{h}"]
    for h in range(DH):
        l += [f"dqss{h}", f"dkss{h}"]
    l += [f"{x}{c}" for x in ("rqp", "rkp") for c in range(2)]
    l += [f"{x}{c}" for x in ("rgt", "scb", "scc", "scx") for c in range(2)]
    for h in range(RH):
        l += [f"rs{h}_{j}" for j in range(NT)]
        l += [f"ro{h // 2}"] if h % 2 else []
    l += ["ross0", "ross1"]
    dunits = [(h, i) for h in range(DH) for i in range(NT)]
    for n, (h, i) in enumerate(dunits):
        l += [f"ds{h}_{i}_0", f"ds{h}_{i}_1"]
        if n:
            ph, pi = dunits[n - 1]
            l.append(f"dt{ph}_{pi}")
            if pi == NT - 1:
                l += [f"do{ph}"]
    l += [f"dt{DH - 1}_{NT - 1}", f"do{DH - 1}"] + [f"doss{h}" for h in range(DH)]
    for m_ in range(8):
        l += [f"gate{b_}_{m_}" for b_ in range(3)] + [f"br{b_}_{m_}" for b_ in range(3)]
    l += [f"wout{m_}" for m_ in range(8)] + ["ssq4"]
    for k in range(KF):
        l += [f"fg{k}", f"fu{k}"]
    l += [f"fo{m_}" for m_ in range(8)]
    return {"A": a, "M": m, "B": [f"bias{h}" for h in range(DH)], "L": l}


def build(nc, ts_, out):
    jobs = job_names()
    JOB = {name: (sec, n) for sec, names in jobs.items() for n, name in enumerate(names)}
    assert len(JOB) == sum(map(len, jobs.values()))
    uses = {s: [len(range(b, len(jobs[s]), 8)) for b in range(8)] for s in jobs}
    base, at = {}, [0] * 8
    for s, times in (("A", 1), ("M", NE), ("B", 1), ("L", L2)):
        base[s] = list(at)
        at = [x + times * u for x, u in zip(at, uses[s])]

    last_user = {"A": [f"win{m}" for m in range(18)] + [f"wo{m}" for m in range(8)],
                 "M": ["mg0", "mu0", "mg1", "mu1", "md3", "md7"],
                 "L": [f"dav{NT - 1}"] * 4 + [f"rv{NT - 1}"] * 2
                      + [f"{x}{c}" for x in ("rq", "rk") for c in range(2)]
                      + [f"d{x}{h}" for h in range(DH) for x in "qk"]
                      + [f"{x}{c}" for x in ("rgt", "scb", "scc", "scx") for c in range(2)]
                      + [f"{g}_{m}" for m in range(8) for g in ("gate0", "gate1", "gate2", "br2")]
                      + [f"wout{m}" for m in range(8)]
                      + [f"f{x}{k}" for k in range(KF) for x in "gu"]
                      + [f"fo{min(7, (8 * s + 7) // KF)}" for s in range(KF)]}
    n_slots = {s: len(v) for s, v in last_user.items()}
    slot0 = {"A": 0, "M": n_slots["A"], "L": n_slots["A"] + NE * n_slots["M"]}
    assert n_slots["M"] % R == 0 and n_slots["L"] % R == 0 and n_slots["A"] % R == slot0["M"] % R

    C, nC = offsets(CONST_COLS)
    A1, nA1 = offsets(P1_COLS)
    W1, nW1 = offsets(W1_COLS)
    A2, nA2 = offsets(P2_COLS)

    with ExitStack() as ctx:
        def sb(name, shape, dt=F32):
            return ctx.enter_context(nc.sbuf_tensor(name, shape, dt))

        def sem(name):
            return ctx.enter_context(nc.semaphore(name))

        X = sb("X", [P, KD, T])
        H = sb("H", [P, KD, T])
        ring = sb("ring", [P, R, TPS * P])
        cst = sb("cst", [P, nC])
        p1 = sb("p1", [P, nA1])
        w1 = sb("w1", [P, nW1])
        p2 = sb("p2", [P, nA2])
        small = sb("small", [P, 64])
        arena = sb("arena", [P, ARENA])
        posi = sb("posi", [P, 2], I32)
        bank = [ctx.enter_context(nc.psum_tensor(f"bank{b}", [P, 512], F32)) for b in range(8)]
        scratch = nc.dram_tensor("comb_scratch", [NE, T], F32, kind="Internal").ap()
        bias_scratch = nc.dram_tensor("bias_scratch", [DH, P * 640], F32, kind="Internal").ap()

        bank_full = [sem(f"bank_full{b}") for b in range(8)]
        bank_free = [sem(f"bank_free{b}") for b in range(8)]
        slot_full = [sem(f"slot_full{r}") for r in range(R)]
        events = {}
        posts = {}
        ended = []

        def ev(name):
            if name not in events:
                events[name] = sem(name)
            return events[name]

        def cc(name, p=slice(0, P), n=None):
            o, w = C[name]
            return cst[p, o:o + (n or w)]

        def par(t, tab, name, i=0, n=1, p=slice(0, P)):
            o, _ = tab[name]
            return t[p, o + i:o + i + n]

        def ch(at_, n=1, w=512):
            return arena[:, at_:at_ + n * w].rearrange("p (n w) -> p n w", n=n)

        class Engine:

            def __init__(self, eng, name):
                self.e, self.name = eng, name
                self.sec, self.l = "A", 0
                self.chain, self.n = (sem(f"{name}_chain"), 0) if name in ("dve", "act", "pool") else (None, 0)

            def use(self, job):
                s, n = JOB[job]
                assert s == self.sec or self.sec != "A", (job, self.sec)
                b = n % 8
                if s == self.sec:
                    return b, base[s][b] + n // 8 + self.l * uses[s][b]
                times = {"A": 1, "M": NE, "B": 1, "L": L2}[s]
                return b, base[s][b] + n // 8 + (times - 1) * uses[s][b]

            def filled(self, job):
                b, n = self.use(job)
                return bank_full[b], n + 1

            def taken(self, job):
                b, n = self.use(job)
                return bank_free[b], n + 1

            def emptied(self, job):
                b, n = self.use(job)
                return bank_free[b], n

            def nth(self, name, n=1):
                return ev(name), n + self.l * PER[name] if name in PER else n

            def landed(self, name):
                return ev(name), 16 + self.l * 16

            def fills(self, job):
                ended.append((job, "full"))
                return bank_full[JOB[job][1] % 8]

            def takes(self, job):
                ended.append((job, "free"))
                return bank_free[JOB[job][1] % 8]

            def tells(self, name):
                posts[name] = posts.get(name, 0) + 1
                return ev(name)

            def chained(self):
                self.n += 1
                return self.chain

            def restart(self):
                self.e.wait_ge(self.chain, self.n)
                self.e.sem_clear(self.chain)
                self.n = 0

        def bank_of(job):
            return bank[JOB[job][1] % 8]

        V, S, G = nc.vector, nc.scalar, nc.gpsimd

        def tt(o, a, b, op):
            return V.tensor_tensor(o, a, b, op)

        def ts(o, a, s1, s2, op0, op1=None):
            return V.tensor_scalar(o, a, s1, s2, op0, op1) if op1 is not None else V.tensor_scalar(o, a, s1, None, op0)

        def stt(o, a, s, b, op0, op1):
            return V.scalar_tensor_tensor(out=o, in0=a, scalar=s, in1=b, op0=op0, op1=op1)

        def act_(o, i, f, bias=0.0, scale=1.0, accum=None):
            if f == ACT.Copy:
                return S.activation(o, i, f)
            kw = {} if accum is None else {"accum_out": accum}
            if isinstance(bias, float) and bias != 0.0:
                bias = small[0:o.shape[0], BIAS[bias]:BIAS[bias] + 1]
            return S.activation(o, i, f, bias=bias, scale=scale, **kw)

        BIAS = {EPS: 60, 1e-12: 61, LNX_EPS: 62}

        def tiles4(ap):
            return ap.rearrange("p (n w) -> p n w", n=4)

        def over4(ap):
            return ap.unsqueeze(1).to_broadcast([ap.shape[0], 4, 128])

        RS_ = 516
        RAW = arena[:, 0:14 * RS_].rearrange("p (n w) -> p n w", n=14)
        m0 = 14 * RS_ + 8
        CQ, KR, COS, SIN = ch(m0, 3), ch(m0 + 1536), ch(m0 + 2048), ch(m0 + 2560)
        Q1, K1 = ch(m0 + 3072, 8), ch(m0 + 3072 + 4096, 8)
        o_ = m0 + 3072 + 8192
        VT1, PT1, S1, TM = ch(o_, 4), ch(o_ + 2048, 4), ch(o_ + 4096, 2), ch(o_ + 5120, 6)
        OM = H[:, 0:4, :]
        names = ["LW", "A", "G", "KK", "KP", "B", "SQ", "RS", "BON", "L", "EL", "ENL", "ELX", "AT", "BT",
                 "KT", "RT", "BH", "KH", "TKV", "TKB", "TKK", "Y", "MT0", "MT1", "TI0", "TI1", "TT0", "TT1",
                 "XX0", "XX1", "MK0", "MK1", "MB0", "MB1", "MR0", "MR1"]
        W = {n: arena[:, m0 + 512 * i:m0 + 512 * (i + 1)] for i, n in enumerate(names)}
        for i, n in enumerate(("ST", "WS", "US")):
            W[n] = arena[:, m0 + 512 * len(names) + 128 * i:m0 + 512 * len(names) + 128 * i + 128]
        units1 = [(h, i) for h in range(HM) for i in range(NT)]
        ident = cc("ident")

        def weights(pe, s, sec="A", it=0):
            g = slot0[sec] + s
            r = g % R
            n = g // R + 1
            if sec != "A":
                n = n + pe.l * (n_slots[sec] // R)
            pe.e.wait_ge(slot_full[r], 16 * n)
            return ring[:, r, :].rearrange("p (k n) -> p k n", k=TPS)

        mm = nc.tensor.matmul

        def pe_A(pe):
            e = pe.e
            e.wait_ge(ev("consts_in"), 16)
            e.wait_ge(ev("p1_in"), 16)
            ps = bank_of("ssq1")
            for c in range(KD):
                pe.e.wait_ge(*pe.nth("sq1", c + 1))
                i = mm(ps[:, :], cc("ones"), Q1[:, c, :], start=c == 0, stop=c == KD - 1)
            i.then_inc(pe.fills("ssq1"), 1)
            for m in range(18):
                w = weights(pe, m)
                if m >= 7:
                    pe.e.wait_ge(*pe.emptied(f"win{m}"))
                ps = bank_of(f"win{m}")
                o = ps[64:96, :] if m == 3 else ps[:, :]
                for k in range(KD):
                    if m == 0:
                        pe.e.wait_ge(*pe.nth("h1", k + 1))
                    i = mm(o, w[:, k, 0:32] if m == 3 else w[:, k, :], H[:, k, :], start=k == 0, stop=k == KD - 1)
                i.then_inc(pe.fills(f"win{m}"), 1)
            pe.e.wait_ge(*pe.emptied("cqss"))
            ps = bank_of("cqss")
            for c in range(2):
                pe.e.wait_ge(*pe.nth("cqsq", c + 1))
                i = mm(ps[:, :], cc("ones"), TM[:, c, :], start=c == 0, stop=c == 1)
            i.then_inc(pe.fills("cqss"), 1)
            pe.e.wait_ge(*pe.emptied("ckvss"))
            ps = bank_of("ckvss")
            pe.e.wait_ge(*pe.nth("cqsq", 3))
            mm(ps[:, :], cc("ones"), TM[:, 2, :], start=True, stop=True).then_inc(pe.fills("ckvss"), 1)
            e.wait_ge(ev("w1_in"), 16)
            uv = par(w1, W1, "uv", 0, 512)
            pe.e.wait_ge(*pe.nth("cqn", 3))
            for i_ in range(NT):
                pe.e.wait_ge(*pe.emptied(f"vm{i_}"))
                ps = bank_of(f"vm{i_}")
                mm(ps[:, :], CQ[:, 2, i_ * P:(i_ + 1) * P], uv, start=True, stop=True).then_inc(pe.fills(f"vm{i_}"), 1)
            for h in range(HM):
                pe.e.wait_ge(*pe.emptied(f"q{h}"))
                ps = bank_of(f"q{h}")
                for k in range(2):
                    i = mm(ps[0:QK, :], par(w1, W1, "uq", k * 768 + h * QK, QK), CQ[:, k, :], start=k == 0, stop=k == 1)
                i.then_inc(pe.fills(f"q{h}"), 1)
                pe.e.wait_ge(*pe.emptied(f"k{h}"))
                ps = bank_of(f"k{h}")
                mm(ps[0:NOPE, :], par(w1, W1, "uk", h * NOPE, NOPE), CQ[:, 2, :], start=True, stop=True).then_inc(pe.fills(f"k{h}"), 1)
                for j, x in enumerate("qk"):
                    pe.e.wait_ge(*pe.emptied(f"{x}ss{h}"))
                    ps = bank_of(f"{x}ss{h}")
                    pe.e.wait_ge(*pe.nth("qksq", 2 * h + j + 1))
                    mm(ps[0:QK, :], cc("ones", slice(0, QK), QK), TM[0:QK, j, :], start=True, stop=True).then_inc(pe.fills(f"{x}ss{h}"), 1)
                for j, x in enumerate("qk"):
                    pe.e.wait_ge(*pe.emptied(f"{x}p{h}"))
                    ps = bank_of(f"{x}p{h}")
                    pe.e.wait_ge(*pe.nth("qkn", 2 * h + j + 1))
                    src = (Q1 if x == "q" else K1)[0:QK, h, :]
                    mm(ps[0:QK, :], cc("perm96", slice(0, QK), QK), src, start=True, stop=True).then_inc(pe.fills(f"{x}p{h}"), 1)

            def scores(n):
                h, i_ = units1[n]
                pe.e.wait_ge(*pe.emptied(f"ms{h}_{i_}"))
                ps = bank_of(f"ms{h}_{i_}")
                if i_ == 0:
                    pe.e.wait_ge(*pe.nth("qkrot", 2 * h + 2))
                i = mm(ps[:, 0:(i_ + 1) * P], Q1[0:QK, h, i_ * P:(i_ + 1) * P], K1[0:QK, h, 0:(i_ + 1) * P], start=True, stop=True)
                i.then_inc(pe.fills(f"ms{h}_{i_}"), 1)

            def turn(n):
                h, i_ = units1[n]
                pe.e.wait_ge(*pe.emptied(f"mt{h}_{i_}"))
                ps = bank_of(f"mt{h}_{i_}")
                pe.e.wait_ge(*pe.nth("mprob", n + 1))
                for j in range(i_ + 1):
                    i = nc.tensor.transpose(ps[:, j * P:(j + 1) * P], S1[:, n % 2, j * P:(j + 1) * P], ident)
                i.then_inc(pe.fills(f"mt{h}_{i_}"), 1)
                if i_ == NT - 1:
                    if h % 2 == 0:
                        pass
                    mo(h)

            def mo(h):
                job = f"mo{h // 2}"
                if h % 2 == 0:
                    return
                pe.e.wait_ge(*pe.emptied(job))
                ps = bank_of(job)
                for hh in (h - 1, h):
                    pe.e.wait_ge(*pe.taken(f"mt{hh}_{NT - 1}"))
                    pt = PTs[hh % 2]
                    for j in range(NT):
                        i = mm(ps[64 * (hh % 2):64 * (hh % 2) + 64, j * P:T], VT1[:, j, hh * 64:hh * 64 + 64],
                               pt[:, j, j * P:T], start=j == 0, stop=j == NT - 1)
                i.then_inc(pe.fills(job), 1)

            for n in range(len(units1)):
                scores(n)
                if n:
                    turn(n - 1)
            turn(len(units1) - 1)
            pe.e.wait_ge(*pe.emptied("moss"))
            ps = bank_of("moss")
            for c in range(4):
                pe.e.wait_ge(*pe.nth("mosq", c + 1))
                i = mm(ps[:, :], cc("ones"), TM[:, c, :], start=c == 0, stop=c == 3)
            i.then_inc(pe.fills("moss"), 1)
            for c in range(4):
                rwkv_pe(pe, c)
            for m in range(8):
                w = weights(pe, 18 + m)
                pe.e.wait_ge(*pe.emptied(f"wo{m}"))
                ps = bank_of(f"wo{m}")
                for k in range(KD):
                    if m == 0 and k == 0:
                        pe.e.wait_ge(*pe.nth("mla_out", 4))
                    if m == 0 and k == 4:
                        pe.e.wait_ge(*pe.nth("rw_out", 4))
                    i = mm(ps[:, :], w[:, k, :], H[:, k, :], start=k == 0, stop=k == KD - 1)
                i.then_inc(pe.fills(f"wo{m}"), 1)
            pe.e.wait_ge(*pe.emptied("ssq2"))
            ps = bank_of("ssq2")
            for c in range(KD):
                pe.e.wait_ge(*pe.nth("sq2", c + 1))
                i = mm(ps[:, :], cc("ones"), Q1[:, c, :], start=c == 0, stop=c == KD - 1)
            i.then_inc(pe.fills("ssq2"), 1)
            pe.e.wait_ge(*pe.emptied("route"))
            ps = bank_of("route")
            for i_ in range(NT):
                for k in range(KD):
                    pe.e.wait_ge(*pe.nth("h2", k + 1))
                    i = mm(ps[:, i_ * 36:i_ * 36 + 36], H[:, k, i_ * P:(i_ + 1) * P], par(p1, A1, "w_route", k * 36, 36),
                           start=k == 0, stop=k == KD - 1)
            i.then_inc(pe.fills("route"), 1)
            pe.e.wait_ge(*pe.emptied("combT"))
            ps = bank_of("combT")
            pe.e.wait_ge(*pe.nth("comb", 1))
            for i_ in range(NT):
                i = nc.tensor.transpose(ps[0:NE, i_ * P:(i_ + 1) * P], COMB[:, i_, :], ident)
            i.then_inc(pe.fills("combT"), 1)

        PTs = [PT1, ch(m0, 4)]

        def rwkv_pe(pe, c):
            e = pe.e
            pe.e.wait_ge(*pe.emptied(f"ru{c}"))
            ps = bank_of(f"ru{c}")
            if c == 0:
                pe.e.wait_ge(*pe.nth("wa_in", 1))
            cw = slice(c * P, (c + 1) * P)
            w2a2 = par(w1, W1, "w2a2", 0, 512)
            mm(ps[:, :], w2a2[0:64, cw], RAW[0:64, 12, 1:513], start=True, stop=True).then_inc(pe.fills(f"ru{c}"), 1)
            pe.e.wait_ge(*pe.emptied(f"ra{c}"))
            ps = bank_of(f"ra{c}")
            mm(ps[:, :], w2a2[64:128, cw], RAW[64:128, 12, 1:513], start=True, stop=True).then_inc(pe.fills(f"ra{c}"), 1)
            pe.e.wait_ge(*pe.emptied(f"rg{c}"))
            ps = bank_of(f"rg{c}")
            if c == 0:
                pe.e.wait_ge(*pe.nth("gl_in", 1))
            mm(ps[:, :], par(w1, W1, "g2", c * P, P), RAW[:, 13, 1:513], start=True, stop=True).then_inc(pe.fills(f"rg{c}"), 1)
            pe.e.wait_ge(*pe.emptied(f"rkk{c}"))
            ps = bank_of(f"rkk{c}")
            pe.e.wait_ge(*pe.nth("kksq", c + 1))
            mm(ps[:, :], cc("blk64"), W["SQ"], start=True, stop=True).then_inc(pe.fills(f"rkk{c}"), 1)
            pe.e.wait_ge(*pe.emptied(f"rb{c}"))
            ps = bank_of(f"rb{c}")
            pe.e.wait_ge(*pe.nth("rkr", c + 1))
            mm(ps[:, :], cc("blk64"), W["Y"], start=True, stop=True).then_inc(pe.fills(f"rb{c}"), 1)
            for j, (x, src) in enumerate((("v", RAW[:, 8 + c, 1:513]), ("b", W["BH"]), ("k", W["KH"]))):
                pe.e.wait_ge(*pe.emptied(f"rt{c}_{x}"))
                ps = bank_of(f"rt{c}_{x}")
                pe.e.wait_ge(*pe.nth("hats", c + 1))
                for i_ in range(NT):
                    i = nc.tensor.transpose(ps[:, i_ * P:(i_ + 1) * P], src[:, i_ * P:(i_ + 1) * P], ident)
                i.then_inc(pe.fills(f"rt{c}_{x}"), 1)
            pairs = {"abT": ("AT", "BT"), "ab": ("BT", "AT"), "ak": ("KT", "AT"), "br": ("BT", "RT"), "kr": ("KT", "RT")}
            for hh in range(2):
                hp = slice(64 * hh, 64 * hh + 64)
                for x, (l_, r_) in pairs.items():
                    pe.e.wait_ge(*pe.emptied(f"m{x}{c}_{hh}"))
                    ps = bank_of(f"m{x}{c}_{hh}")
                    for i_ in range(NT):
                        tk = slice(i_ * P, (i_ + 1) * P)
                        i = mm(ps[:, tk], W[l_][hp, tk], W[r_][hp, tk], start=True, stop=True)
                    i.then_inc(pe.fills(f"m{x}{c}_{hh}"), 1)
            for lev in (2, 4, 8, 16, 32):
                for hh in range(2):
                    pe.e.wait_ge(*pe.emptied(f"ix{c}_{lev}_{hh}"))
                    ps = bank_of(f"ix{c}_{lev}_{hh}")
                    pe.e.wait_ge(*pe.nth("tinv", 2 * c + hh + 1)) if lev == 2 else pe.e.wait_ge(*pe.taken(f"iy{c}_{lev // 2}_{hh}"))
                    for i_ in range(NT):
                        tk = slice(i_ * P, (i_ + 1) * P)
                        i = mm(ps[:, tk], W[f"MT{hh}"][:, tk], W[f"TI{hh}"][:, tk], start=True, stop=True)
                    i.then_inc(pe.fills(f"ix{c}_{lev}_{hh}"), 1)
                for hh in range(2):
                    pe.e.wait_ge(*pe.taken(f"ix{c}_{lev}_{hh}"))
                    for x, l_, r_ in (("y", "TT", "XX"), ("z", "XX", "TT")):
                        if x == "z" and lev == 32:
                            continue
                        pe.e.wait_ge(*pe.emptied(f"i{x}{c}_{lev}_{hh}"))
                        ps = bank_of(f"i{x}{c}_{lev}_{hh}")
                        for i_ in range(NT):
                            tk = slice(i_ * P, (i_ + 1) * P)
                            i = mm(ps[:, tk], W[f"{l_}{hh}"][:, tk], W[f"{r_}{hh}"][:, tk], start=True, stop=True)
                        i.then_inc(pe.fills(f"i{x}{c}_{lev}_{hh}"), 1)
            for n in range(NCH):
                i_, pp = n // 2, n % 2
                tp = slice(64 * pp, 64 * pp + 64)
                blk = slice(i_ * P + 64 * pp, i_ * P + 64 * pp + 64)
                tk = slice(n * 64, n * 64 + 64)
                hps = [slice(0, 64), slice(64, 128)]
                if n == 0:
                    for hh in range(2):
                        pe.e.wait_ge(*pe.taken(f"iy{c}_32_{hh}"))
                pe.e.wait_ge(*pe.emptied(f"cw{c}_{n}"))
                ps = bank_of(f"cw{c}_{n}")
                if n:
                    pe.e.wait_ge(*pe.taken(f"cs{c}_{n - 1}"))
                if n:
                    mm(ps[tp, 0:P], W["AT"][:, tk], W["ST"], start=True, stop=True)
                for hh in range(2):
                    i = mm(ps[tp, hps[hh]], W[f"MK{hh}"][:, blk], W["TKV"][:, i_ * P + 64 * hh:i_ * P + 64 * hh + 64],
                           start=n == 0, stop=True, skip_group_check=True)
                i.then_inc(pe.fills(f"cw{c}_{n}"), 1)
                pe.e.wait_ge(*pe.emptied(f"cu{c}_{n}"))
                ps = bank_of(f"cu{c}_{n}")
                pe.e.wait_ge(*pe.taken(f"cw{c}_{n}"))
                for hh in range(2):
                    i = mm(ps[tp, hps[hh]], W[f"TI{hh}"][:, blk], W["WS"][:, hps[hh]], start=True, stop=True)
                i.then_inc(pe.fills(f"cu{c}_{n}"), 1)
                pe.e.wait_ge(*pe.emptied(f"cy{c}_{n}"))
                ps = bank_of(f"cy{c}_{n}")
                pe.e.wait_ge(*pe.taken(f"cu{c}_{n}"))
                if n:
                    mm(ps[:, 0:64], W["ST"], W["RT"][:, tk], start=True, stop=True)
                for hh in range(2):
                    hp = hps[hh]
                    mm(ps[hp, 0:64], W["US"][:, hp], W[f"MB{hh}"][:, blk], start=n == 0, stop=True, skip_group_check=True)
                    i = mm(ps[hp, 0:64], W["TKV"][:, i_ * P + 64 * hh:i_ * P + 64 * hh + 64], W[f"MR{hh}"][:, blk],
                           start=False, stop=True, skip_group_check=True)
                i.then_inc(pe.fills(f"cy{c}_{n}"), 1)
                if n < NCH - 1:
                    pe.e.wait_ge(*pe.emptied(f"cs{c}_{n}"))
                    ps = bank_of(f"cs{c}_{n}")
                    for hh in range(2):
                        hp = hps[hh]
                        fe = slice(i_ * P + 64 * hh, i_ * P + 64 * hh + 64)
                        mm(ps[hp, 0:64], W["TKB"][tp, fe], W["US"][tp, hp], start=True, stop=False)
                        i = mm(ps[hp, 0:64], W["TKK"][tp, fe], W["TKV"][tp, fe], start=False, stop=True)
                    i.then_inc(pe.fills(f"cs{c}_{n}"), 1)
            pe.e.wait_ge(*pe.emptied(f"gm{c}"))
            ps = bank_of(f"gm{c}")
            pe.e.wait_ge(*pe.taken(f"cy{c}_{NCH - 1}"))
            mm(ps[:, :], cc("blk64"), W["Y"], start=True, stop=True).then_inc(pe.fills(f"gm{c}"), 1)
            pe.e.wait_ge(*pe.emptied(f"gv{c}"))
            ps = bank_of(f"gv{c}")
            pe.e.wait_ge(*pe.nth("gnsq", c + 1))
            mm(ps[:, :], cc("blk64"), W["SQ"], start=True, stop=True).then_inc(pe.fills(f"gv{c}"), 1)

        def act_A(sc):
            e = sc.e
            e.wait_ge(ev("x_in"), 16)
            for c in range(KD):
                act_(Q1[:, c, :], X[:, c, :], ACT.Square).then_inc(sc.tells("sq1"), 1)
            sc.e.wait_ge(*sc.filled("ssq1"))
            ps = bank_of("ssq1")
            sc.e.wait_ge(*sc.nth("bias_cols", 3))
            act_(TM[:, 0, :], ps[:, :], ACT.Sqrt, EPS, 1.0 / D).then_inc(sc.takes("ssq1"), 1)
            for n, o in enumerate((COS, SIN)):
                sc.e.wait_ge(*sc.nth("angles", n + 1))
                act_(o[0:QK, 0, :], o[0:QK, 0, :], ACT.Sin).then_inc(sc.tells("sines"), 1)
            for m in range(18):
                sc.e.wait_ge(*sc.filled(f"win{m}"))
                ps = bank_of(f"win{m}")
                if m < 3:
                    o = CQ[:, m, :]
                elif m == 3:
                    act_(KR[64:96, 0, :], ps[64:96, :], ACT.Copy).then_inc(sc.takes("win3"), 1)
                    continue
                else:
                    k = {4: 12, 5: 13}.get(m, m - 6)
                    o = RAW[:, k, 1:513]
                if m < 3:
                    if m == 0:
                        sc.e.wait_ge(*sc.taken("ssq1"))
                        sc.e.wait_ge(*sc.nth("h1", 8))
                    act_(o, ps[:, :], ACT.Copy).then_inc(sc.takes(f"win{m}"), 1)
                    sc.e.wait_ge(*sc.taken(f"win{m}"))
                    act_(TM[:, m, :], o, ACT.Square).then_inc(sc.tells("cqsq"), 1)
                else:
                    act_(o, ps[:, :], ACT.Copy).then_inc(sc.takes(f"win{m}"), 1)
            for j, (x, n, k) in enumerate((("cqss", QR, 3), ("ckvss", KVR, 4))):
                sc.e.wait_ge(*sc.filled(x))
                ps = bank_of(x)
                act_(TM[:, k, :], ps[:, :], ACT.Sqrt, EPS, 1.0 / n).then_inc(sc.takes(x), 1)
            for i_ in range(NT):
                sc.e.wait_ge(*sc.filled(f"vm{i_}"))
                ps = bank_of(f"vm{i_}")
                act_(VT1[:, i_, :], ps[:, :], ACT.Copy).then_inc(sc.takes(f"vm{i_}"), 1)
            for h in range(HM):
                for j, x in enumerate("qk"):
                    sc.e.wait_ge(*sc.taken(f"q{h}")) if x == "q" else sc.e.wait_ge(*sc.nth("kev", h + 1))
                    if h:
                        sc.e.wait_ge(*sc.filled(f"{x}ss{h - 1}"))
                    act_(TM[0:QK, j, :], (Q1 if x == "q" else K1)[0:QK, h, :], ACT.Square).then_inc(sc.tells("qksq"), 1)
                for j, x in enumerate("qk"):
                    sc.e.wait_ge(*sc.filled(f"{x}ss{h}"))
                    ps = bank_of(f"{x}ss{h}")
                    if h:
                        sc.e.wait_ge(*sc.nth("qkn", 2 * h - 1 + j))
                    act_(TM[0:QK, 2 + j, :], ps[0:QK, :], ACT.Sqrt, EPS, 1.0 / QK).then_inc(sc.takes(f"{x}ss{h}"), 1)
            for n, (h, i_) in enumerate(units1):
                sc.e.wait_ge(*sc.nth("mmax", n + 1))
                w = (i_ + 1) * P
                s = S1[:, n % 2, 0:w]
                act_(s, s, ACT.Exp, bias=small[:, 2 + n % 2:3 + n % 2], accum=small[:, 4 + n % 2:5 + n % 2]).then_inc(sc.tells("mexp"), 1)
                if n:
                    mla_turned(sc, n - 1)
            mla_turned(sc, len(units1) - 1)
            for c in range(4):
                sc.e.wait_ge(*sc.taken(f"mo{c}"))
                act_(TM[:, c, :], OM[:, c, :], ACT.Square).then_inc(sc.tells("mosq"), 1)
            sc.e.wait_ge(*sc.filled("moss"))
            ps = bank_of("moss")
            act_(TM[:, 4, :], ps[:, :], ACT.Sqrt, EPS, 1.0 / 512).then_inc(sc.takes("moss"), 1)
            sc.e.wait_ge(*sc.nth("shifted", 14))
            act_(RAW[0:64, 12, 1:513], RAW[0:64, 12, 1:513], ACT.Tanh).then_inc(sc.tells("wa_in"), 1)
            act_(RAW[:, 13, 1:513], RAW[:, 13, 1:513], ACT.Tanh, scale=0.5).then_inc(sc.tells("gl_t"), 1)
            for c in range(4):
                rwkv_act(sc, c)
            for c in range(KD):
                sc.e.wait_ge(*sc.taken(f"wo{c}"))
                act_(Q1[:, c, :], X[:, c, :], ACT.Square).then_inc(sc.tells("sq2"), 1)
            sc.e.wait_ge(*sc.filled("ssq2"))
            ps = bank_of("ssq2")
            act_(TM[:, 0, :], ps[:, :], ACT.Sqrt, EPS, 1.0 / D).then_inc(sc.takes("ssq2"), 1)
            sc.e.wait_ge(*sc.nth("gsub", 1))
            act_(RT("gexp"), RT("gsub"), ACT.Exp).then_inc(sc.tells("gexp"), 1)
            sc.e.wait_ge(*sc.nth("vdiff", 1))
            act_(RT("e21"), RT("vdiff"), ACT.Exp).then_inc(sc.tells("e21"), 1)
            sc.e.wait_ge(*sc.filled("combT"))
            ps = bank[JOB["combT"][1] % 8]
            act_(CT[0:NE, 0, :], ps[0:NE, :], ACT.Copy).then_inc(sc.takes("combT"), 1)
            sc.e.wait_ge(*sc.taken("combT"))
            e.dma_start(scratch, CT[0:NE, 0, :]).then_inc(ev("comb_stored"), 16)

        def mla_turned(sc, n):
            h, i_ = units1[n]
            sc.e.wait_ge(*sc.filled(f"mt{h}_{i_}"))
            ps = bank_of(f"mt{h}_{i_}")
            if i_ == 0 and h >= 2:
                sc.e.wait_ge(*sc.filled(f"mo{(h - 2) // 2}"))
            o = PTs[h % 2][:, 0:i_ + 1, i_ * P:(i_ + 1) * P]
            act_(o, ps[:, 0:(i_ + 1) * P].rearrange("p (n w) -> p n w", n=i_ + 1), ACT.Copy).then_inc(sc.takes(f"mt{h}_{i_}"), 1)

        def rwkv_act(sc, c):
            if c == 0:
                sc.e.wait_ge(*sc.nth("mla_out", 4))
            else:
                sc.e.wait_ge(*sc.nth("rw_out", c))
            sc.e.wait_ge(*sc.nth("halves", 2))
            sc.e.wait_ge(*sc.filled(f"ru{c}"))
            ps = bank_of(f"ru{c}")
            act_(W["LW"], ps[:, :], ACT.Tanh, bias=small[:, 8 + c:9 + c], scale=0.5).then_inc(sc.takes(f"ru{c}"), 1)
            sc.e.wait_ge(*sc.filled(f"ra{c}"))
            ps = bank_of(f"ra{c}")
            act_(W["A"], ps[:, :], ACT.Tanh, bias=small[:, 12 + c:13 + c], scale=0.5).then_inc(sc.takes(f"ra{c}"), 1)
            sc.e.wait_ge(*sc.filled(f"rg{c}"))
            ps = bank_of(f"rg{c}")
            act_(W["G"], ps[:, :], ACT.Copy).then_inc(sc.takes(f"rg{c}"), 1)
            sc.e.wait_ge(*sc.nth("kk0", c + 1))
            act_(W["SQ"], W["KK"], ACT.Square).then_inc(sc.tells("kksq"), 1)
            sc.e.wait_ge(*sc.filled(f"rkk{c}"))
            ps = bank_of(f"rkk{c}")
            act_(W["RS"], ps[:, :], ACT.Sqrt, 1e-12).then_inc(sc.takes(f"rkk{c}"), 1)
            sc.e.wait_ge(*sc.nth("scan", 2 * c + 1))
            act_(W["EL"], W["L"], ACT.Exp).then_inc(sc.chained(), 1)
            act_(W["ENL"], W["L"], ACT.Exp, scale=-1.0).then_inc(sc.chained(), 1)
            sc.e.wait_ge(*sc.nth("scan", 2 * c + 2))
            act_(W["ELX"], W["ELX"], ACT.Exp).then_inc(sc.tells("explog"), 1)
            for x, d in (("v", "TKV"), ("b", "TKB"), ("k", "TKK")):
                sc.e.wait_ge(*sc.filled(f"rt{c}_{x}"))
                ps = bank_of(f"rt{c}_{x}")
                act_(W[d], ps[:, :], ACT.Copy).then_inc(sc.takes(f"rt{c}_{x}"), 1)
            for n in range(NCH):
                pp = n % 2
                sc.e.wait_ge(*sc.filled(f"cy{c}_{n}"))
                ps = bank_of(f"cy{c}_{n}")
                if n == 0:
                    sc.e.wait_ge(*sc.taken(f"rb{c}"))
                act_(W["Y"][:, n * 64:n * 64 + 64], ps[:, 0:64], ACT.Copy).then_inc(sc.takes(f"cy{c}_{n}"), 1)
            sc.e.wait_ge(*sc.taken(f"gm{c}"))
            act_(W["SQ"], W["L"], ACT.Square).then_inc(sc.tells("gnsq"), 1)
            sc.e.wait_ge(*sc.filled(f"gv{c}"))
            ps = bank_of(f"gv{c}")
            act_(W["RS"], ps[:, :], ACT.Sqrt, LNX_EPS, 1.0 / RN).then_inc(sc.takes(f"gv{c}"), 1)

        def dve_A(dv):
            e = dv.e
            for i, v in enumerate((EPS, 1e-12, LNX_EPS)):
                V.memset(small[:, 60 + i:61 + i], v).then_inc(dv.tells("bias_cols"), 1)
            V.memset(RAW[:, :, 0:1], 0.0).then_inc(dv.chained(), 1)
            e.wait_ge(ev("pos_in"), 16)
            e.wait_ge(ev("consts_in"), 16)
            e.wait_ge(ev("p1_in"), 16)
            e.wait_ge(ev("x_in"), 16)
            pos = PT1[0:QK, 0, :].bitcast(I32)
            ang, kf, r = PT1[0:QK, 1, :], PT1[0:QK, 2, :], PT1[0:QK, 3, :]
            V.tensor_copy(ang, pos).then_inc(dv.chained(), 1); dv.e.wait_ge(dv.chain, dv.n)
            ts(ang, ang, cc("inv_freq", slice(0, QK)), None, ALU.mult).then_inc(dv.chained(), 1); dv.e.wait_ge(dv.chain, dv.n)
            MAGIC, C1, C2 = 12582912.0, 6.28125, 0.0019353071795864769
            for quarter, o in ((0.25, COS), (0.0, SIN)):
                o = o[0:QK, 0, :]
                ts(kf, ang, 0.15915494309189535, quarter, ALU.mult, ALU.add).then_inc(dv.chained(), 1); dv.e.wait_ge(dv.chain, dv.n)
                ts(kf, kf, MAGIC, None, ALU.add).then_inc(dv.chained(), 1); dv.e.wait_ge(dv.chain, dv.n)
                ts(kf, kf, -MAGIC, None, ALU.add).then_inc(dv.chained(), 1); dv.e.wait_ge(dv.chain, dv.n)
                stt(r, kf, -C1, ang, ALU.mult, ALU.add).then_inc(dv.chained(), 1); dv.e.wait_ge(dv.chain, dv.n)
                stt(r, kf, -C2, r, ALU.mult, ALU.add).then_inc(dv.chained(), 1); dv.e.wait_ge(dv.chain, dv.n)
                if quarter:
                    ts(r, r, 1.5707963267948966, None, ALU.add).then_inc(dv.chained(), 1); dv.e.wait_ge(dv.chain, dv.n)
                ts(o, r, 3.1415925, -3.1415925, ALU.min, ALU.max).then_inc(dv.tells("angles"), 1)
            norm(dv, "ssq1", X, H, lambda c: par(p1, A1, "g_mix", c), TM[:, 0, :], "h1")
            for x, ks, t, g in (("cqss", (0, 1), 3, "g_cq"), ("ckvss", (2,), 4, "g_ckv")):
                dv.e.wait_ge(*dv.taken(x))
                V.reciprocal(TM[:, t, :], TM[:, t, :]).then_inc(dv.chained(), 1); dv.e.wait_ge(dv.chain, dv.n)
                for k in ks:
                    stt(CQ[:, k, :], CQ[:, k, :], par(p1, A1, g, k if k < 2 else 0), TM[:, t, :], ALU.mult, ALU.mult).then_inc(dv.tells("cqn"), 1)
            dv.e.wait_ge(*dv.nth("sines", 2))
            for h in range(HM):
                dv.e.wait_ge(*dv.filled(f"q{h}"))
                ps = bank_of(f"q{h}")
                V.tensor_copy(Q1[0:QK, h, :], ps[0:QK, :]).then_inc(dv.takes(f"q{h}"), 1)
                dv.e.wait_ge(*dv.filled(f"k{h}"))
                ps = bank_of(f"k{h}")
                V.tensor_copy(K1[0:NOPE, h, :], ps[0:NOPE, :]).then_inc(dv.takes(f"k{h}"), 1)
                if h == 0:
                    dv.e.wait_ge(*dv.taken("win3"))
                V.tensor_copy(K1[NOPE:QK, h, :], KR[64:96, 0, :]).then_inc(dv.tells("kev"), 1)
                dv.e.wait_ge(*dv.nth("kev", h + 1))
                for j, x in enumerate("qk"):
                    dst = (Q1 if x == "q" else K1)[0:QK, h, :]
                    dv.e.wait_ge(*dv.taken(f"{x}ss{h}"))
                    V.reciprocal(TM[0:QK, 2 + j, :], TM[0:QK, 2 + j, :]).then_inc(dv.chained(), 1); dv.e.wait_ge(dv.chain, dv.n)
                    stt(dst, dst, par(p1, A1, f"g_{x}n", p=slice(0, QK)), TM[0:QK, 2 + j, :], ALU.mult, ALU.mult).then_inc(dv.tells("qkn"), 1)
                for j, x in enumerate("qk"):
                    dst = (Q1 if x == "q" else K1)[0:QK, h, :]
                    dv.e.wait_ge(*dv.filled(f"{x}p{h}"))
                    ps = bank_of(f"{x}p{h}")
                    tt(TM[0:QK, 4 + j, :], ps[0:QK, :], SIN[0:QK, 0, :], ALU.mult).then_inc(dv.takes(f"{x}p{h}"), 1)
                    dv.e.wait_ge(*dv.nth("qkn", 2 * h + 1 + j))
                    tt(dst, dst, COS[0:QK, 0, :], ALU.mult).then_inc(dv.chained(), 1); dv.e.wait_ge(dv.chain, dv.n)
                    dv.e.wait_ge(*dv.taken(f"{x}p{h}"))
                    tt(dst, dst, TM[0:QK, 4 + j, :], ALU.add).then_inc(dv.tells("qkrot"), 1)
            for n in range(len(units1)):
                mla_scores_dve(dv, n)
                if n:
                    mla_prob_dve(dv, n - 1)
            mla_prob_dve(dv, len(units1) - 1)
            dv.e.wait_ge(*dv.taken("mo3"))
            dv.e.wait_ge(*dv.taken("moss"))
            V.reciprocal(TM[:, 4, :], TM[:, 4, :]).then_inc(dv.chained(), 1); dv.e.wait_ge(dv.chain, dv.n)
            for c in range(4):
                stt(H[:, c, :], OM[:, c, :], par(p1, A1, "g_mla_out", c), TM[:, 4, :], ALU.mult, ALU.mult).then_inc(dv.tells("mla_out"), 1)
            dv.e.wait_ge(*dv.nth("mla_out", 4))
            for c0 in range(0, 14, 4):
                cs = range(c0, min(14, c0 + 4))
                for c in cs:
                    dv.e.wait_ge(*dv.taken(f"win{ {12: 4, 13: 5}.get(c, c + 6)}"))
                    tt(TM[:, c - c0, :], RAW[:, c, 0:512], RAW[:, c, 1:513], ALU.subtract).then_inc(dv.chained(), 1)
                dv.e.wait_ge(dv.chain, dv.n)
                for c in cs:
                    stt(RAW[:, c, 1:513], TM[:, c - c0, :], par(p1, A1, "mu", c), RAW[:, c, 1:513], ALU.mult, ALU.add).then_inc(dv.tells("shifted"), 1)
                dv.e.wait_ge(*dv.nth("shifted", cs[-1] + 1))
            ts(small[:, 8:12], par(p1, A1, "w0", 0, 4), 0.5, None, ALU.mult).then_inc(dv.tells("halves"), 1)
            ts(small[:, 12:16], par(p1, A1, "a0", 0, 4), 0.5, None, ALU.mult).then_inc(dv.tells("halves"), 1)
            dv.e.wait_ge(*dv.nth("gl_t", 1))
            ts(RAW[:, 13, 1:513], RAW[:, 13, 1:513], 0.5, 0.5, ALU.mult, ALU.add).then_inc(dv.tells("gl_in"), 1)
            for c in range(4):
                rwkv_dve(dv, c)
            for m in range(8):
                dv.e.wait_ge(*dv.filled(f"wo{m}"))
                ps = bank_of(f"wo{m}")
                tt(X[:, m, :], X[:, m, :], ps[:, :], ALU.add).then_inc(dv.takes(f"wo{m}"), 1)
            dv.e.wait_ge(*dv.taken("wo7"))
            norm(dv, "ssq2", X, H, lambda c: par(p1, A1, "g_ffn", c), TM[:, 0, :], "h2")
            router(dv)

        def norm(dv, job, src, dst, g, r, event):
            dv.e.wait_ge(*dv.taken(job))
            V.reciprocal(r, r).then_inc(dv.chained(), 1); dv.e.wait_ge(dv.chain, dv.n)
            for c in range(KD):
                stt(dst[:, c, :], src[:, c, :], g(c), r, ALU.mult, ALU.mult).then_inc(dv.tells(event), 1)

        def mla_scores_dve(dv, n):
            h, i_ = units1[n]
            w = (i_ + 1) * P
            dv.e.wait_ge(*dv.filled(f"ms{h}_{i_}"))
            ps = bank_of(f"ms{h}_{i_}")
            if n >= 2:
                dv.e.wait_ge(*dv.filled("mt%d_%d" % units1[n - 2]))
            s = small[:, n % 2:n % 2 + 1]
            V.tensor_tensor_reduce(S1[:, n % 2, 0:w], ps[:, 0:w], cc("causal")[:, 512 - w:512], QK ** -0.5, 3 * NEG,
                                           ALU.add, ALU.max, s).then_inc(dv.takes(f"ms{h}_{i_}"), 1)
            dv.e.wait_ge(*dv.taken(f"ms{h}_{i_}"))
            ts(small[:, 2 + n % 2:3 + n % 2], s, -1.0, None, ALU.mult).then_inc(dv.tells("mmax"), 1)

        def mla_prob_dve(dv, n):
            h, i_ = units1[n]
            w = (i_ + 1) * P
            dv.e.wait_ge(*dv.nth("mexp", n + 1))
            r = small[:, 6 + n % 2:7 + n % 2]
            V.reciprocal(r, small[:, 4 + n % 2:5 + n % 2]).then_inc(dv.chained(), 1); dv.e.wait_ge(dv.chain, dv.n)
            ts(S1[:, n % 2, 0:w], S1[:, n % 2, 0:w], r, None, ALU.mult).then_inc(dv.tells("mprob"), 1)
            if i_ == NT - 1 and h % 2 == 1:
                pass
            if n >= 4 and i_ == 1 and h % 2 == 0 and h:
                p = h // 2 - 1
                dv.e.wait_ge(*dv.filled(f"mo{p}"))
                ps = bank_of(f"mo{p}")
                V.tensor_copy(OM[:, p, :], ps[:, :]).then_inc(dv.takes(f"mo{p}"), 1)
            if n == len(units1) - 1:
                dv.e.wait_ge(*dv.filled("mo3"))
                ps = bank_of("mo3")
                V.tensor_copy(OM[:, 3, :], ps[:, :]).then_inc(dv.takes("mo3"), 1)

        def rwkv_dve(dv, c):
            r_, k_, v_ = (RAW[:, j + c, 1:513] for j in (0, 4, 8))
            w = W
            one = lambda n, i=None: par(p1, A1, n, c)
            if c == 0:
                dv.e.wait_ge(dv.chain, dv.n)
            dv.e.wait_ge(*dv.taken(f"ru{c}")); dv.e.wait_ge(*dv.taken(f"ra{c}"))
            ts(w["LW"], w["LW"], -0.5 * EXP_NEG_HALF, -0.5 * EXP_NEG_HALF, ALU.mult, ALU.add).then_inc(dv.chained(), 1)
            ts(w["A"], w["A"], 0.5, 0.5, ALU.mult, ALU.add).then_inc(dv.chained(), 1)
            ts(w["KK"], k_, one("k_k"), None, ALU.mult).then_inc(dv.tells("kk0"), 1)
            dv.e.wait_ge(dv.chain, dv.n)
            V.tensor_tensor_scan(w["L"], cc("scan_keep"), w["LW"], 0.0, ALU.mult, ALU.add).then_inc(dv.tells("scan"), 1)
            dv.e.wait_ge(*dv.nth("scan", 2 * c + 1))
            tt(w["ELX"], w["L"], w["LW"], ALU.subtract).then_inc(dv.tells("scan"), 1)
            ts(w["B"], w["A"], -1.0, one("k_a"), ALU.add, ALU.mult).then_inc(dv.chained(), 1); dv.e.wait_ge(dv.chain, dv.n)
            stt(w["KP"], w["B"], 1.0, k_, ALU.add, ALU.mult).then_inc(dv.chained(), 1); dv.e.wait_ge(dv.chain, dv.n)
            stt(w["Y"], r_, one("r_k"), w["KP"], ALU.mult, ALU.mult).then_inc(dv.tells("rkr"), 1)
            dv.e.wait_ge(*dv.taken(f"rkk{c}"))
            V.reciprocal(w["RS"], w["RS"]).then_inc(dv.chained(), 1); dv.e.wait_ge(dv.chain, dv.n)
            tt(w["KK"], w["KK"], w["RS"], ALU.mult).then_inc(dv.chained(), 1); dv.e.wait_ge(dv.chain, dv.n)
            tt(w["B"], w["KK"], w["A"], ALU.mult).then_inc(dv.chained(), 1)
            dv.e.wait_ge(*dv.filled(f"rb{c}"))
            ps = bank_of(f"rb{c}")
            tt(w["BON"], ps[:, :], v_, ALU.mult).then_inc(dv.takes(f"rb{c}"), 1)
            dv.e.wait_ge(dv.chain, dv.n)
            dv.e.wait_ge(*dv.nth("explog", c + 1))
            stt(w["AT"], w["KK"], -1.0, w["ELX"], ALU.mult, ALU.mult).then_inc(dv.chained(), 1)
            tt(w["BT"], w["B"], w["ENL"], ALU.mult).then_inc(dv.chained(), 1)
            tt(w["KT"], w["KP"], w["ENL"], ALU.mult).then_inc(dv.chained(), 1)
            tt(w["RT"], r_, w["EL"], ALU.mult).then_inc(dv.chained(), 1); dv.e.wait_ge(dv.chain, dv.n)
            c64 = lambda a: a.rearrange("p (n w) -> p n w", n=NCH)
            dc = c64(w["EL"])[:, :, 63:64].to_broadcast([P, NCH, 64])
            tt(c64(w["BH"]), c64(w["BT"]), dc, ALU.mult).then_inc(dv.chained(), 1)
            tt(c64(w["KH"]), c64(w["KT"]), dc, ALU.mult).then_inc(dv.tells("hats"), 1)
            for hh in range(2):
                dv.e.wait_ge(*dv.filled(f"mabT{c}_{hh}"))
                ps = bank_of(f"mabT{c}_{hh}")
                tt(tiles4(w[f"MT{hh}"]), tiles4(ps[:, :]), over4(cc("lower")), ALU.mult).then_inc(dv.chained(), 1)
                tt(tiles4(w[f"TT{hh}"]), tiles4(ps[:, :]), over4(cc("lev1T")), ALU.mult).then_inc(dv.takes(f"mabT{c}_{hh}"), 1)
                dv.e.wait_ge(*dv.taken(f"mabT{c}_{hh}"))
                tt(tiles4(w[f"TT{hh}"]), tiles4(w[f"TT{hh}"]), over4(ident), ALU.add).then_inc(dv.chained(), 1)
                dv.e.wait_ge(*dv.filled(f"mab{c}_{hh}"))
                ps = bank_of(f"mab{c}_{hh}")
                tt(tiles4(w[f"TI{hh}"]), tiles4(ps[:, :]), over4(cc("lev1")), ALU.mult).then_inc(dv.takes(f"mab{c}_{hh}"), 1)
                dv.e.wait_ge(*dv.taken(f"mab{c}_{hh}"))
                tt(tiles4(w[f"TI{hh}"]), tiles4(w[f"TI{hh}"]), over4(ident), ALU.add).then_inc(dv.tells("tinv"), 1)
                for x, d, m in (("ak", "MK", "upper"), ("br", "MB", "upper_eq"), ("kr", "MR", "upper_eq")):
                    dv.e.wait_ge(*dv.filled(f"m{x}{c}_{hh}"))
                    ps = bank_of(f"m{x}{c}_{hh}")
                    tt(tiles4(w[f"{d}{hh}"]), tiles4(ps[:, :]), over4(cc(m)), ALU.mult).then_inc(dv.takes(f"m{x}{c}_{hh}"), 1)
            for n, lev in enumerate((2, 4, 8, 16, 32)):
                for hh in range(2):
                    dv.e.wait_ge(*dv.filled(f"ix{c}_{lev}_{hh}"))
                    ps = bank_of(f"ix{c}_{lev}_{hh}")
                    tt(tiles4(w[f"XX{hh}"]), tiles4(ps[:, :]), over4(cc(f"lev{lev}")), ALU.mult).then_inc(dv.takes(f"ix{c}_{lev}_{hh}"), 1)
                for hh in range(2):
                    dv.e.wait_ge(*dv.nth("tinv", 2 * c + hh + 1)) if lev == 2 else dv.e.wait_ge(*dv.taken(f"iy{c}_{lev // 2}_{hh}"))
                    if lev != 32:
                        dv.e.wait_ge(*dv.filled(f"iz{c}_{lev}_{hh}"))
                        ps2 = bank_of(f"iz{c}_{lev}_{hh}")
                        dv.e.wait_ge(*dv.filled(f"iy{c}_{lev}_{hh}"))
                        ps = bank_of(f"iy{c}_{lev}_{hh}")
                        tt(w[f"TT{hh}"], w[f"TT{hh}"], ps2[:, :], ALU.add).then_inc(dv.takes(f"iz{c}_{lev}_{hh}"), 1)
                    else:
                        dv.e.wait_ge(*dv.filled(f"iy{c}_{lev}_{hh}"))
                        ps = bank_of(f"iy{c}_{lev}_{hh}")
                    tt(w[f"TI{hh}"], w[f"TI{hh}"], ps[:, :], ALU.add).then_inc(dv.takes(f"iy{c}_{lev}_{hh}"), 1)
            dcol = c64(w["EL"])[:, :, 63]
            for x in ("ST", "WS", "US"):
                V.memset(w[x], 0.0).then_inc(dv.chained(), 1)
            dv.e.wait_ge(dv.chain, dv.n)
            for n in range(NCH):
                tp = slice(64 * (n % 2), 64 * (n % 2) + 64)
                dv.e.wait_ge(*dv.filled(f"cw{c}_{n}"))
                ps = bank_of(f"cw{c}_{n}")
                V.tensor_copy(w["WS"][tp, :], ps[tp, 0:P]).then_inc(dv.takes(f"cw{c}_{n}"), 1)
                dv.e.wait_ge(*dv.filled(f"cu{c}_{n}"))
                ps = bank_of(f"cu{c}_{n}")
                V.tensor_copy(w["US"][tp, :], ps[tp, 0:P]).then_inc(dv.takes(f"cu{c}_{n}"), 1)
                if n < NCH - 1:
                    dv.e.wait_ge(*dv.filled(f"cs{c}_{n}"))
                    ps = bank_of(f"cs{c}_{n}")
                    if n:
                        dv.e.wait_ge(*dv.taken(f"cs{c}_{n - 1}"))
                    else:
                        dv.e.wait_ge(dv.chain, dv.n)
                    for hh in range(2):
                        hp = slice(64 * hh, 64 * hh + 64)
                        i = stt(w["ST"][hp, hp], w["ST"][hp, hp], dcol[hp, n:n + 1], ps[hp, 0:64], ALU.mult, ALU.add)
                    i.then_inc(dv.takes(f"cs{c}_{n}"), 1)
            dv.e.wait_ge(*dv.filled(f"gm{c}"))
            ps = bank_of(f"gm{c}")
            stt(w["L"], ps[:, :], -1.0 / RN, w["Y"], ALU.mult, ALU.add).then_inc(dv.takes(f"gm{c}"), 1)
            dv.e.wait_ge(*dv.taken(f"gv{c}"))
            V.reciprocal(w["RS"], w["RS"]).then_inc(dv.chained(), 1); dv.e.wait_ge(dv.chain, dv.n)
            stt(w["L"], w["L"], one("lnx_g"), w["RS"], ALU.mult, ALU.mult).then_inc(dv.chained(), 1); dv.e.wait_ge(dv.chain, dv.n)
            dv.e.wait_ge(*dv.taken(f"rb{c}"))
            stt(w["L"], w["L"], one("lnx_b"), w["BON"], ALU.add, ALU.add).then_inc(dv.chained(), 1); dv.e.wait_ge(dv.chain, dv.n)
            dv.e.wait_ge(*dv.taken(f"rg{c}"))
            tt(H[:, 4 + c, :], w["L"], w["G"], ALU.mult).then_inc(dv.tells("rw_out"), 1)

        rt_cols = [("lg", 144), ("gmax", 4), ("geq", 16), ("gidx", 16), ("gmin", 4), ("goh", 16), ("gsub", 16),
                   ("gexp", 16), ("gsum", 4), ("pg", 4), ("gpen", 16), ("me", 128), ("v1", 4), ("eq", 128),
                   ("idx", 128), ("imin", 4), ("oh1", 128), ("oh2", 128), ("v2", 4), ("vdiff", 4), ("e21", 4),
                   ("w1", 4), ("w2", 4), ("comb", 128)]
        RTC, nRT = offsets(rt_cols)
        rt0 = m0 + 3072 + 8192 + 8192
        def RT(n):
            o, w = RTC[n]
            return arena[:, rt0 + o:rt0 + o + w]
        COMB = RT("comb").rearrange("p (n e) -> p n e", n=NT)
        CT = ch(m0 + 3072 + 8192, 1)
        assert rt0 + nRT <= ARENA

        def router(dv):
            t = lambda n, e: RT(n).rearrange("p (n e) -> p n e", n=NT)
            st = lambda ins: (ins.then_inc(dv.chained(), 1), dv.e.wait_ge(dv.chain, dv.n))
            dv.e.wait_ge(*dv.filled("route"))
            ps = bank_of("route")
            lg = t("lg", 36)
            br = par(p1, A1, "b_route", 0, 36).unsqueeze(1).to_broadcast([P, NT, 36])
            tt(lg, ps[:, 0:144].rearrange("p (n e) -> p n e", n=NT), br, ALU.add).then_inc(dv.takes("route"), 1)
            dv.e.wait_ge(*dv.taken("route"))
            g = lg[:, :, 0:NG]
            x = lg[:, :, NG:36]
            bc = lambda n, e: t(n, 1).to_broadcast([P, NT, e])

            def first_max(src, mx, eq, idx, imin, oh, e, iota):
                st(V.tensor_reduce(t(mx, 1)[:, :, 0], src, AX.X, ALU.max))
                st(tt(t(eq, e), src, bc(mx, e), ALU.is_equal))
                it = cc(iota).unsqueeze(1).to_broadcast([P, NT, e])
                st(stt(t(idx, e), t(eq, e), -100.0, it, ALU.mult, ALU.add))
                st(V.tensor_reduce(t(imin, 1)[:, :, 0], t(idx, e), AX.X, ALU.min))
                st(tt(t(oh, e), t(idx, e), bc(imin, e), ALU.is_equal))

            first_max(g, "gmax", "geq", "gidx", "gmin", "goh", NG, "iota4")
            tt(t("gsub", NG), g, bc("gmax", NG), ALU.subtract).then_inc(dv.tells("gsub"), 1)
            st(ts(RT("gpen"), RT("goh"), -NEG, NEG, ALU.mult, ALU.add))
            me4 = RT("me").rearrange("p (n g e) -> p (n g) e", n=NT, g=NG)
            st(V.tensor_copy(t("me", 32), x))
            pen = RT("gpen").unsqueeze(2).to_broadcast([P, NT * NG, EG])
            st(tt(me4, me4, pen, ALU.add))
            first_max(t("me", 32), "v1", "eq", "idx", "imin", "oh1", NE, "iota32")
            st(stt(RT("me"), RT("oh1"), 3 * NEG, RT("me"), ALU.mult, ALU.add))
            first_max(t("me", 32), "v2", "eq", "idx", "imin", "oh2", NE, "iota32")
            tt(RT("vdiff"), RT("v2"), RT("v1"), ALU.subtract).then_inc(dv.tells("vdiff"), 1)
            dv.e.wait_ge(*dv.nth("gexp", 1))
            st(V.tensor_reduce(RT("gsum"), t("gexp", NG), AX.X, ALU.add))
            st(V.reciprocal(RT("pg"), RT("gsum")))
            dv.e.wait_ge(*dv.nth("e21", 1))
            st(ts(RT("w1"), RT("e21"), 1.0, None, ALU.add))
            st(V.reciprocal(RT("w1"), RT("w1")))
            st(tt(RT("w1"), RT("w1"), RT("pg"), ALU.mult))
            st(tt(RT("w2"), RT("w1"), RT("e21"), ALU.mult))
            st(tt(t("oh1", NE), t("oh1", NE), bc("w1", NE), ALU.mult))
            st(tt(t("oh2", NE), t("oh2", NE), bc("w2", NE), ALU.mult))
            tt(RT("comb"), RT("oh1"), RT("oh2"), ALU.add).then_inc(dv.tells("comb"), 1)

        HID = ch(m0, 2)
        TG = ch(m0 + 1024, 2)
        CB = ch(m0 + 2048, 1)

        def pe_M(pe):
            pe.sec = "M"
            with pe.e.Fori(0, NE) as l:
                pe.l = l
                for s, (x, k) in enumerate((("g", 0), ("u", 0), ("g", 1), ("u", 1))):
                    w = weights(pe, s, "M")
                    pe.e.wait_ge(*pe.emptied(f"m{x}{k}"))
                    ps = bank_of(f"m{x}{k}")
                    for c in range(KD):
                        i = mm(ps[:, :], w[:, c, :], H[:, c, :], start=c == 0, stop=c == KD - 1)
                    i.then_inc(pe.fills(f"m{x}{k}"), 1)
                for k in range(2):
                    pe.e.wait_ge(*pe.taken(f"mu{k}"))
                for m in range(8):
                    if m % 4 == 0:
                        w = weights(pe, 4 + m // 4, "M")
                    pe.e.wait_ge(*pe.emptied(f"md{m}"))
                    ps = bank_of(f"md{m}")
                    for k in range(2):
                        i = mm(ps[:, :], w[:, (2 * m + k) % 8, :], HID[:, k, :], start=k == 0, stop=k == 1)
                    i.then_inc(pe.fills(f"md{m}"), 1)

        def act_M(sc):
            sc.sec = "M"
            with sc.e.Fori(0, NE) as l:
                sc.l = l
                for k in range(2):
                    sc.e.wait_ge(*sc.filled(f"mg{k}"))
                    ps = bank_of(f"mg{k}")
                    act_(TG[:, k, :], ps[:, :], ACT.Tanh, scale=0.5).then_inc(sc.tells("m_tanh"), 1)
            sc.l = 0

        def dve_M(dv):
            dv.sec = "M"
            dv.restart()
            with dv.e.Fori(0, NE) as l:
                dv.l = l
                dv.e.wait_ge(*dv.landed("comb_row"))
                for k in range(2):
                    dv.e.wait_ge(*dv.nth("m_tanh", k + 1))
                    dv.e.wait_ge(*dv.filled(f"mg{k}"))
                    ps = bank_of(f"mg{k}")
                    stt(HID[:, k, :], TG[:, k, :], 1.0, ps[:, :], ALU.add, ALU.mult).then_inc(dv.takes(f"mg{k}"), 1)
                    dv.e.wait_ge(*dv.taken(f"mg{k}"))
                    tt(HID[:, k, :], HID[:, k, :], CB[:, 0, :], ALU.mult).then_inc(dv.tells("m_comb"), 1)
                    dv.e.wait_ge(*dv.nth("m_comb", k + 1))
                    dv.e.wait_ge(*dv.filled(f"mu{k}"))
                    ps = bank_of(f"mu{k}")
                    tt(HID[:, k, :], HID[:, k, :], ps[:, :], ALU.mult).then_inc(dv.takes(f"mu{k}"), 1)
                for m in range(8):
                    dv.e.wait_ge(*dv.filled(f"md{m}"))
                    ps = bank_of(f"md{m}")
                    stt(X[:, m, :], ps[:, :], 0.5, X[:, m, :], ALU.mult, ALU.add).then_inc(dv.takes(f"md{m}"), 1)
                dv.e.wait_ge(*dv.taken("md7"))
            dv.l = 0

        c_ = lambda i, n=1: ch(512 * i, n)
        QL, KL, DAV, RQL, RKL, RV, RG, SCB = c_(0, 4), c_(4, 4), c_(8, 4), c_(12, 2), c_(14, 2), c_(16, 2), c_(18, 2), c_(20, 2)
        RVt = arena[:, 512 * 16:512 * 18].rearrange("p (n w) -> p n w", n=NT)
        BIASB = c_(22, 4)
        SCX = arena[:, 512 * 26:512 * 26 + 1032].rearrange("p (n w) -> p n w", n=2)
        ODA, ORET, OSC = c_(29, 4), c_(33, 2), c_(35, 2)
        PTL = [c_(37, 4), c_(41, 4)]
        SQL = c_(37, 8)
        SE = c_(45, 4)
        TL = c_(49, 6)
        YL = c_(0, 8)
        HL = c_(0, 22)
        GP = arena[:, 512 * 37:512 * 37 + 1032].rearrange("p (n w) -> p n w", n=2)
        dunits = [(h, i) for h in range(DH) for i in range(NT)]
        q2 = lambda name, i=0, n=1: par(p2, A2, name, i, n)

        RELB, ONEH, REPB, RROW = c_(0), c_(1), c_(2), arena[:, 512 * 4:512 * 4 + 4 * 640].rearrange("p (n w) -> p n w", n=4)

        def pe_B(pe):
            pe.sec, pe.l = "B", 0
            for h in range(DH):
                pe.e.wait_ge(*pe.emptied(f"bias{h}"))
                ps = bank_of(f"bias{h}")
                pe.e.wait_ge(*pe.nth("rel_rep", h + 1))
                mm(ps[:, :], REPB[0:32, 0, h * P:(h + 1) * P], ONEH[0:32, 0, :], start=True, stop=True).then_inc(pe.fills(f"bias{h}"), 1)

        def dve_B(dv):
            dv.sec = "B"
            dv.e.wait_ge(ev("rel_in"), 32)
            for h in range(DH):
                ts(REPB[0:32, 0, h * P:(h + 1) * P], cc("ones", slice(0, 32)), RELB[0:32, 0, h:h + 1], None, ALU.mult).then_inc(dv.tells("rel_rep"), 1)
            for h in range(DH):
                V.memset(RROW[:, h, 512:640], NEG).then_inc(dv.tells("bias_pad"), 1)
            for h in range(DH):
                dv.e.wait_ge(*dv.filled(f"bias{h}"))
                ps = bank_of(f"bias{h}")
                V.tensor_copy(RROW[:, h, 0:512], ps[:, :]).then_inc(dv.takes(f"bias{h}"), 1)
            dv.e.wait_ge(*dv.taken(f"bias{DH - 1}"))
            V.memset(small[:, 59:60], 0.0).then_inc(dv.tells("x_ready"), 1)

        def act_B(sc):
            sc.sec = "B"
            e = sc.e
            sc.sec = "M"
            sc.l = NE - 1
            sc.e.wait_ge(*sc.taken("md7"))
            sc.sec, sc.l = "B", 0
            e.dma_start(RELB[0:32, 0, 0:DH], ts_["rel_bias"]).then_inc(ev("rel_in"), 16)
            e.dma_start(ONEH[0:32, 0, :], ts_["onehot"]).then_inc(ev("rel_in"), 16)
            sc.e.wait_ge(*sc.nth("bias_pad", DH))
            for h in range(DH):
                sc.e.wait_ge(*sc.taken(f"bias{h}"))
                e.dma_start(bias_scratch[h].rearrange("(p w) -> p w", w=640), RROW[:, h, :]).then_inc(ev("bias_stored"), 16)
            e.wait_ge(ev("bias_stored"), 16 * DH)
            for h in range(DH):
                skew = bias_scratch[h, 127:127 + P * 639].rearrange("(p w) -> p w", w=639)[:, 0:512]
                e.dma_start(BIASB[:, h, :], skew).then_inc(ev("bias_in"), 16)

        def branch_rhs(b):
            return [[(k, ODA[:, k, :]) for k in range(4)], [(4 + k, ORET[:, k, :]) for k in range(2)],
                    [(6 + k, OSC[:, k, :]) for k in range(2)]][b]

        def pe_L(pe):
            pe.sec = "L"
            e = pe.e
            with e.Fori(0, L2) as l:
                pe.l = l
                slot = iter(range(n_slots["L"]))
                W_ = lambda: weights(pe, next(slot), "L")
                pe.e.wait_ge(*pe.emptied("ssq3"))
                ps = bank_of("ssq3")
                for c in range(KD):
                    pe.e.wait_ge(*pe.nth("Lsq", c + 1))
                    i = mm(ps[:, :], cc("ones"), SQL[:, c, :], start=c == 0, stop=c == KD - 1)
                i.then_inc(pe.fills("ssq3"), 1)
                for x, w_, per in (("dav", 512, 2), ("rv", 256, 4)):
                    for i_ in range(NT):
                        pe.e.wait_ge(*pe.emptied(f"{x}{i_}"))
                    pss = [bank_of(f"{x}{i_}") for i_ in range(NT)]
                    for k in range(KD):
                        if k % per == 0:
                            w = W_().rearrange("p k n -> p (k n)").rearrange("p (k n) -> p k n", k=per)
                        if x == "dav":
                            pe.e.wait_ge(*pe.nth("Lh", k + 1))
                        for i_ in range(NT):
                            i = mm(pss[i_][:, 0:w_], H[:, k, i_ * P:(i_ + 1) * P], w[:, k % per, :], start=k == 0, stop=k == KD - 1)
                            if k == KD - 1:
                                i.then_inc(pe.fills(f"{x}{i_}"), 1)

                def chunk(job):
                    w = W_()
                    pe.e.wait_ge(*pe.emptied(job))
                    ps = bank_of(job)
                    for k in range(KD):
                        i = mm(ps[:, :], w[:, k, :], H[:, k, :], start=k == 0, stop=k == KD - 1)
                    i.then_inc(pe.fills(job), 1)

                for x in ("rq", "rk"):
                    for c in range(2):
                        chunk(f"{x}{c}")
                for h in range(DH):
                    chunk(f"dq{h}")
                    chunk(f"dk{h}")
                for h in range(DH):
                    for j, x in enumerate("qk"):
                        pe.e.wait_ge(*pe.emptied(f"d{x}ss{h}"))
                        ps = bank_of(f"d{x}ss{h}")
                        pe.e.wait_ge(*pe.nth("Lqsq", 2 * h + j + 1))
                        mm(ps[:, :], cc("blk64"), SQL[:, 2 * h + j, :], start=True, stop=True).then_inc(pe.fills(f"d{x}ss{h}"), 1)
                for x, src in (("rq", RQL), ("rk", RKL)):
                    for c in range(2):
                        pe.e.wait_ge(*pe.emptied(f"{x}p{c}"))
                        ps = bank_of(f"{x}p{c}")
                        pe.e.wait_ge(*pe.taken(f"{x}{c}"))
                        mm(ps[:, :], cc("perm64"), src[:, c, :], start=True, stop=True).then_inc(pe.fills(f"{x}p{c}"), 1)
                for x in ("rgt", "scb", "scc", "scx"):
                    for c in range(2):
                        chunk(f"{x}{c}")
                for h in range(RH):
                    hp, c = slice(64 * (h % 2), 64 * (h % 2) + 64), h // 2
                    for j in range(NT):
                        pe.e.wait_ge(*pe.emptied(f"rs{h}_{j}"))
                        ps = bank_of(f"rs{h}_{j}")
                        if h == 0 and j == 0:
                            pe.e.wait_ge(*pe.nth("Lrot", 4))
                        n = T - j * P
                        mm(ps[:, 0:n], RKL[hp, c, j * P:(j + 1) * P], RQL[hp, c, j * P:T], start=True, stop=True).then_inc(pe.fills(f"rs{h}_{j}"), 1)
                    if h % 2:
                        pe.e.wait_ge(*pe.emptied(f"ro{c}"))
                        ps = bank_of(f"ro{c}")
                        for hh in (h - 1, h):
                            for j in range(NT):
                                pe.e.wait_ge(*pe.taken(f"rs{hh}_{j}"))
                                sd = (SE if hh % 2 == 0 else TL)[:, j, 0:T - j * P]
                                i = mm(ps[64 * (hh % 2):64 * (hh % 2) + 64, j * P:T], RVt[:, j, hh * 64:hh * 64 + 64], sd,
                                       start=j == 0, stop=j == NT - 1)
                        i.then_inc(pe.fills(f"ro{c}"), 1)
                for c in range(2):
                    pe.e.wait_ge(*pe.emptied(f"ross{c}"))
                    ps = bank_of(f"ross{c}")
                    pe.e.wait_ge(*pe.nth("Lrsq", c + 1))
                    mm(ps[:, :], cc("blk64"), TL[:, 4 + c, :], start=True, stop=True).then_inc(pe.fills(f"ross{c}"), 1)

                def turn(n):
                    h, i_ = dunits[n]
                    pe.e.wait_ge(*pe.emptied(f"dt{h}_{i_}"))
                    ps = bank_of(f"dt{h}_{i_}")
                    pe.e.wait_ge(*pe.nth("Lprob", n + 1))
                    for j in range(i_ + 1):
                        i = nc.tensor.transpose(ps[:, j * P:(j + 1) * P], SE[:, 2 * (n % 2), j * P:(j + 1) * P], ident)
                    i.then_inc(pe.fills(f"dt{h}_{i_}"), 1)
                    if i_ == NT - 1:
                        pe.e.wait_ge(*pe.emptied(f"do{h}"))
                        ps = bank_of(f"do{h}")
                        pe.e.wait_ge(*pe.taken(f"dt{h}_{i_}"))
                        for j in range(NT):
                            i = mm(ps[:, j * P:T], DAV[:, j, h * P:(h + 1) * P], PTL[h % 2][:, j, j * P:T], start=j == 0, stop=j == NT - 1)
                        i.then_inc(pe.fills(f"do{h}"), 1)

                for n, (h, i_) in enumerate(dunits):
                    for m in range(2):
                        pe.e.wait_ge(*pe.emptied(f"ds{h}_{i_}_{m}"))
                        ps = bank_of(f"ds{h}_{i_}_{m}")
                        if n == 0 and m == 0:
                            pe.e.wait_ge(*pe.nth("Lqkn", 8))
                        hp = slice(64 * m, 64 * m + 64)
                        i = mm(ps[:, 0:(i_ + 1) * P], QL[hp, h, i_ * P:(i_ + 1) * P], KL[hp, h, 0:(i_ + 1) * P], start=True, stop=True)
                        i.then_inc(pe.fills(f"ds{h}_{i_}_{m}"), 1)
                    if n:
                        turn(n - 1)
                turn(len(dunits) - 1)
                for h in range(DH):
                    pe.e.wait_ge(*pe.emptied(f"doss{h}"))
                    ps = bank_of(f"doss{h}")
                    pe.e.wait_ge(*pe.nth("Losq", h + 1))
                    mm(ps[:, :], cc("ones"), TL[:, h, :], start=True, stop=True).then_inc(pe.fills(f"doss{h}"), 1)
                for m in range(8):
                    for b in range(3):
                        chunk(f"gate{b}_{m}")
                    w = W_()
                    for b in range(3):
                        pe.e.wait_ge(*pe.emptied(f"br{b}_{m}"))
                        ps = bank_of(f"br{b}_{m}")
                        if m == 0 and b == 0:
                            pe.e.wait_ge(*pe.nth("Loda", 4))
                        if m == 0 and b == 1:
                            pe.e.wait_ge(*pe.nth("Loret", 2))
                        if m == 0 and b == 2:
                            pe.e.wait_ge(*pe.nth("Losc", 2))
                        rs = branch_rhs(b)
                        for k, r in rs:
                            i = mm(ps[:, :], w[:, k, :], r, start=k == rs[0][0], stop=k == rs[-1][0])
                        i.then_inc(pe.fills(f"br{b}_{m}"), 1)
                for m in range(8):
                    w = W_()
                    pe.e.wait_ge(*pe.emptied(f"wout{m}"))
                    ps = bank_of(f"wout{m}")
                    for k in range(KD):
                        if m == 0:
                            pe.e.wait_ge(*pe.nth("Ly", k + 1))
                        i = mm(ps[:, :], w[:, k, :], YL[:, k, :], start=k == 0, stop=k == KD - 1)
                    i.then_inc(pe.fills(f"wout{m}"), 1)
                pe.e.wait_ge(*pe.emptied("ssq4"))
                ps = bank_of("ssq4")
                for c in range(KD):
                    pe.e.wait_ge(*pe.nth("Lsq", KD + c + 1))
                    i = mm(ps[:, :], cc("ones"), SQL[:, c, :], start=c == 0, stop=c == KD - 1)
                i.then_inc(pe.fills("ssq4"), 1)
                pe.e.wait_ge(*pe.nth("Lh", 2 * KD))
                for k in range(KF):
                    chunk(f"fg{k}")
                    chunk(f"fu{k}")
                w = None
                for m in range(8):
                    pe.e.wait_ge(*pe.emptied(f"fo{m}"))
                    ps = bank_of(f"fo{m}")
                    for k in range(KF):
                        t_ = m * KF + k
                        if t_ % 8 == 0:
                            w = W_()
                        if m == 0:
                            pe.e.wait_ge(*pe.taken(f"fu{k}"))
                        i = mm(ps[:, :], w[:, t_ % 8, :], HL[:, k, :], start=k == 0, stop=k == KF - 1)
                    i.then_inc(pe.fills(f"fo{m}"), 1)

        def act_L(sc):
            sc.sec = "L"
            e = sc.e
            sc.restart()
            with e.Fori(0, L2) as l:
                sc.l = l
                sc.e.wait_ge(*sc.nth("x_ready", 1))
                e.dma_start(p2[:, :], ts_["p2"][bass.ds(l, 1)].rearrange("a p n -> (a p) n")).then_inc(ev("p2_in"), 16)
                for c in range(KD):
                    act_(SQL[:, c, :], X[:, c, :], ACT.Square).then_inc(sc.tells("Lsq"), 1)
                sc.e.wait_ge(*sc.filled("ssq3"))
                ps = bank_of("ssq3")
                act_(TL[:, 0, :], ps[:, :], ACT.Sqrt, EPS, 1.0 / D).then_inc(sc.takes("ssq3"), 1)
                for i_ in range(NT):
                    sc.e.wait_ge(*sc.filled(f"dav{i_}"))
                    ps = bank_of(f"dav{i_}")
                    act_(DAV[:, i_, :], ps[:, :], ACT.Copy).then_inc(sc.takes(f"dav{i_}"), 1)
                for i_ in range(NT):
                    sc.e.wait_ge(*sc.filled(f"rv{i_}"))
                    ps = bank_of(f"rv{i_}")
                    act_(RVt[:, i_, :], ps[:, 0:256], ACT.Copy).then_inc(sc.takes(f"rv{i_}"), 1)
                for h in range(DH):
                    for j, x in enumerate("qk"):
                        sc.e.wait_ge(*sc.taken(f"d{x}{h}"))
                        act_(SQL[:, 2 * h + j, :], (QL if x == "q" else KL)[:, h, :], ACT.Square).then_inc(sc.tells("Lqsq"), 1)
                for h in range(DH):
                    for j, x in enumerate("qk"):
                        sc.e.wait_ge(*sc.filled(f"d{x}ss{h}"))
                        ps = bank_of(f"d{x}ss{h}")
                        act_(SQL[:, 2 * h + j, :], ps[:, :], ACT.Sqrt, EPS, 1.0 / DQ).then_inc(sc.takes(f"d{x}ss{h}"), 1)
                sc.e.wait_ge(*sc.nth("Llam", 1))
                act_(small[:, 24:26], small[:, 22:24], ACT.Exp).then_inc(sc.tells("Llexp"), 1)
                for c in range(2):
                    sc.e.wait_ge(*sc.filled(f"rgt{c}"))
                    ps = bank_of(f"rgt{c}")
                    act_(TL[:, 1 + c, :], ps[:, :], ACT.Tanh, scale=0.5).then_inc(sc.tells("Lrgt"), 1)
                for c in range(2):
                    sc.e.wait_ge(*sc.filled(f"scb{c}"))
                    ps = bank_of(f"scb{c}")
                    act_(SCB[:, c, :], ps[:, :], ACT.Copy).then_inc(sc.takes(f"scb{c}"), 1)
                for c in range(2):
                    sc.e.wait_ge(*sc.filled(f"scc{c}"))
                    ps = bank_of(f"scc{c}")
                    act_(TL[:, 3 + c, :], ps[:, :], ACT.Copy).then_inc(sc.takes(f"scc{c}"), 1)
                for c in range(2):
                    sc.e.wait_ge(*sc.taken(f"ro{c}"))
                    act_(TL[:, 4 + c, :], ORET[:, c, :], ACT.Square).then_inc(sc.tells("Lrsq"), 1)
                for c in range(2):
                    sc.e.wait_ge(*sc.filled(f"ross{c}"))
                    ps = bank_of(f"ross{c}")
                    act_(TL[:, 4 + c, :], ps[:, :], ACT.Sqrt, EPS, 1.0 / 64).then_inc(sc.takes(f"ross{c}"), 1)
                for n, (h, i_) in enumerate(dunits):
                    for m in range(2):
                        sc.e.wait_ge(*sc.nth("Lmax", 2 * n + m + 1))
                        s = SE[:, 2 * (n % 2) + m, 0:(i_ + 1) * P]
                        c0 = 2 * (n % 2) + m
                        act_(s, s, ACT.Exp, bias=small[:, 36 + c0:37 + c0], accum=small[:, 40 + c0:41 + c0]).then_inc(sc.tells("Lexp"), 1)
                    if n:
                        turned_L(sc, n - 1)
                turned_L(sc, len(dunits) - 1)
                for h in range(DH):
                    sc.e.wait_ge(*sc.taken(f"do{h}"))
                    act_(TL[:, h, :], ODA[:, h, :], ACT.Square).then_inc(sc.tells("Losq"), 1)
                for h in range(DH):
                    sc.e.wait_ge(*sc.filled(f"doss{h}"))
                    ps = bank_of(f"doss{h}")
                    act_(TL[:, h, :], ps[:, :], ACT.Sqrt, EPS, 1.0 / DV).then_inc(sc.takes(f"doss{h}"), 1)
                for m in range(8):
                    for b in range(3):
                        sc.e.wait_ge(*sc.filled(f"gate{b}_{m}"))
                        ps = bank_of(f"gate{b}_{m}")
                        if m == 0 and b == 0:
                            sc.e.wait_ge(*sc.nth("Loda", 4))
                            sc.e.wait_ge(*sc.nth("Lbgate", 1))
                        if m >= 2:
                            sc.e.wait_ge(*sc.nth("Ly", m - 1))
                        act_(TL[:, b + 3 * (m % 2), :], ps[:, :], ACT.Tanh, bias=arena_small("bgh", b * 8 + m), scale=0.5).then_inc(sc.takes(f"gate{b}_{m}"), 1)
                for c in range(KD):
                    sc.e.wait_ge(*sc.taken(f"wout{c}"))
                    act_(SQL[:, c, :], X[:, c, :], ACT.Square).then_inc(sc.tells("Lsq"), 1)
                sc.e.wait_ge(*sc.filled("ssq4"))
                ps = bank_of("ssq4")
                act_(TL[:, 0, :], ps[:, :], ACT.Sqrt, EPS, 1.0 / D).then_inc(sc.takes("ssq4"), 1)
                for k in range(KF):
                    sc.e.wait_ge(*sc.filled(f"fg{k}"))
                    ps = bank_of(f"fg{k}")
                    if k == 0:
                        sc.e.wait_ge(*sc.nth("Lh", 2 * KD))
                        sc.e.wait_ge(*sc.nth("Lgpad", 1))
                    if k >= 2:
                        sc.e.wait_ge(*sc.taken(f"fu{k - 2}"))
                    act_(GP[:, k % 2, 2:514], ps[:, :], ACT.Copy).then_inc(sc.takes(f"fg{k}"), 1)
                    sc.e.wait_ge(*sc.taken(f"fg{k}"))
                    act_(TL[:, k % 2, :], GP[:, k % 2, 2:514], ACT.Identity, bias=q2("fcb", k), scale=q2("fcw", 2 * KF + k)).then_inc(sc.tells("Lfc"), 1)
                    sc.e.wait_ge(*sc.nth("Lconv", k + 1))
                    act_(TL[:, 2 + k % 2, :], TL[:, k % 2, :], ACT.Tanh, scale=0.5).then_inc(sc.tells("Lft"), 1)
            sc.l = 0

        def arena_small(name, i, n=1):
            return arena[:, 55 * 512 + i:55 * 512 + i + n]

        def turned_L(sc, n):
            h, i_ = dunits[n]
            sc.e.wait_ge(*sc.filled(f"dt{h}_{i_}"))
            ps = bank_of(f"dt{h}_{i_}")
            if i_ == 0 and h >= 2:
                sc.e.wait_ge(*sc.filled(f"do{h - 2}"))
            act_(PTL[h % 2][:, 0:i_ + 1, i_ * P:(i_ + 1) * P],
                         ps[:, 0:(i_ + 1) * P].rearrange("p (n w) -> p n w", n=i_ + 1), ACT.Copy).then_inc(sc.takes(f"dt{h}_{i_}"), 1)

        def dve_L(dv):
            dv.sec = "L"
            e = dv.e
            dv.restart()
            e.wait_ge(ev("bias_in"), 16 * DH)
            with e.Fori(0, L2) as l:
                dv.l = l
                dv.e.wait_ge(*dv.landed("p2_in"))
                norm(dv, "ssq3", X, H, lambda c: q2("g_mix", c), TL[:, 0, :], "Lh")
                st = lambda ins: (ins.then_inc(dv.chained(), 1), dv.e.wait_ge(dv.chain, dv.n))
                lm = q2("lam", 0, 256).rearrange("p (a b d) -> p a b d", a=2, b=2)
                dv.e.wait_ge(*dv.nth("Lh", KD))
                st(tt(TL[:, 5, 0:128].rearrange("p (a d) -> p a d", a=2), lm[:, :, 0, :], lm[:, :, 1, :], ALU.mult))
                V.tensor_reduce(small[:, 22:24], TL[:, 5, 0:128].rearrange("p (a d) -> p a d", a=2), AX.X, ALU.add).then_inc(dv.tells("Llam"), 1)
                ts(small[:, 26:27], q2("gq"), DQ ** -0.5, None, ALU.mult).then_inc(dv.chained(), 1)
                ts(small[:, 27:28], q2("retg"), 0.5, None, ALU.mult).then_inc(dv.chained(), 1)
                tt(small[:, 28:29], q2("subln"), q2("one_minus"), ALU.mult).then_inc(dv.chained(), 1)
                ts(arena_small("bgh", 0, 24), q2("b_gate", 0, 24), 0.5, None, ALU.mult).then_inc(dv.tells("Lbgate"), 1)
                V.memset(SCX[:, :, 0:2], 0.0).then_inc(dv.chained(), 1)
                for x, o in (("rq", RQL), ("rk", RKL)):
                    for c in range(2):
                        dv.e.wait_ge(*dv.filled(f"{x}{c}"))
                        ps = bank_of(f"{x}{c}")
                        V.tensor_copy(o[:, c, :], ps[:, :]).then_inc(dv.takes(f"{x}{c}"), 1)
                for h in range(DH):
                    for x, o in (("q", QL), ("k", KL)):
                        dv.e.wait_ge(*dv.filled(f"d{x}{h}"))
                        ps = bank_of(f"d{x}{h}")
                        V.tensor_copy(o[:, h, :], ps[:, :]).then_inc(dv.takes(f"d{x}{h}"), 1)
                for h in range(DH):
                    for j, (x, o, g) in enumerate((("q", QL, small[:, 26:27]), ("k", KL, q2("gk")))):
                        dv.e.wait_ge(*dv.taken(f"d{x}ss{h}"))
                        r = SQL[:, 2 * h + j, :]
                        st(V.reciprocal(r, r))
                        stt(o[:, h, :], o[:, h, :], g, r, ALU.mult, ALU.mult).then_inc(dv.tells("Lqkn"), 1)
                for x, o in (("rq", RQL), ("rk", RKL)):
                    for c in range(2):
                        t = TL[:, 5, :]
                        dv.e.wait_ge(*dv.filled(f"{x}p{c}"))
                        ps = bank_of(f"{x}p{c}")
                        dv.e.wait_ge(dv.chain, dv.n)
                        tt(t, ps[:, :], cc("ret_sin"), ALU.mult).then_inc(dv.takes(f"{x}p{c}"), 1)
                        st(tt(o[:, c, :], o[:, c, :], cc("ret_cos"), ALU.mult))
                        dv.e.wait_ge(*dv.taken(f"{x}p{c}"))
                        tt(o[:, c, :], o[:, c, :], t, ALU.add).then_inc(dv.tells("Lrot"), 1)
                        dv.e.wait_ge(*dv.nth("Lrot", 2 * (x == "rk") + c + 1))
                dv.e.wait_ge(*dv.nth("Llexp", 1))
                st(tt(small[:, 29:30], small[:, 25:26], small[:, 24:25], ALU.subtract))
                st(tt(small[:, 29:30], small[:, 29:30], q2("lam_init"), ALU.subtract))
                for c in range(2):
                    dv.e.wait_ge(*dv.nth("Lrgt", c + 1))
                    dv.e.wait_ge(*dv.filled(f"rgt{c}"))
                    ps = bank_of(f"rgt{c}")
                    stt(RG[:, c, :], TL[:, 1 + c, :], 1.0, ps[:, :], ALU.add, ALU.mult).then_inc(dv.takes(f"rgt{c}"), 1)
                for c in range(2):
                    dv.e.wait_ge(*dv.taken(f"scc{c}"))
                    dv.e.wait_ge(*dv.filled(f"scx{c}"))
                    ps = bank_of(f"scx{c}")
                    tt(SCX[:, c, 2:514], TL[:, 3 + c, :], ps[:, :], ALU.mult).then_inc(dv.takes(f"scx{c}"), 1)
                for c in range(2):
                    o = OSC[:, c, :]
                    dv.e.wait_ge(*dv.taken(f"scx{c}"))
                    st(ts(o, SCX[:, c, 2:514], q2("scw", 4 + c), q2("scb", c), ALU.mult, ALU.add))
                    st(stt(o, SCX[:, c, 1:513], q2("scw", 2 + c), o, ALU.mult, ALU.add))
                    st(stt(o, SCX[:, c, 0:512], q2("scw", c), o, ALU.mult, ALU.add))
                    dv.e.wait_ge(*dv.taken(f"scb{c}"))
                    tt(o, o, SCB[:, c, :], ALU.mult).then_inc(dv.tells("Losc"), 1)
                for h in range(RH):
                    for j in range(NT):
                        dv.e.wait_ge(*dv.filled(f"rs{h}_{j}"))
                        ps = bank_of(f"rs{h}_{j}")
                        if h >= 2 and j == 0:
                            dv.e.wait_ge(*dv.filled("ro0"))
                        n = T - j * P
                        dec = cc("ret_decay")[:, h * 512:h * 512 + n]
                        stt((SE if h % 2 == 0 else TL)[:, j, 0:n], ps[:, 0:n], RQ ** -0.5, dec, ALU.mult, ALU.mult).then_inc(dv.takes(f"rs{h}_{j}"), 1)
                    if h % 2:
                        dv.e.wait_ge(*dv.filled(f"ro{h // 2}"))
                        ps = bank_of(f"ro{h // 2}")
                        V.tensor_copy(ORET[:, h // 2, :], ps[:, :]).then_inc(dv.takes(f"ro{h // 2}"), 1)
                for c in range(2):
                    dv.e.wait_ge(*dv.taken(f"ross{c}"))
                    r = TL[:, 4 + c, :]
                    st(V.reciprocal(r, r))
                    st(stt(ORET[:, c, :], ORET[:, c, :], small[:, 27:28], r, ALU.mult, ALU.mult))
                    dv.e.wait_ge(*dv.taken(f"rgt{c}"))
                    tt(ORET[:, c, :], ORET[:, c, :], RG[:, c, :], ALU.mult).then_inc(dv.tells("Loret"), 1)

                def prob(n):
                    h, i_ = dunits[n]
                    w = (i_ + 1) * P
                    b0 = 2 * (n % 2)
                    dv.e.wait_ge(*dv.nth("Lexp", 2 * n + 2))
                    r = small[:, 44 + b0:46 + b0]
                    st(V.reciprocal(r, small[:, 40 + b0:42 + b0]))
                    tt(r[:, 1:2], r[:, 1:2], small[:, 29:30], ALU.mult).then_inc(dv.chained(), 1)
                    st(ts(SE[:, b0, 0:w], SE[:, b0, 0:w], r[:, 0:1], None, ALU.mult))
                    stt(SE[:, b0, 0:w], SE[:, b0 + 1, 0:w], r[:, 1:2], SE[:, b0, 0:w], ALU.mult, ALU.add).then_inc(dv.tells("Lprob"), 1)
                    if i_ == 1 and h:
                        dv.e.wait_ge(*dv.filled(f"do{h - 1}"))
                        ps = bank_of(f"do{h - 1}")
                        V.tensor_copy(ODA[:, h - 1, :], ps[:, :]).then_inc(dv.takes(f"do{h - 1}"), 1)

                for n, (h, i_) in enumerate(dunits):
                    w = (i_ + 1) * P
                    for m in range(2):
                        b0 = 2 * (n % 2) + m
                        dv.e.wait_ge(*dv.filled(f"ds{h}_{i_}_{m}"))
                        ps = bank_of(f"ds{h}_{i_}_{m}")
                        if n >= 2 and m == 0:
                            dv.e.wait_ge(*dv.filled("dt%d_%d" % dunits[n - 2]))
                            dv.e.wait_ge(*dv.nth("Lprob", n - 1))
                        if n == 0:
                            dv.e.wait_ge(*dv.filled("ro1"))
                        mx = small[:, 32 + b0:33 + b0]
                        V.memset(small[0:1, 58:59], 0.0)
                        V.tensor_tensor_reduce(SE[:, b0, 0:w], ps[:, 0:w], BIASB[:, h, 512 - w:512], 1.0, 3 * NEG,
                                                       ALU.add, ALU.max, mx).then_inc(dv.takes(f"ds{h}_{i_}_{m}"), 1)
                        dv.e.wait_ge(*dv.taken(f"ds{h}_{i_}_{m}"))
                        ts(small[:, 36 + b0:37 + b0], mx, -1.0, None, ALU.mult).then_inc(dv.tells("Lmax"), 1)
                    if n:
                        prob(n - 1)
                prob(len(dunits) - 1)
                dv.e.wait_ge(*dv.filled(f"do{DH - 1}"))
                ps = bank_of(f"do{DH - 1}")
                V.tensor_copy(ODA[:, DH - 1, :], ps[:, :]).then_inc(dv.takes(f"do{DH - 1}"), 1)
                for h in range(DH):
                    dv.e.wait_ge(*dv.taken(f"doss{h}"))
                    r = TL[:, h, :]
                    st(V.reciprocal(r, r))
                    stt(ODA[:, h, :], ODA[:, h, :], small[:, 28:29], r, ALU.mult, ALU.mult).then_inc(dv.tells("Loda"), 1)
                for m in range(8):
                    t = [TL[:, b + 3 * (m % 2), :] for b in range(3)]
                    for b in range(3):
                        dv.e.wait_ge(*dv.taken(f"gate{b}_{m}"))
                        dv.e.wait_ge(*dv.filled(f"br{b}_{m}"))
                        ps = bank_of(f"br{b}_{m}")
                        stt(t[b], t[b], 1.0, ps[:, :], ALU.add, ALU.mult).then_inc(dv.takes(f"br{b}_{m}"), 1)
                    dv.e.wait_ge(*dv.taken(f"br1_{m}"))
                    st(tt(t[0], t[0], t[1], ALU.add))
                    dv.e.wait_ge(*dv.taken(f"br2_{m}"))
                    tt(YL[:, m, :], t[0], t[2], ALU.add).then_inc(dv.tells("Ly"), 1)
                for m in range(8):
                    dv.e.wait_ge(*dv.filled(f"wout{m}"))
                    ps = bank_of(f"wout{m}")
                    stt(X[:, m, :], ps[:, :], 0.5, X[:, m, :], ALU.mult, ALU.add).then_inc(dv.takes(f"wout{m}"), 1)
                dv.e.wait_ge(*dv.taken("wout7"))
                norm(dv, "ssq4", X, H, lambda c: q2("g_ffn", c), TL[:, 0, :], "Lh")
                V.memset(GP[:, :, 0:2], 0.0).then_inc(dv.tells("Lgpad"), 1)
                for k in range(KF):
                    c = TL[:, k % 2, :]
                    g = GP[:, k % 2, :]
                    dv.e.wait_ge(*dv.nth("Lfc", k + 1))
                    st(stt(c, g[:, 1:513], q2("fcw", KF + k), c, ALU.mult, ALU.add))
                    stt(c, g[:, 0:512], q2("fcw", k), c, ALU.mult, ALU.add).then_inc(dv.tells("Lconv"), 1)
                    dv.e.wait_ge(*dv.nth("Lft", k + 1))
                    dv.e.wait_ge(*dv.nth("Lconv", k + 1))
                    st(stt(HL[:, k, :], TL[:, 2 + k % 2, :], 1.0, c, ALU.add, ALU.mult))
                    dv.e.wait_ge(*dv.filled(f"fu{k}"))
                    ps = bank_of(f"fu{k}")
                    tt(HL[:, k, :], HL[:, k, :], ps[:, :], ALU.mult).then_inc(dv.takes(f"fu{k}"), 1)
                for m in range(8):
                    dv.e.wait_ge(*dv.filled(f"fo{m}"))
                    ps = bank_of(f"fo{m}")
                    stt(X[:, m, :], ps[:, :], 0.5, X[:, m, :], ALU.mult, ALU.add).then_inc(dv.takes(f"fo{m}"), 1)
                dv.e.wait_ge(*dv.taken("fo7"))
                V.memset(small[:, 59:60], 0.0).then_inc(dv.tells("x_ready"), 1)
                dv.restart()
            dv.l = 0

        stream = ts_["stream"]

        def load(sp, g, wait=None):
            pass

        def sp_all(sp):
            e = sp.e
            e.dma_start(X[:, :, :], ts_["x"]).then_inc(ev("x_in"), 16)
            e.dma_start(cst[:, :], ts_["consts"]).then_inc(ev("consts_in"), 16)
            e.dma_start(p1[:, :], ts_["p1"]).then_inc(ev("p1_in"), 16)

            def fill(s, sec, at_=None):
                r = (slot0[sec] + s) % R
                src = stream[slot0[sec] + s] if at_ is None else \
                    stream[bass.ds(at_ + (slot0[sec] + s), 1)].rearrange("a p n -> (a p) n")
                e.dma_start(ring[:, r, :], src).then_inc(slot_full[r], 16)

            for s in range(n_slots["A"]):
                if s >= R:
                    sp.e.wait_ge(*sp.filled(last_user["A"][s - R]))
                fill(s, "A")
                if s == 0:
                    e.dma_start(w1[:, :], ts_["w1"]).then_inc(ev("w1_in"), 16)
            for s in range(R):
                sp.e.wait_ge(*sp.filled(last_user["A"][n_slots["A"] - R + s]))
                fill(s, "M")
            e.wait_ge(ev("comb_stored"), 16)
            sp.sec = "M"
            sp.l = 0

            def comb_row(l, static):
                src = scratch[0:1, :] if static else scratch[bass.ds(l, 1), :]
                e.dma_start(CB[:, 0, :], src.to_broadcast([P, T])).then_inc(ev("comb_row"), 16)

            e.dma_start(CB[:, 0, :], scratch[0:1, :].to_broadcast([P, T])).then_inc(ev("comb_row"), 16)
            with e.Fori(0, NE - 1) as l:
                sp.l = l
                for s in range(n_slots["M"]):
                    sp.e.wait_ge(*sp.filled(last_user["M"][s]))
                    fill(s, "M", (l + 1) * n_slots["M"])
                    if s == 3:
                        sp.e.wait_ge(*sp.taken("mu1"))
                        e.dma_start(CB[:, 0, :], scratch[bass.ds(l + 1, 1), :].to_broadcast([P, T])).then_inc(ev("comb_row"), 16)
            sp.l = NE - 1
            for s in range(R):
                sp.e.wait_ge(*sp.filled(last_user["M"][n_slots["M"] - R + s]))
                fill(s, "L")
            sp.sec = "L"
            nl = n_slots["L"]
            with e.Fori(0, L2 - 1) as l:
                sp.l = l
                for s in range(R, nl):
                    sp.e.wait_ge(*sp.filled(last_user["L"][s - R]))
                    fill(s, "L", l * nl)
                for s in range(R):
                    sp.e.wait_ge(*sp.filled(last_user["L"][nl - R + s]))
                    fill(s, "L", (l + 1) * nl)
            sp.l = L2 - 1
            for s in range(R, nl):
                sp.e.wait_ge(*sp.filled(last_user["L"][s - R]))
                fill(s, "L", (L2 - 1) * nl)

        block = ctx.enter_context(nc.Block())

        @block.sync
        def _(eng):
            sp = Engine(eng, "sp")
            sp_all(sp)

        @block.tensor
        def _(eng):
            pe = Engine(eng, "pe")
            pe_A(pe)
            pe_M(pe)
            pe_B(pe)
            pe_L(pe)

        @block.scalar
        def _(eng):
            sc = Engine(eng, "act")
            eng.dma_start(arena[0:QK, o_ + 2048:o_ + 2048 + 512].bitcast(I32), ts_["positions"].to_broadcast([QK, T])).then_inc(ev("pos_in"), 16)
            act_A(sc)
            act_M(sc)
            act_B(sc)
            act_L(sc)
            sc.e.wait_ge(*sc.nth("x_ready", 1 + L2))
            for c in range(KD):
                eng.dma_start(out[c], X[:, c, :]).then_inc(ev("out_stored"), 16)
            eng.wait_ge(ev("out_stored"), 16 * KD)

        @block.vector
        def _(eng):
            dv = Engine(eng, "dve")
            dve_A(dv)
            dve_M(dv)
            dve_B(dv)
            dve_L(dv)
        assert sorted(ended) == sorted((j, x) for j in JOB for x in ("free", "full")), \
            (set((j, x) for j in JOB for x in ("free", "full")) ^ set(ended), len(ended))
        for n, per in PER.items():
            assert posts.get(n, 0) == per or n in ("x_ready",), (n, posts.get(n), per)


PER = {"m_tanh": 2, "m_comb": 2, "x_ready": 1, "Lsq": 16, "Lh": 16, "Lqsq": 8, "Lqkn": 8, "Lrot": 4, "Lrgt": 2, "Llam": 1,
       "Llexp": 1, "Lrsq": 2, "Lmax": 32, "Lexp": 32, "Lprob": 16, "Losq": 4, "Loda": 4, "Loret": 2, "Losc": 2, "Ly": 8,
       "Lfc": 22, "Lconv": 22, "Lft": 22, "Lgpad": 1, "Lbgate": 1}


def shape_constants():
    f = np.float32
    i = np.arange(P)
    a, b = i[:, None], i[None, :]
    same64 = (a // 64) == (b // 64)
    c = {"ident": a == b, "ones": np.ones((P, P)), "blk64": same64,
         "upper": same64 & (a < b), "upper_eq": same64 & (a <= b), "lower": same64 & (b < a)}
    for lev in (1, 2, 4, 8, 16, 32):
        m = ((a // (2 * lev)) == (b // (2 * lev))) & (a % (2 * lev) < lev) & (b % (2 * lev) >= lev)
        c[f"lev{lev}"] = m
    c["lev1T"] = c["lev1"].T
    p = np.zeros((P, P))
    for m in range(P):
        if m % 64 < 32:
            p[m + 32, m] = -1
        else:
            p[m - 32, m] = 1
    c["perm64"] = p
    p = np.zeros((P, P))
    for m in range(64, 80):
        p[m + 16, m] = -1
        p[m, m + 16] = 1
    c["perm96"] = p
    u = np.arange(512)
    c["causal"] = np.where(u[None, :] - 384 > a, NEG, 0.0)
    lg = np.log(1.0 - 2.0 ** (-5.0 - np.arange(4, dtype=f)))
    d = u[None, :] - a
    c["ret_decay"] = np.concatenate([np.where(d >= 0, np.exp(lg[h] * np.maximum(d, 0)), 0.0) for h in range(4)], 1)
    inv = (10000.0 ** (-np.arange(32, dtype=f) / f(32))).astype(f)
    ang = (u.astype(f)[None, :] * inv[i % 32][:, None]).astype(f)
    c["ret_cos"], c["ret_sin"] = np.cos(ang.astype(np.float64)), np.sin(ang.astype(np.float64))
    c["scan_keep"] = np.broadcast_to(u % CH != 0, (P, 512))
    inv1 = (f(1.0) / (f(10000.0) ** (np.arange(16, dtype=f) / f(16)))).astype(f)
    q = np.zeros((P, 1), f)
    q[64:96, 0] = inv1[np.arange(32) % 16]
    c["inv_freq"] = q
    c["iota32"] = np.broadcast_to(np.arange(32), (P, 32))
    c["iota4"] = np.broadcast_to(np.arange(4), (P, 4))
    return np.ascontiguousarray(np.concatenate([np.broadcast_to(c[n], (P, w)).astype(f) for n, w in CONST_COLS], 1))


def bucket_onehot():
    f = np.float32
    n = 511 - np.arange(512)
    large = 16 + (np.log(np.maximum(n, 1).astype(f) / f(16)) / f(np.log(8.0)) * f(16)).astype(np.int32)
    b = np.where(n < 16, n, np.minimum(large, 31))
    return np.ascontiguousarray((b[None, :] == np.arange(32)[:, None]).astype(f))


def kernel(**a):
    import concourse.bacc as _bacc
    from concourse.bass_utils import run_bass_kernel_spmd as _run

    a = {k: np.asarray(v) for k, v in a.items()}

    def cols(v):
        return v.reshape(-1, P).T

    def tiled(w):
        k, n = w.shape
        return w.reshape(k // P, P, n // P, P).transpose(2, 1, 0, 3).reshape(n // P, P, k)

    def by_tile(w):
        k, n = w.shape
        return w.reshape(k // P, P, n // P, P).transpose(2, 0, 1, 3).reshape(-1, P, P)

    def slots(t):
        return t.reshape(-1, TPS, P, P).transpose(0, 2, 1, 3).reshape(-1, P, TPS * P)

    def moving(w, per):
        k, n = w.shape
        return w.reshape(k // P // per, per, P, n).transpose(0, 2, 1, 3).reshape(-1, P, per * n)

    w = a["w_in"][0]
    n1 = QR + KVR + ROPE
    kr = np.zeros((D, P), np.float32)
    kr[:, 0:ROPE] = w[:, QR + KVR:n1]
    feat = w[:, n1:]
    win = np.concatenate([w[:, 0:QR + KVR], kr, feat[:, 3 * RW:3 * RW + P], feat[:, 3 * RW + P:], feat[:, 0:3 * RW]], 1)
    stream = [tiled(win), tiled(a["w_o"][0])]
    for e in range(NE):
        g, u = tiled(a["w_gate"][0, e]), tiled(a["w_up"][0, e])
        stream += [g[0:1], u[0:1], g[1:2], u[1:2], slots(by_tile(a["w_down"][0, e]))]
    for l in range(L2):
        w = a["w_in_2"][l]
        o = np.cumsum([0, 512, 512, 512, 256, 256, 256, 256, 256, 256, 256, 3072])
        dq, dk, dv, rq, rk, rv, rg, sb_, sc_, sx, gt = (w[:, o[i]:o[i + 1]] for i in range(11))
        stream += [moving(dv, 2), moving(rv, 4), tiled(rq), tiled(rk)]
        tq, tk = tiled(dq), tiled(dk)
        for h in range(DH):
            stream += [tq[h:h + 1], tk[h:h + 1]]
        stream += [tiled(rg), tiled(sb_), tiled(sc_), tiled(sx)]
        gt = tiled(gt)
        br = [by_tile(a[n][l]).reshape(8, -1, P, P) for n in ("w_branch_da_2", "w_branch_ret_2", "w_branch_sc_2")]
        br = slots(np.concatenate(br, 1).reshape(-1, P, P))
        for m in range(8):
            stream += [gt[m:m + 1], gt[8 + m:9 + m], gt[16 + m:17 + m], br[m:m + 1]]
        stream += [tiled(a["w_out_2"][l])]
        f = tiled(a["w_ffn_in_2"][l])
        for k in range(KF):
            stream += [f[k:k + 1], f[KF + k:KF + k + 1]]
        stream += [slots(by_tile(a["w_ffn_out_2"][l]))]
    stream = np.ascontiguousarray(np.concatenate(stream, 0))

    rep = lambda v: np.broadcast_to(v.reshape(1, -1), (P, v.size))

    def pad(v):
        out = np.zeros((P, 1), np.float32)
        out[0:v.size, 0] = v
        return out

    p1 = {"g_mix": cols(a["g_mix"][0]), "g_cq": cols(a["g_cq"][0]), "g_ckv": cols(a["g_ckv"][0]),
          "g_qn": pad(a["g_qn"][0]), "g_kn": pad(a["g_kn"][0]), "g_mla_out": cols(a["g_mla_out"][0]),
          "mu": cols(a["rw_mu"][0]), "w0": cols(a["rw_w0"][0]), "a0": cols(a["rw_a0"][0]),
          "k_k": cols(a["rw_k_k"][0]), "k_a": cols(a["rw_k_a"][0]), "r_k": cols(a["rw_r_k"][0].reshape(-1)),
          "lnx_g": cols(a["rw_lnx_g"][0]), "lnx_b": cols(a["rw_lnx_b"][0]), "g_ffn": cols(a["g_ffn"][0]),
          "b_route": rep(np.concatenate([a["b_group"][0], a["b_expert"][0]])),
          "w_route": np.concatenate([a["w_group"][0], a["w_expert"][0]], 1).reshape(KD, P, 36).transpose(1, 0, 2).reshape(P, -1)}
    w1 = {"uq": a["w_uq"][0].reshape(2, P, 768).transpose(1, 0, 2).reshape(P, -1), "uk": a["w_uk"][0].reshape(P, -1),
          "uv": a["w_uv"][0].reshape(P, -1), "w2a2": np.concatenate([a["rw_w2"][0], a["rw_a2"][0]], 0), "g2": a["rw_g2"][0]}
    p2 = []
    for l in range(L2):
        li = 0.8 - 0.6 * np.exp(-0.3 * l)
        twice = lambda v: np.concatenate([v, v]).reshape(P, 1)
        d = {"g_mix": cols(a["norm_mix_g_2"][l]), "b_gate": cols(a["b_gate_2"][l]), "gq": twice(a["da_q_norm_g_2"][l]),
             "gk": twice(a["da_k_norm_g_2"][l]), "subln": a["da_subln_g_2"][l].reshape(P, 1), "retg": twice(a["ret_norm_g_2"][l]),
             "scw": cols(a["sc_conv_w_2"][l].reshape(-1)), "scb": cols(a["sc_conv_b_2"][l]), "g_ffn": cols(a["norm_ffn_g_2"][l]),
             "fcw": cols(a["ffn_conv_w_2"][l].reshape(-1)), "fcb": cols(a["ffn_conv_b_2"][l]),
             "lam_init": np.full((P, 1), li, np.float32), "one_minus": np.full((P, 1), 1.0 - li, np.float32),
             "lam": rep(a["da_lambda_2"][l])}
        p2.append(np.concatenate([d[n] for n, _ in P2_COLS], 1))
    arrays = {"x": np.ascontiguousarray(a["x"][0].T.reshape(KD, P, T).transpose(1, 0, 2)),
              "positions": np.ascontiguousarray(a["positions"]),
              "consts": shape_constants(),
              "p1": np.ascontiguousarray(np.concatenate([p1[n] for n, _ in P1_COLS], 1)),
              "w1": np.ascontiguousarray(np.concatenate([w1[n] for n, _ in W1_COLS], 1)),
              "p2": np.ascontiguousarray(np.stack(p2)),
              "rel_bias": np.ascontiguousarray(a["rel_bias_2"]), "onehot": bucket_onehot(), "stream": stream}
    nc = _bacc.Bacc("TRN2", target_bir_lowering=False, num_devices=1)
    aps = {n: nc.dram_tensor(f"in_{n}", v.shape, mybir.dt.from_np(v.dtype), kind="ExternalInput").ap() for n, v in arrays.items()}
    out = nc.dram_tensor("out", (KD, P, T), F32, kind="ExternalOutput").ap()
    build(nc, aps, out)
    r = _run(nc, [{f"in_{n}": v for n, v in arrays.items()}], core_ids=[0])
    y = r.results[0]["out"]
    return np.ascontiguousarray(y.reshape(D, T).T).reshape(1, T, D)
```

```python
from contextlib import ExitStack

import numpy as np
import concourse.bass as bass
from concourse import mybir

F32 = mybir.dt.float32
F32R = mybir.dt.float32r
I32 = mybir.dt.int32
ALU = mybir.AluOpType
ACT = mybir.ActivationFunctionType
AX = mybir.AxisListType

P = 128
T = 512
NT = T // P
D = 1024
KD = D // P
EPS = 1e-6
NEG = -1.0e30

HM, NOPE, ROPE = 8, 64, 32
QK = NOPE + ROPE
QR, KVR = 256, 128
HR, RN = 8, 64
RW = HR * RN
LNX_EPS = 64e-5
CH = 64
NCH = T // CH
EXP_NEG_HALF = 0.6065306597126334
NG, EG, NE, DE = 4, 8, 32, 256
CAP = 64
NPAIR = NE // 2
ROWS = NE * CAP
RM = 12
RF = 6

L2 = 2
DH, DQ, DV = 4, 64, 128
RH, RQ = 4, 64
SCW = 256
DFF = 2816
KF = DFF // P
R = 6
ARENA = 55 * 512 + 40
TPS = 8

CONST_COLS = [("ident", 128), ("ones", 128), ("blk64", 128), ("perm64", 128),
              ("ret_decay", 4 * 512), ("ret_cos", 512), ("ret_sin", 512)]
EARLY_COLS = [("perm96", 128), ("upper", 128), ("upper_eq", 128), ("lower", 128), ("lev1", 128), ("lev1T", 128),
              ("lev2", 128), ("lev4", 128), ("lev8", 128), ("lev16", 128), ("lev32", 128),
              ("causal", 512), ("scan_keep", 512), ("inv_freq", 1), ("iota32", 32), ("iota4", 4), ("spare_row", 8)]
P1_COLS = [("g_mix", 8), ("g_cq", 2), ("g_ckv", 1), ("g_qn", 1), ("g_kn", 1), ("g_mla_out", 4),
           ("mu", 14), ("w0", 4), ("a0", 4), ("k_k", 4), ("k_a", 4), ("r_k", 4), ("lnx_g", 4),
           ("lnx_b", 4), ("g_ffn", 8), ("b_route", 36), ("w_route", 8 * 36)]
W1_COLS = [("uq", 2 * 768), ("uk", 512), ("uv", 512), ("w2a2", 512), ("g2", 512)]
P2_COLS = [("g_mix", 8), ("b_gate", 24), ("gq", 1), ("gk", 1), ("subln", 1), ("retg", 1), ("scw", 6),
           ("scb", 2), ("g_ffn", 8), ("fcw", 66), ("fcb", 22), ("lam_init", 1), ("one_minus", 1),
           ("lam", 256)]


def offsets(cols):
    at, out = 0, {}
    for name, n in cols:
        out[name] = (at, n)
        at += n
    return out, at


AMID = {12: ["rqp0", "rqp1"], 14: ["rkp0", "rkp1"]}
HALVES = [f"{x}{c}" for x in ("rgt", "scb", "scc", "scx") for c in range(2)]


def between(h, x):
    return [f"win{6 + 2 * h + x}"] if 6 + 2 * h + x < 18 else []


def job_names():
    a = ["ssq1"]
    a += [f"win{m}" for m in range(4)]
    a += ["cqss", "ckvss", "win4", "win5"]
    a += [f"vm{i}" for i in range(NT)]
    for h in range(HM):
        a += [f"q{h}", f"k{h}"] + between(h, 0) + [f"qss{h}", f"kss{h}"] + between(h, 1) + [f"qp{h}", f"kp{h}"]
    units = [(h, i) for h in range(HM) for i in range(NT)]
    for n, (h, i) in enumerate(units):
        a.append(f"ms{h}_{i}")
        if n:
            ph, pi = units[n - 1]
            a.append(f"mt{ph}_{pi}")
            if pi == NT - 1 and ph % 2 == 1:
                a.append(f"mo{ph // 2}")
    a += [f"mt{HM - 1}_{NT - 1}", f"mo{HM // 2 - 1}", "moss"]
    for c in range(4):
        a += [f"ru{c}", f"ra{c}", f"rg{c}", f"rkk{c}", f"rb{c}"]
        a += [f"rt{c}_{x}" for x in "vbka"]
        for hh in range(2):
            a += [f"m{x}{c}_{hh}" for x in ("abT", "ab", "ak", "br", "kr")]
        a.append(f"rwk{c}")
        for lev in (2, 4, 8, 16, 32):
            for hh in range(2):
                a.append(f"ix{c}_{lev}_{hh}")
            for hh in range(2):
                a.append(f"iy{c}_{lev}_{hh}")
                if lev != 32:
                    a.append(f"iz{c}_{lev}_{hh}")
        a.append(f"rta{c}")
        for n in range(NCH):
            a += [f"cu{c}_{n}", f"cy{c}_{n}"]
            if n < NCH - 1:
                a.append(f"cs{c}_{n}")
        a += [f"gm{c}", f"gv{c}"]
    a += [f"wo{m}" for m in range(8)]
    a += ["ssq2", "route"] + [f"ht{i}_{x}" for i in range(NT) for x in range(2)]
    a += ["pos", "combT", "pxt0", "pxt1"]
    m = ["mg0", "mg1", "xt0", "xt1", "md0", "md1"]
    f = ["fg0", "fu0", "fg1", "fu1"] + [f"fd{m_}" for m_ in range(8)]
    l = ["ssq3"] + [f"dav{i}" for i in range(NT)] + [f"rv{i}" for i in range(NT)]
    for h in range(DH):
        l += [f"dq{h}", f"dk{h}"]
    for h in range(DH):
        l += [f"dqss{h}", f"dkss{h}"]
    l += [f"{x}{c}" for x in ("rq", "rk") for c in range(2)]
    dunits = [(h, i) for h in range(DH) for i in range(NT)]
    for n, (h, i) in enumerate(dunits):
        l += [f"ds{h}_{i}_0", f"ds{h}_{i}_1"] + ([HALVES[n // 2]] if n % 2 == 0 else [])
        if n:
            ph, pi = dunits[n - 1]
            l.append(f"dt{ph}_{pi}")
            if pi == NT - 1:
                l += [f"do{ph}"]
        l += AMID.get(n, [])
    l += [f"dt{DH - 1}_{NT - 1}", f"do{DH - 1}"]
    for h in range(RH):
        l += [f"rs{h}_{j}" for j in range(NT)]
        l += [f"ro{h // 2}"] if h % 2 else []
    l += ["ross0", "ross1"] + [f"doss{h}" for h in range(DH)]
    l += [f"gate{b_}_0" for b_ in range(3)]
    for m_ in range(8):
        l += [f"gate{b_}_{m_ + 1}" for b_ in range(3) if m_ < 7] + [f"br{b_}_{m_}" for b_ in range(3)]
    l += [f"wout{m_}" for m_ in range(8)] + ["ssq4"]
    for k in range(KF):
        l += [f"ffg{k}", f"ffu{k}"]
    l += [f"fo{m_}" for m_ in range(8)]
    return {"A": a, "M": m, "B": [f"bias{h}" for h in range(DH)] + [f"gt{m_}" for m_ in range(8)], "L": l, "F": f}


def build(nc, ts_, out):
    jobs = job_names()
    JOB = {name: (sec, n) for sec, names in jobs.items() for n, name in enumerate(names)}
    assert len(JOB) == sum(map(len, jobs.values()))
    uses = {s: [len(range(b, len(jobs[s]), 8)) for b in range(8)] for s in jobs}
    base, at = {}, [0] * 8
    TIMES = {"A": 1, "M": NPAIR, "B": 1, "L": L2}
    for s, times in TIMES.items():
        base[s] = list(at)
        at = [x + times * u for x, u in zip(at, uses[s])]
    base["F"] = [0] * 8

    last_user = {"A": [f"win{m}" for m in range(18)] + [f"wo{m}" for m in range(8)],
                 "M": ["mg0"] * 4 + ["md1"] * 2 + ["mg1"] * 4 + ["md1"] * 2,
                 "F": ["fg0", "fu0", "fg1", "fu1", "fd7", "fd7"],
                 "L": [f"dav{NT - 1}"] * 4 + [f"rv{NT - 1}"] * 2
                      + [f"d{x}{h}" for h in range(DH) for x in "qk"]
                      + [f"{x}{c}" for x in ("rq", "rk") for c in range(2)] + HALVES
                      + [f"gate{b}_0" for b in range(3)]
                      + [j for m in range(8) for j in [f"gate{b}_{m + 1}" for b in range(3) if m < 7] + [f"br2_{m}"]]
                      + [f"wout{m}" for m in range(8)]
                      + [f"ff{x}{k}" for k in range(KF) for x in "gu"]
                      + [f"fo{min(7, (8 * s + 7) // KF)}" for s in range(KF)]}
    n_slots = {s: len(v) for s, v in last_user.items()}
    slot0 = {"A": 0, "L": n_slots["A"]}
    at0 = {"A": 0, "M": n_slots["A"], "L": n_slots["A"] + NPAIR * n_slots["M"]}
    SPLIT = [s for s, job in enumerate(last_user["L"]) if not job.startswith(("br", "wout", "fo"))]
    assert n_slots["M"] == RM and n_slots["F"] == RF and n_slots["L"] % R == 0

    C, nC = offsets(CONST_COLS)
    CE, nCE = offsets(EARLY_COLS)
    A1, nA1 = offsets(P1_COLS)
    W1, nW1 = offsets(W1_COLS)
    A2, nA2 = offsets(P2_COLS)

    with ExitStack() as ctx:
        def sb(name, shape, dt=F32):
            return ctx.enter_context(nc.sbuf_tensor(name, shape, dt))

        def sem(name):
            return ctx.enter_context(nc.semaphore(name))

        X = sb("X", [P, KD, T])
        with nc.sbuf_tensor("H", [P, KD, T], F32) as H:
            pass
        H_high = sb("H_high", [P, KD, T], F32R)
        with nc.sbuf_tensor("ring", [P, R, TPS * P], F32) as ring:
            pass
        ring_low = sb("ring_low", [P, R, TPS * P], F32R)
        with nc.sbuf_tensor("early", [P, nCE + nA1 + nW1], F32) as early:
            pass
        H_low = sb("H_low", [P, KD, T], F32R)
        W_high = sb("W_high", [P, 2, TPS * P], F32R)
        sb("early_rest", [P, nCE + nA1 + nW1 - KD * T - 2 * TPS * P])
        p1 = early[:, nCE:nCE + nA1]
        w1 = early[:, nCE + nA1:nCE + nA1 + nW1]
        cst = sb("cst", [P, nC])
        p2 = sb("p2", [P, nA2])
        small = sb("small", [P, 64])
        arena = sb("arena", [P, ARENA])
        bank = [ctx.enter_context(nc.psum_tensor(f"bank{b}", [P, 512], F32)) for b in range(8)]
        scratch = nc.dram_tensor("comb_scratch", [NE, T], F32, kind="Internal").ap()
        sorted_x = nc.dram_tensor("sorted_x", [ROWS + 2 * T, D], F32, kind="Internal").ap()
        sorted_y = nc.dram_tensor("sorted_y", [ROWS, D], F32, kind="Internal").ap()
        bias_scratch = nc.dram_tensor("bias_scratch", [DH, P * 640], F32, kind="Internal").ap()

        bank_full = [sem(f"bank_full{b}") for b in range(8)]
        bank_free = [sem(f"bank_free{b}") for b in range(8)]
        slot_full = [sem(f"slot_full{r}") for r in range(R)]
        expert_slot_full = [sem(f"expert_slot_full{r}") for r in range(RM)]
        dense_slot_full = [sem(f"dense_slot_full{r}") for r in range(RF)]
        dense_bank_full = [sem(f"dense_bank_full{b}") for b in range(8)]
        dense_bank_free = [sem(f"dense_bank_free{b}") for b in range(8)]
        FULL = {x: dense_bank_full if x == "F" else bank_full for x in jobs}
        FREE = {x: dense_bank_free if x == "F" else bank_free for x in jobs}
        events = {}
        posts = {}
        ended = []

        def ev(name):
            if name not in events:
                events[name] = sem(name)
            return events[name]

        def cc(name, p=slice(0, P), n=None):
            o, w = C[name] if name in C else CE[name]
            return (cst if name in C else early)[p, o:o + (n or w)]

        def par(t, tab, name, i=0, n=1, p=slice(0, P)):
            o, _ = tab[name]
            return t[p, o + i:o + i + n]

        def ch(at_, n=1, w=512):
            return arena[:, at_:at_ + n * w].rearrange("p (n w) -> p n w", n=n)

        class Engine:

            def __init__(self, eng, name):
                self.e, self.name = eng, name
                self.sec, self.l = "A", 0
                self.chain, self.n = (sem(f"{name}_chain"), 0) if name in ("dve", "act", "pool") else (None, 0)

            def use(self, job):
                s, n = JOB[job]
                assert s == self.sec or self.sec != "A", (job, self.sec)
                b = n % 8
                if s == self.sec:
                    return b, base[s][b] + n // 8 + self.l * uses[s][b]
                return b, base[s][b] + n // 8 + (TIMES[s] - 1) * uses[s][b]

            def filled(self, job):
                b, n = self.use(job)
                return FULL[JOB[job][0]][b], n + 1

            def taken(self, job):
                b, n = self.use(job)
                return FREE[JOB[job][0]][b], n + 1 + (JOB[job][0] == "F")

            def emptied(self, job):
                b, n = self.use(job)
                return FREE[JOB[job][0]][b], n + (JOB[job][0] == "F")

            def nth(self, name, n=1):
                return ev(name), n + self.l * PER[name] if name in PER else n

            def landed(self, name):
                return ev(name), 16 + self.l * 16

            def fills(self, job):
                ended.append((job, "full"))
                return FULL[JOB[job][0]][JOB[job][1] % 8]

            def takes(self, job):
                ended.append((job, "free"))
                return FREE[JOB[job][0]][JOB[job][1] % 8]

            def tells(self, name):
                posts[name] = posts.get(name, 0) + 1
                return ev(name)

            def chained(self):
                self.n += 1
                return self.chain

            def restart(self):
                self.e.wait_ge(self.chain, self.n)
                self.e.sem_clear(self.chain)
                self.n = 0

        def bank_of(job):
            return bank[JOB[job][1] % 8]

        V, S, G = nc.vector, nc.scalar, nc.gpsimd

        def tt(o, a, b, op):
            return V.tensor_tensor(o, a, b, op)

        def ts(o, a, s1, s2, op0, op1=None):
            return V.tensor_scalar(o, a, s1, s2, op0, op1) if op1 is not None else V.tensor_scalar(o, a, s1, None, op0)

        def stt(o, a, s, b, op0, op1):
            return V.scalar_tensor_tensor(out=o, in0=a, scalar=s, in1=b, op0=op0, op1=op1)

        def act_(o, i, f, bias=0.0, scale=1.0, accum=None):
            if f == ACT.Copy:
                return S.activation(o, i, f)
            kw = {} if accum is None else {"accum_out": accum}
            if isinstance(bias, float) and bias != 0.0:
                bias = small[0:o.shape[0], BIAS[bias]:BIAS[bias] + 1]
            return S.activation(o, i, f, bias=bias, scale=scale, **kw)

        BIAS = {EPS: 60, 1e-12: 61, LNX_EPS: 62}

        def tiles4(ap):
            return ap.rearrange("p (n w) -> p n w", n=4)

        def over4(ap):
            return ap.unsqueeze(1).to_broadcast([ap.shape[0], 4, 128])

        RS_ = 516
        RAW = arena[:, 0:14 * RS_].rearrange("p (n w) -> p n w", n=14)
        m0 = 14 * RS_ + 8
        CQ, KR, COS, SIN = ch(m0, 3), ch(m0 + 1536), ch(m0 + 2048), ch(m0 + 2560)
        Q1, K1 = ch(m0 + 3072, 8), ch(m0 + 3072 + 4096, 8)
        o_ = m0 + 3072 + 8192
        VT1, PT1, S1, TM = ch(o_, 4), ch(o_ + 2048, 4), ch(o_ + 4096, 2), ch(o_ + 5120, 6)
        OM = H[:, 0:4, :]
        names = ["LW", "A", "G", "KK", "KP", "B", "SQ", "RS", "BON", "L", "EL", "ENL", "ELX", "AT", "BT",
                 "KT", "RT", "BH", "KH", "TKV", "TKB", "TKK", "Y", "MT0", "MT1", "TI0", "TI1", "TT0", "TT1",
                 "XX0", "XX1", "MK0", "MK1", "MB0", "MB1", "MR0", "MR1"]
        W = {n: arena[:, m0 + 512 * i:m0 + 512 * (i + 1)] for i, n in enumerate(names)}
        for i, n in enumerate(("ST", "US")):
            W[n] = arena[:, m0 + 512 * len(names) + 128 * i:m0 + 512 * len(names) + 128 * i + 128]
        units1 = [(h, i) for h in range(HM) for i in range(NT)]
        ident = cc("ident")

        def weights(pe, s, sec="A", it=0):
            g = slot0[sec] + s
            r = g % R
            n = g // R + 1
            if sec != "A":
                n = n + pe.l * (n_slots[sec] // R)
            pe.e.wait_ge(slot_full[r], 16 * n)
            return ring[:, r, :].rearrange("p (k n) -> p k n", k=TPS)

        mm = nc.tensor.matmul

        def pe_A(pe):
            e = pe.e
            e.wait_ge(ev("consts_in"), 16)
            e.wait_ge(ev("p1_in"), 16)
            ps = bank_of("ssq1")
            for c in range(KD):
                pe.e.wait_ge(*pe.nth("sq1", c + 1))
                i = mm(ps[:, :], cc("ones"), Q1[:, c, :], start=c == 0, stop=c == KD - 1)
            i.then_inc(pe.fills("ssq1"), 1)

            def project(m):
                w = weights(pe, m)
                if m >= 5:
                    pe.e.wait_ge(*pe.emptied(f"win{m}"))
                ps = bank_of(f"win{m}")
                o = ps[64:96, :] if m == 3 else ps[:, :]
                for k in range(KD):
                    if m == 0:
                        pe.e.wait_ge(*pe.nth("h1", k + 1))
                    i = mm(o, w[:, k, 0:32] if m == 3 else w[:, k, :], H[:, k, :], start=k == 0, stop=k == KD - 1)
                i.then_inc(pe.fills(f"win{m}"), 1)

            for m in range(4):
                project(m)
            ps = bank_of("cqss")
            for c in range(2):
                pe.e.wait_ge(*pe.nth("cqsq", c + 1))
                i = mm(ps[:, :], cc("ones"), TM[:, c, :], start=c == 0, stop=c == 1)
            i.then_inc(pe.fills("cqss"), 1)
            ps = bank_of("ckvss")
            pe.e.wait_ge(*pe.nth("cqsq", 3))
            mm(ps[:, :], cc("ones"), TM[:, 2, :], start=True, stop=True).then_inc(pe.fills("ckvss"), 1)
            project(4)
            project(5)
            e.wait_ge(ev("w1_in"), 16)
            uv = par(w1, W1, "uv", 0, 512)
            pe.e.wait_ge(*pe.nth("cqn", 3))
            for i_ in range(NT):
                pe.e.wait_ge(*pe.emptied(f"vm{i_}"))
                ps = bank_of(f"vm{i_}")
                mm(ps[:, :], CQ[:, 2, i_ * P:(i_ + 1) * P], uv, start=True, stop=True).then_inc(pe.fills(f"vm{i_}"), 1)
            for h in range(HM):
                pe.e.wait_ge(*pe.emptied(f"q{h}"))
                ps = bank_of(f"q{h}")
                for k in range(2):
                    i = mm(ps[0:QK, :], par(w1, W1, "uq", k * 768 + h * QK, QK), CQ[:, k, :], start=k == 0, stop=k == 1)
                i.then_inc(pe.fills(f"q{h}"), 1)
                pe.e.wait_ge(*pe.emptied(f"k{h}"))
                ps = bank_of(f"k{h}")
                mm(ps[0:NOPE, :], par(w1, W1, "uk", h * NOPE, NOPE), CQ[:, 2, :], start=True, stop=True).then_inc(pe.fills(f"k{h}"), 1)
                if between(h, 0):
                    project(6 + 2 * h)
                for j, x in enumerate("qk"):
                    pe.e.wait_ge(*pe.emptied(f"{x}ss{h}"))
                    ps = bank_of(f"{x}ss{h}")
                    pe.e.wait_ge(*pe.nth("qksq", 2 * h + j + 1))
                    mm(ps[0:QK, :], cc("ones", slice(0, QK), QK), TM[0:QK, j, :], start=True, stop=True).then_inc(pe.fills(f"{x}ss{h}"), 1)
                if between(h, 1):
                    project(7 + 2 * h)
                for j, x in enumerate("qk"):
                    pe.e.wait_ge(*pe.emptied(f"{x}p{h}"))
                    ps = bank_of(f"{x}p{h}")
                    pe.e.wait_ge(*pe.nth("qkn", 2 * h + j + 1))
                    src = (Q1 if x == "q" else K1)[0:QK, h, :]
                    mm(ps[0:QK, :], cc("perm96", slice(0, QK), QK), src, start=True, stop=True).then_inc(pe.fills(f"{x}p{h}"), 1)

            def scores(n):
                h, i_ = units1[n]
                pe.e.wait_ge(*pe.emptied(f"ms{h}_{i_}"))
                ps = bank_of(f"ms{h}_{i_}")
                if i_ == 0:
                    pe.e.wait_ge(*pe.nth("qkrot", 2 * h + 2))
                i = mm(ps[:, 0:(i_ + 1) * P], Q1[0:QK, h, i_ * P:(i_ + 1) * P], K1[0:QK, h, 0:(i_ + 1) * P], start=True, stop=True)
                i.then_inc(pe.fills(f"ms{h}_{i_}"), 1)

            def turn(n):
                h, i_ = units1[n]
                pe.e.wait_ge(*pe.emptied(f"mt{h}_{i_}"))
                ps = bank_of(f"mt{h}_{i_}")
                pe.e.wait_ge(*pe.nth("mprob", n + 1))
                for j in range(i_ + 1):
                    i = nc.tensor.transpose(ps[:, j * P:(j + 1) * P], S1[:, n % 2, j * P:(j + 1) * P], ident)
                i.then_inc(pe.fills(f"mt{h}_{i_}"), 1)
                if i_ == NT - 1:
                    mo(h)

            def mo(h):
                job = f"mo{h // 2}"
                if h % 2 == 0:
                    return
                pe.e.wait_ge(*pe.emptied(job))
                ps = bank_of(job)
                for hh in (h - 1, h):
                    pe.e.wait_ge(*pe.taken(f"mt{hh}_{NT - 1}"))
                    pt = PTs[hh % 2]
                    for j in range(NT):
                        i = mm(ps[64 * (hh % 2):64 * (hh % 2) + 64, j * P:T], VT1[:, j, hh * 64:hh * 64 + 64],
                               pt[:, j, j * P:T], start=j == 0, stop=j == NT - 1)
                i.then_inc(pe.fills(job), 1)

            for n in range(len(units1)):
                scores(n)
                if n:
                    turn(n - 1)
            turn(len(units1) - 1)
            pe.e.wait_ge(*pe.emptied("moss"))
            ps = bank_of("moss")
            for c in range(4):
                pe.e.wait_ge(*pe.nth("mosq", c + 1))
                i = mm(ps[:, :], cc("ones"), TM[:, c, :], start=c == 0, stop=c == 3)
            i.then_inc(pe.fills("moss"), 1)
            for c in range(4):
                rwkv_pe(pe, c)
            for m in range(8):
                w = weights(pe, 18 + m)
                pe.e.wait_ge(*pe.emptied(f"wo{m}"))
                ps = bank_of(f"wo{m}")
                for k in range(KD):
                    if m == 0 and k == 0:
                        pe.e.wait_ge(*pe.nth("mla_out", 4))
                    if m == 0 and k == 4:
                        pe.e.wait_ge(*pe.nth("rw_out", 4))
                    i = mm(ps[:, :], w[:, k, :], H[:, k, :], start=k == 0, stop=k == KD - 1)
                i.then_inc(pe.fills(f"wo{m}"), 1)
            pe.e.wait_ge(*pe.emptied("ssq2"))
            ps = bank_of("ssq2")
            for c in range(KD):
                pe.e.wait_ge(*pe.nth("sq2", c + 1))
                i = mm(ps[:, :], cc("ones"), SQ2[:, c, :], start=c == 0, stop=c == KD - 1)
            i.then_inc(pe.fills("ssq2"), 1)
            pe.e.wait_ge(*pe.emptied("route"))
            ps = bank_of("route")
            for i_ in range(NT):
                for k in range(KD):
                    pe.e.wait_ge(*pe.nth("h2", k + 1))
                    i = mm(ps[:, i_ * 36:i_ * 36 + 36], H[:, k, i_ * P:(i_ + 1) * P], par(p1, A1, "w_route", k * 36, 36),
                           start=k == 0, stop=k == KD - 1)
            i.then_inc(pe.fills("route"), 1)
            for i_ in range(NT):
                for x in range(2):
                    job = f"ht{i_}_{x}"
                    pe.e.wait_ge(*pe.emptied(job))
                    ps = bank_of(job)
                    for c in range(4):
                        i = nc.tensor.transpose(ps[:, c * P:(c + 1) * P], H[:, 4 * x + c, i_ * P:(i_ + 1) * P], ident)
                    i.then_inc(pe.fills(job), 1)
            pe.e.wait_ge(*pe.emptied("pos"))
            ps = bank_of("pos")
            e.wait_ge(ev("before_in"), 16)
            pe.e.wait_ge(*pe.nth("mask", 1))
            mask = RT("mask").rearrange("p (n e) -> p n e", n=NT)
            for i_ in range(NT + 1):
                for j in range(min(i_ + 1, NT)):
                    i = mm(ps[:, i_ * NE:(i_ + 1) * NE], BEFORE if j == i_ else cc("ones"), mask[:, j, :],
                           start=j == 0, stop=j == min(i_, NT - 1))
            i.then_inc(pe.fills("pos"), 1)
            pe.e.wait_ge(*pe.emptied("combT"))
            ps = bank_of("combT")
            pe.e.wait_ge(*pe.nth("comb", 1))
            for i_ in range(NT):
                i = nc.tensor.transpose(ps[0:NE, i_ * P:(i_ + 1) * P], COMB[:, i_, :], ident)
            i.then_inc(pe.fills("combT"), 1)
            pe.e.wait_ge(ev("rows_in"), 16)
            turn_rows(pe, "pxt")

        def turn_rows(pe, job):
            for x in range(2):
                pe.e.wait_ge(*pe.emptied(f"{job}{x}"))
                ps = bank_of(f"{job}{x}")
                for c in range(4):
                    i = nc.tensor.transpose(ps[:, c * P:(c + 1) * P], XG[:, (4 * x + c) * P:(4 * x + c + 1) * P], ident)
                i.then_inc(pe.fills(f"{job}{x}"), 1)

        PTs = [PT1, ch(m0, 4)]

        def rwkv_pe(pe, c):
            e = pe.e
            pe.e.wait_ge(*pe.emptied(f"ru{c}"))
            ps = bank_of(f"ru{c}")
            if c == 0:
                pe.e.wait_ge(*pe.nth("wa_in", 1))
            cw = slice(c * P, (c + 1) * P)
            w2a2 = par(w1, W1, "w2a2", 0, 512)
            mm(ps[:, :], w2a2[0:64, cw], RAW[0:64, 12, 1:513], start=True, stop=True).then_inc(pe.fills(f"ru{c}"), 1)
            pe.e.wait_ge(*pe.emptied(f"ra{c}"))
            ps = bank_of(f"ra{c}")
            mm(ps[:, :], w2a2[64:128, cw], RAW[64:128, 12, 1:513], start=True, stop=True).then_inc(pe.fills(f"ra{c}"), 1)
            pe.e.wait_ge(*pe.emptied(f"rg{c}"))
            ps = bank_of(f"rg{c}")
            if c == 0:
                pe.e.wait_ge(*pe.nth("gl_in", 1))
            mm(ps[:, :], par(w1, W1, "g2", c * P, P), RAW[:, 13, 1:513], start=True, stop=True).then_inc(pe.fills(f"rg{c}"), 1)
            pe.e.wait_ge(*pe.emptied(f"rkk{c}"))
            ps = bank_of(f"rkk{c}")
            pe.e.wait_ge(*pe.nth("kksq", c + 1))
            mm(ps[:, :], cc("blk64"), W["SQ"], start=True, stop=True).then_inc(pe.fills(f"rkk{c}"), 1)
            pe.e.wait_ge(*pe.emptied(f"rb{c}"))
            ps = bank_of(f"rb{c}")
            pe.e.wait_ge(*pe.nth("rkr", c + 1))
            mm(ps[:, :], cc("blk64"), W["Y"], start=True, stop=True).then_inc(pe.fills(f"rb{c}"), 1)
            for j, (x, src) in enumerate((("v", RAW[:, 8 + c, 1:513]), ("b", W["BH"]), ("k", W["KH"]), ("a", W["AT"]))):
                pe.e.wait_ge(*pe.emptied(f"rt{c}_{x}"))
                ps = bank_of(f"rt{c}_{x}")
                pe.e.wait_ge(*pe.nth("hats", c + 1))
                for i_ in range(NT):
                    i = nc.tensor.transpose(ps[:, i_ * P:(i_ + 1) * P], src[:, i_ * P:(i_ + 1) * P], ident)
                i.then_inc(pe.fills(f"rt{c}_{x}"), 1)
            pairs = {"abT": ("AT", "BT"), "ab": ("BT", "AT"), "ak": ("KT", "AT"), "br": ("BT", "RT"), "kr": ("KT", "RT")}
            for hh in range(2):
                hp = slice(64 * hh, 64 * hh + 64)
                for x, (l_, r_) in pairs.items():
                    pe.e.wait_ge(*pe.emptied(f"m{x}{c}_{hh}"))
                    ps = bank_of(f"m{x}{c}_{hh}")
                    for i_ in range(NT):
                        tk = slice(i_ * P, (i_ + 1) * P)
                        i = mm(ps[:, tk], W[l_][hp, tk], W[r_][hp, tk], start=True, stop=True)
                    i.then_inc(pe.fills(f"m{x}{c}_{hh}"), 1)
            pe.e.wait_ge(*pe.emptied(f"rwk{c}"))
            ps = bank_of(f"rwk{c}")
            pe.e.wait_ge(*pe.taken(f"rt{c}_v"))
            for hh in range(2):
                pe.e.wait_ge(*pe.taken(f"mak{c}_{hh}"))
                for i_ in range(NT):
                    tk, fe = slice(i_ * P, (i_ + 1) * P), slice(i_ * P + 64 * hh, i_ * P + 64 * hh + 64)
                    i = mm(ps[:, fe], W[f"MK{hh}"][:, tk], W["TKV"][:, fe], start=True, stop=True)
            i.then_inc(pe.fills(f"rwk{c}"), 1)
            for lev in (2, 4, 8, 16, 32):
                for hh in range(2):
                    pe.e.wait_ge(*pe.emptied(f"ix{c}_{lev}_{hh}"))
                    ps = bank_of(f"ix{c}_{lev}_{hh}")
                    pe.e.wait_ge(*pe.nth("tinv", 2 * c + hh + 1)) if lev == 2 else pe.e.wait_ge(*pe.taken(f"iy{c}_{lev // 2}_{hh}"))
                    for i_ in range(NT):
                        tk = slice(i_ * P, (i_ + 1) * P)
                        i = mm(ps[:, tk], W[f"MT{hh}"][:, tk], W[f"TI{hh}"][:, tk], start=True, stop=True)
                    i.then_inc(pe.fills(f"ix{c}_{lev}_{hh}"), 1)
                for hh in range(2):
                    pe.e.wait_ge(*pe.taken(f"ix{c}_{lev}_{hh}"))
                    for x, l_, r_ in (("y", "TT", "XX"), ("z", "XX", "TT")):
                        if x == "z" and lev == 32:
                            continue
                        pe.e.wait_ge(*pe.emptied(f"i{x}{c}_{lev}_{hh}"))
                        ps = bank_of(f"i{x}{c}_{lev}_{hh}")
                        for i_ in range(NT):
                            tk = slice(i_ * P, (i_ + 1) * P)
                            i = mm(ps[:, tk], W[f"{l_}{hh}"][:, tk], W[f"{r_}{hh}"][:, tk], start=True, stop=True)
                        i.then_inc(pe.fills(f"i{x}{c}_{lev}_{hh}"), 1)
            pe.e.wait_ge(*pe.emptied(f"rta{c}"))
            ps = bank_of(f"rta{c}")
            pe.e.wait_ge(*pe.taken(f"rt{c}_a"))
            for hh in range(2):
                pe.e.wait_ge(*pe.taken(f"iy{c}_32_{hh}"))
                for i_ in range(NT):
                    tk, fe = slice(i_ * P, (i_ + 1) * P), slice(i_ * P + 64 * hh, i_ * P + 64 * hh + 64)
                    i = mm(ps[64 * hh:64 * hh + 64, tk], W["KK"][:, fe], W[f"TI{hh}"][:, tk], start=True, stop=True)
            i.then_inc(pe.fills(f"rta{c}"), 1)
            pe.e.wait_ge(*pe.taken(f"rwk{c}"))
            hps = [slice(0, 64), slice(64, 128)]
            for n in range(NCH):
                i_, pp = n // 2, n % 2
                tp = slice(64 * pp, 64 * pp + 64)
                blk = slice(i_ * P + 64 * pp, i_ * P + 64 * pp + 64)
                tk = slice(n * 64, n * 64 + 64)
                fes = [slice(i_ * P + 64 * hh, i_ * P + 64 * hh + 64) for hh in range(2)]
                pe.e.wait_ge(*pe.emptied(f"cu{c}_{n}"))
                ps = bank_of(f"cu{c}_{n}")
                if n:
                    pe.e.wait_ge(*pe.taken(f"rta{c}"))
                    pe.e.wait_ge(*pe.taken(f"cs{c}_{n - 1}"))
                    mm(ps[tp, 0:P], W["B"][:, tk], W["ST"], start=True, stop=True)
                for hh in range(2):
                    i = mm(ps[tp, hps[hh]], W[f"TI{hh}"][:, blk], W["RS"][:, fes[hh]], start=n == 0, stop=True, skip_group_check=True)
                i.then_inc(pe.fills(f"cu{c}_{n}"), 1)
                pe.e.wait_ge(*pe.emptied(f"cy{c}_{n}"))
                py = bank_of(f"cy{c}_{n}")
                if n:
                    mm(py[:, 0:64], W["ST"], W["RT"][:, tk], start=True, stop=True)
                for hh in range(2):
                    mm(py[hps[hh], 0:64], W["TKV"][:, fes[hh]], W[f"MR{hh}"][:, blk], start=n == 0, stop=True, skip_group_check=True)
                if n < NCH - 1:
                    pe.e.wait_ge(*pe.emptied(f"cs{c}_{n}"))
                    ps = bank_of(f"cs{c}_{n}")
                    for hh in range(2):
                        mm(ps[hps[hh], 0:64], W["TKK"][tp, fes[hh]], W["TKV"][tp, fes[hh]], start=True, stop=True, skip_group_check=True)
                pe.e.wait_ge(*pe.taken(f"cu{c}_{n}"))
                if n < NCH - 1:
                    for hh in range(2):
                        i = mm(ps[hps[hh], 0:64], W["TKB"][tp, fes[hh]], W["US"][tp, hps[hh]], start=False, stop=True, skip_group_check=True)
                    i.then_inc(pe.fills(f"cs{c}_{n}"), 1)
                for hh in range(2):
                    i = mm(py[hps[hh], 0:64], W["US"][:, hps[hh]], W[f"MB{hh}"][:, blk], start=False, stop=True, skip_group_check=True)
                i.then_inc(pe.fills(f"cy{c}_{n}"), 1)
            pe.e.wait_ge(*pe.emptied(f"gm{c}"))
            ps = bank_of(f"gm{c}")
            pe.e.wait_ge(*pe.taken(f"cy{c}_{NCH - 1}"))
            mm(ps[:, :], cc("blk64"), W["Y"], start=True, stop=True).then_inc(pe.fills(f"gm{c}"), 1)
            pe.e.wait_ge(*pe.emptied(f"gv{c}"))
            ps = bank_of(f"gv{c}")
            pe.e.wait_ge(*pe.nth("gnsq", c + 1))
            mm(ps[:, :], cc("blk64"), W["SQ"], start=True, stop=True).then_inc(pe.fills(f"gv{c}"), 1)

        def act_A(sc):
            e = sc.e
            e.wait_ge(ev("x_in"), 16)
            for c in range(KD):
                act_(Q1[:, c, :], X[:, c, :], ACT.Square).then_inc(sc.tells("sq1"), 1)
            sc.e.wait_ge(*sc.filled("ssq1"))
            ps = bank_of("ssq1")
            sc.e.wait_ge(*sc.nth("bias_cols", 3))
            act_(TM[:, 0, :], ps[:, :], ACT.Sqrt, EPS, 1.0 / D).then_inc(sc.takes("ssq1"), 1)
            for n, o in enumerate((COS, SIN)):
                sc.e.wait_ge(*sc.nth("angles", n + 1))
                act_(o[0:QK, 0, :], o[0:QK, 0, :], ACT.Sin).then_inc(sc.tells("sines"), 1)
            for m in range(3):
                sc.e.wait_ge(*sc.filled(f"win{m}"))
                ps = bank_of(f"win{m}")
                if m == 0:
                    sc.e.wait_ge(*sc.taken("ssq1"))
                    sc.e.wait_ge(*sc.nth("h1", 8))
                act_(CQ[:, m, :], ps[:, :], ACT.Copy).then_inc(sc.takes(f"win{m}"), 1)
                sc.e.wait_ge(*sc.taken(f"win{m}"))
                act_(TM[:, m, :], CQ[:, m, :], ACT.Square).then_inc(sc.tells("cqsq"), 1)
            sc.e.wait_ge(*sc.filled("win3"))
            act_(KR[64:96, 0, :], bank_of("win3")[64:96, :], ACT.Copy).then_inc(sc.takes("win3"), 1)

            def feature_out(m):
                sc.e.wait_ge(*sc.filled(f"win{m}"))
                ps = bank_of(f"win{m}")
                act_(RAW[:, {4: 12, 5: 13}.get(m, m - 6), 1:513], ps[:, :], ACT.Copy).then_inc(sc.takes(f"win{m}"), 1)

            for j, (x, n, k) in enumerate((("cqss", QR, 3), ("ckvss", KVR, 4))):
                sc.e.wait_ge(*sc.filled(x))
                ps = bank_of(x)
                act_(TM[:, k, :], ps[:, :], ACT.Sqrt, EPS, 1.0 / n).then_inc(sc.takes(x), 1)
            feature_out(4)
            feature_out(5)
            for i_ in range(NT):
                sc.e.wait_ge(*sc.filled(f"vm{i_}"))
                ps = bank_of(f"vm{i_}")
                act_(VT1[:, i_, :], ps[:, :], ACT.Copy).then_inc(sc.takes(f"vm{i_}"), 1)
            for h in range(HM):
                for j, x in enumerate("qk"):
                    sc.e.wait_ge(*sc.taken(f"q{h}")) if x == "q" else sc.e.wait_ge(*sc.nth("kev", h + 1))
                    if h:
                        sc.e.wait_ge(*sc.filled(f"{x}ss{h - 1}"))
                    act_(TM[0:QK, j, :], (Q1 if x == "q" else K1)[0:QK, h, :], ACT.Square).then_inc(sc.tells("qksq"), 1)
                if between(h, 0):
                    feature_out(6 + 2 * h)
                for j, x in enumerate("qk"):
                    sc.e.wait_ge(*sc.filled(f"{x}ss{h}"))
                    ps = bank_of(f"{x}ss{h}")
                    if h:
                        sc.e.wait_ge(*sc.nth("qkn", 2 * h - 1 + j))
                    act_(TM[0:QK, 2 + j, :], ps[0:QK, :], ACT.Sqrt, EPS, 1.0 / QK).then_inc(sc.takes(f"{x}ss{h}"), 1)
                if between(h, 1):
                    feature_out(7 + 2 * h)
            for n, (h, i_) in enumerate(units1):
                sc.e.wait_ge(*sc.nth("mmax", n + 1))
                w = (i_ + 1) * P
                s = S1[:, n % 2, 0:w]
                act_(s, s, ACT.Exp, bias=small[:, 2 + n % 2:3 + n % 2], accum=small[:, 4 + n % 2:5 + n % 2]).then_inc(sc.tells("mexp"), 1)
                if n:
                    mla_turned(sc, n - 1)
            mla_turned(sc, len(units1) - 1)
            for c in range(4):
                sc.e.wait_ge(*sc.taken(f"mo{c}"))
                act_(TM[:, c, :], OM[:, c, :], ACT.Square).then_inc(sc.tells("mosq"), 1)
            sc.e.wait_ge(*sc.filled("moss"))
            ps = bank_of("moss")
            act_(TM[:, 4, :], ps[:, :], ACT.Sqrt, EPS, 1.0 / 512).then_inc(sc.takes("moss"), 1)
            sc.e.wait_ge(*sc.nth("shifted", 14))
            act_(RAW[0:64, 12, 1:513], RAW[0:64, 12, 1:513], ACT.Tanh).then_inc(sc.tells("wa_in"), 1)
            act_(RAW[:, 13, 1:513], RAW[:, 13, 1:513], ACT.Tanh, scale=0.5).then_inc(sc.tells("gl_t"), 1)
            for c in range(4):
                rwkv_act(sc, c)
            for c in range(KD):
                sc.e.wait_ge(*sc.taken(f"wo{c}"))
                act_(SQ2[:, c, :], X[:, c, :], ACT.Square).then_inc(sc.tells("sq2"), 1)
            sc.e.wait_ge(*sc.filled("ssq2"))
            ps = bank_of("ssq2")
            act_(TM[:, 0, :], ps[:, :], ACT.Sqrt, EPS, 1.0 / D).then_inc(sc.takes("ssq2"), 1)
            rows_out(sc, 0)
            rows_out(sc, 1)
            sc.e.wait_ge(*sc.nth("gsub", 1))
            act_(RT("gexp"), RT("gsub"), ACT.Exp).then_inc(sc.tells("gexp"), 1)
            rows_out(sc, 2)
            sc.e.wait_ge(*sc.nth("vdiff", 1))
            act_(RT("e21"), RT("vdiff"), ACT.Exp).then_inc(sc.tells("e21"), 1)
            rows_out(sc, 3)
            sc.e.wait_ge(*sc.filled("combT"))
            ps = bank_of("combT")
            act_(CT[0:NE, 0, :], ps[0:NE, :], ACT.Copy).then_inc(sc.takes("combT"), 1)
            sc.e.wait_ge(*sc.taken("combT"))
            e.dma_start(scratch, CT[0:NE, 0, :]).then_inc(ev("comb_stored"), 16)

        def rows_out(sc, i_):
            for x in range(2):
                sc.e.wait_ge(*sc.filled(f"ht{i_}_{x}"))
                ps = bank_of(f"ht{i_}_{x}")
                act_(HT[:, i_, 512 * x:512 * x + 512], ps[:, :], ACT.Copy).then_inc(sc.takes(f"ht{i_}_{x}"), 1)

        def mla_turned(sc, n):
            h, i_ = units1[n]
            sc.e.wait_ge(*sc.filled(f"mt{h}_{i_}"))
            ps = bank_of(f"mt{h}_{i_}")
            if i_ == 0 and h >= 2:
                sc.e.wait_ge(*sc.filled(f"mo{(h - 2) // 2}"))
            o = PTs[h % 2][:, 0:i_ + 1, i_ * P:(i_ + 1) * P]
            act_(o, ps[:, 0:(i_ + 1) * P].rearrange("p (n w) -> p n w", n=i_ + 1), ACT.Copy).then_inc(sc.takes(f"mt{h}_{i_}"), 1)

        def rwkv_act(sc, c):
            if c == 0:
                sc.e.wait_ge(*sc.nth("mla_out", 4))
            else:
                sc.e.wait_ge(*sc.nth("rw_out", c))
            sc.e.wait_ge(*sc.nth("halves", 2))
            sc.e.wait_ge(*sc.filled(f"ru{c}"))
            ps = bank_of(f"ru{c}")
            act_(W["LW"], ps[:, :], ACT.Tanh, bias=small[:, 8 + c:9 + c], scale=0.5).then_inc(sc.takes(f"ru{c}"), 1)
            sc.e.wait_ge(*sc.filled(f"ra{c}"))
            ps = bank_of(f"ra{c}")
            act_(W["A"], ps[:, :], ACT.Tanh, bias=small[:, 12 + c:13 + c], scale=0.5).then_inc(sc.takes(f"ra{c}"), 1)
            sc.e.wait_ge(*sc.filled(f"rg{c}"))
            ps = bank_of(f"rg{c}")
            act_(W["G"], ps[:, :], ACT.Copy).then_inc(sc.takes(f"rg{c}"), 1)
            sc.e.wait_ge(*sc.nth("kk0", c + 1))
            act_(W["SQ"], W["KK"], ACT.Square).then_inc(sc.tells("kksq"), 1)
            sc.e.wait_ge(*sc.filled(f"rkk{c}"))
            ps = bank_of(f"rkk{c}")
            act_(W["RS"], ps[:, :], ACT.Sqrt, 1e-12).then_inc(sc.takes(f"rkk{c}"), 1)
            sc.e.wait_ge(*sc.nth("scan", 2 * c + 1))
            act_(W["EL"], W["L"], ACT.Exp).then_inc(sc.chained(), 1)
            act_(W["ENL"], W["L"], ACT.Exp, scale=-1.0).then_inc(sc.chained(), 1)
            sc.e.wait_ge(*sc.nth("scan", 2 * c + 2))
            act_(W["ELX"], W["ELX"], ACT.Exp).then_inc(sc.tells("explog"), 1)
            for x, d in (("v", "TKV"), ("b", "TKB"), ("k", "TKK"), ("a", "KK")):
                sc.e.wait_ge(*sc.filled(f"rt{c}_{x}"))
                ps = bank_of(f"rt{c}_{x}")
                act_(W[d], ps[:, :], ACT.Copy).then_inc(sc.takes(f"rt{c}_{x}"), 1)
            sc.e.wait_ge(*sc.filled(f"rwk{c}"))
            act_(W["RS"], bank_of(f"rwk{c}")[:, :], ACT.Copy).then_inc(sc.takes(f"rwk{c}"), 1)
            sc.e.wait_ge(*sc.filled(f"rta{c}"))
            act_(W["B"], bank_of(f"rta{c}")[:, :], ACT.Copy).then_inc(sc.takes(f"rta{c}"), 1)
            for n in range(NCH):
                pp = n % 2
                sc.e.wait_ge(*sc.filled(f"cy{c}_{n}"))
                ps = bank_of(f"cy{c}_{n}")
                if n == 0:
                    sc.e.wait_ge(*sc.taken(f"rb{c}"))
                act_(W["Y"][:, n * 64:n * 64 + 64], ps[:, 0:64], ACT.Copy).then_inc(sc.takes(f"cy{c}_{n}"), 1)
            sc.e.wait_ge(*sc.taken(f"gm{c}"))
            act_(W["SQ"], W["L"], ACT.Square).then_inc(sc.tells("gnsq"), 1)
            sc.e.wait_ge(*sc.filled(f"gv{c}"))
            ps = bank_of(f"gv{c}")
            act_(W["RS"], ps[:, :], ACT.Sqrt, LNX_EPS, 1.0 / RN).then_inc(sc.takes(f"gv{c}"), 1)

        def dve_A(dv):
            e = dv.e
            for i, v in enumerate((EPS, 1e-12, LNX_EPS)):
                V.memset(small[:, 60 + i:61 + i], v).then_inc(dv.tells("bias_cols"), 1)
            V.memset(RAW[:, :, 0:1], 0.0).then_inc(dv.chained(), 1)
            e.wait_ge(ev("pos_in"), 16)
            e.wait_ge(ev("consts_in"), 16)
            e.wait_ge(ev("p1_in"), 16)
            e.wait_ge(ev("x_in"), 16)
            pos = PT1[0:QK, 0, :].bitcast(I32)
            ang, kf, r = PT1[0:QK, 1, :], PT1[0:QK, 2, :], PT1[0:QK, 3, :]
            V.tensor_copy(ang, pos).then_inc(dv.chained(), 1); dv.e.wait_ge(dv.chain, dv.n)
            ts(ang, ang, cc("inv_freq", slice(0, QK)), None, ALU.mult).then_inc(dv.chained(), 1); dv.e.wait_ge(dv.chain, dv.n)
            MAGIC, C1, C2 = 12582912.0, 6.28125, 0.0019353071795864769
            for quarter, o in ((0.25, COS), (0.0, SIN)):
                o = o[0:QK, 0, :]
                ts(kf, ang, 0.15915494309189535, quarter, ALU.mult, ALU.add).then_inc(dv.chained(), 1); dv.e.wait_ge(dv.chain, dv.n)
                ts(kf, kf, MAGIC, None, ALU.add).then_inc(dv.chained(), 1); dv.e.wait_ge(dv.chain, dv.n)
                ts(kf, kf, -MAGIC, None, ALU.add).then_inc(dv.chained(), 1); dv.e.wait_ge(dv.chain, dv.n)
                stt(r, kf, -C1, ang, ALU.mult, ALU.add).then_inc(dv.chained(), 1); dv.e.wait_ge(dv.chain, dv.n)
                stt(r, kf, -C2, r, ALU.mult, ALU.add).then_inc(dv.chained(), 1); dv.e.wait_ge(dv.chain, dv.n)
                if quarter:
                    ts(r, r, 1.5707963267948966, None, ALU.add).then_inc(dv.chained(), 1); dv.e.wait_ge(dv.chain, dv.n)
                ts(o, r, 3.1415925, -3.1415925, ALU.min, ALU.max).then_inc(dv.tells("angles"), 1)
            norm(dv, "ssq1", X, H, lambda c: par(p1, A1, "g_mix", c), TM[:, 0, :], "h1")
            for x, ks, t, g in (("cqss", (0, 1), 3, "g_cq"), ("ckvss", (2,), 4, "g_ckv")):
                dv.e.wait_ge(*dv.taken(x))
                V.reciprocal(TM[:, t, :], TM[:, t, :]).then_inc(dv.chained(), 1); dv.e.wait_ge(dv.chain, dv.n)
                for k in ks:
                    stt(CQ[:, k, :], CQ[:, k, :], par(p1, A1, g, k if k < 2 else 0), TM[:, t, :], ALU.mult, ALU.mult).then_inc(dv.tells("cqn"), 1)
            dv.e.wait_ge(*dv.nth("sines", 2))
            for h in range(HM):
                dv.e.wait_ge(*dv.filled(f"q{h}"))
                ps = bank_of(f"q{h}")
                V.tensor_copy(Q1[0:QK, h, :], ps[0:QK, :]).then_inc(dv.takes(f"q{h}"), 1)
                dv.e.wait_ge(*dv.filled(f"k{h}"))
                ps = bank_of(f"k{h}")
                V.tensor_copy(K1[0:NOPE, h, :], ps[0:NOPE, :]).then_inc(dv.takes(f"k{h}"), 1)
                if h == 0:
                    dv.e.wait_ge(*dv.taken("win3"))
                V.tensor_copy(K1[NOPE:QK, h, :], KR[64:96, 0, :]).then_inc(dv.tells("kev"), 1)
                dv.e.wait_ge(*dv.nth("kev", h + 1))
                for j, x in enumerate("qk"):
                    dst = (Q1 if x == "q" else K1)[0:QK, h, :]
                    dv.e.wait_ge(*dv.taken(f"{x}ss{h}"))
                    V.reciprocal(TM[0:QK, 2 + j, :], TM[0:QK, 2 + j, :]).then_inc(dv.chained(), 1); dv.e.wait_ge(dv.chain, dv.n)
                    stt(dst, dst, par(p1, A1, f"g_{x}n", p=slice(0, QK)), TM[0:QK, 2 + j, :], ALU.mult, ALU.mult).then_inc(dv.tells("qkn"), 1)
                for j, x in enumerate("qk"):
                    dst = (Q1 if x == "q" else K1)[0:QK, h, :]
                    dv.e.wait_ge(*dv.filled(f"{x}p{h}"))
                    ps = bank_of(f"{x}p{h}")
                    tt(TM[0:QK, 4 + j, :], ps[0:QK, :], SIN[0:QK, 0, :], ALU.mult).then_inc(dv.takes(f"{x}p{h}"), 1)
                    dv.e.wait_ge(*dv.nth("qkn", 2 * h + 1 + j))
                    tt(dst, dst, COS[0:QK, 0, :], ALU.mult).then_inc(dv.chained(), 1); dv.e.wait_ge(dv.chain, dv.n)
                    dv.e.wait_ge(*dv.taken(f"{x}p{h}"))
                    tt(dst, dst, TM[0:QK, 4 + j, :], ALU.add).then_inc(dv.tells("qkrot"), 1)
            for n in range(len(units1)):
                mla_scores_dve(dv, n)
                if n:
                    mla_prob_dve(dv, n - 1)
                if n % 2 and n // 2 < 14:
                    c = n // 2
                    dv.e.wait_ge(*dv.taken(f"win{ {12: 4, 13: 5}.get(c, c + 6)}"))
                    tt(TM[:, c % 2, :], RAW[:, c, 0:512], RAW[:, c, 1:513], ALU.subtract).then_inc(dv.chained(), 1); dv.e.wait_ge(dv.chain, dv.n)
                    stt(RAW[:, c, 1:513], TM[:, c % 2, :], par(p1, A1, "mu", c), RAW[:, c, 1:513], ALU.mult, ALU.add).then_inc(dv.tells("shifted"), 1)
            mla_prob_dve(dv, len(units1) - 1)
            dv.e.wait_ge(*dv.taken("mo3"))
            dv.e.wait_ge(*dv.taken("moss"))
            V.reciprocal(TM[:, 4, :], TM[:, 4, :]).then_inc(dv.chained(), 1); dv.e.wait_ge(dv.chain, dv.n)
            for c in range(4):
                stt(H[:, c, :], OM[:, c, :], par(p1, A1, "g_mla_out", c), TM[:, 4, :], ALU.mult, ALU.mult).then_inc(dv.tells("mla_out"), 1)
            ts(small[:, 8:12], par(p1, A1, "w0", 0, 4), 0.5, None, ALU.mult).then_inc(dv.tells("halves"), 1)
            ts(small[:, 12:16], par(p1, A1, "a0", 0, 4), 0.5, None, ALU.mult).then_inc(dv.tells("halves"), 1)
            dv.e.wait_ge(*dv.nth("gl_t", 1))
            ts(RAW[:, 13, 1:513], RAW[:, 13, 1:513], 0.5, 0.5, ALU.mult, ALU.add).then_inc(dv.tells("gl_in"), 1)
            for c in range(4):
                rwkv_dve(dv, c)
            for m in range(8):
                dv.e.wait_ge(*dv.filled(f"wo{m}"))
                ps = bank_of(f"wo{m}")
                tt(X[:, m, :], X[:, m, :], ps[:, :], ALU.add).then_inc(dv.takes(f"wo{m}"), 1)
            dv.e.wait_ge(*dv.taken("wo7"))
            norm(dv, "ssq2", X, H, lambda c: par(p1, A1, "g_ffn", c), TM[:, 0, :], "h2")
            router(dv)

        def norm(dv, job, src, dst, g, r, event):
            dv.e.wait_ge(*dv.taken(job))
            V.reciprocal(r, r).then_inc(dv.chained(), 1); dv.e.wait_ge(dv.chain, dv.n)
            for c in range(KD):
                stt(dst[:, c, :], src[:, c, :], g(c), r, ALU.mult, ALU.mult).then_inc(dv.tells(event), 1)

        def norm_split(dv, job, g):
            dv.e.wait_ge(*dv.taken(job))
            r = TL[:, 0, :]
            V.reciprocal(r, r).then_inc(dv.chained(), 1); dv.e.wait_ge(dv.chain, dv.n)
            for c in range(KD):
                h = TL[:, 2 + c % 2, :]
                stt(h, X[:, c, :], g(c), r, ALU.mult, ALU.mult).then_inc(dv.chained(), 1); dv.e.wait_ge(dv.chain, dv.n)
                V.tensor_copy(H_high[:, c, :], h).then_inc(dv.chained(), 1); dv.e.wait_ge(dv.chain, dv.n)
                tt(H_low[:, c, :], h, H_high[:, c, :].bitcast(F32), ALU.subtract).then_inc(dv.tells("Lh"), 1)

        def mla_scores_dve(dv, n):
            h, i_ = units1[n]
            w = (i_ + 1) * P
            dv.e.wait_ge(*dv.filled(f"ms{h}_{i_}"))
            ps = bank_of(f"ms{h}_{i_}")
            if n >= 2:
                dv.e.wait_ge(*dv.filled("mt%d_%d" % units1[n - 2]))
            s = small[:, n % 2:n % 2 + 1]
            V.tensor_tensor_reduce(S1[:, n % 2, 0:w], ps[:, 0:w], cc("causal")[:, 512 - w:512], QK ** -0.5, 3 * NEG,
                                           ALU.add, ALU.max, s).then_inc(dv.takes(f"ms{h}_{i_}"), 1)
            dv.e.wait_ge(*dv.taken(f"ms{h}_{i_}"))
            ts(small[:, 2 + n % 2:3 + n % 2], s, -1.0, None, ALU.mult).then_inc(dv.tells("mmax"), 1)

        def mla_prob_dve(dv, n):
            h, i_ = units1[n]
            w = (i_ + 1) * P
            dv.e.wait_ge(*dv.nth("mexp", n + 1))
            r = small[:, 6 + n % 2:7 + n % 2]
            V.reciprocal(r, small[:, 4 + n % 2:5 + n % 2]).then_inc(dv.chained(), 1); dv.e.wait_ge(dv.chain, dv.n)
            ts(S1[:, n % 2, 0:w], S1[:, n % 2, 0:w], r, None, ALU.mult).then_inc(dv.tells("mprob"), 1)
            if n >= 4 and i_ == 1 and h % 2 == 0 and h:
                p = h // 2 - 1
                dv.e.wait_ge(*dv.filled(f"mo{p}"))
                ps = bank_of(f"mo{p}")
                V.tensor_copy(OM[:, p, :], ps[:, :]).then_inc(dv.takes(f"mo{p}"), 1)
            if n == len(units1) - 1:
                dv.e.wait_ge(*dv.filled("mo3"))
                ps = bank_of("mo3")
                V.tensor_copy(OM[:, 3, :], ps[:, :]).then_inc(dv.takes("mo3"), 1)

        def rwkv_dve(dv, c):
            r_, k_, v_ = (RAW[:, j + c, 1:513] for j in (0, 4, 8))
            w = W
            one = lambda n, i=None: par(p1, A1, n, c)
            if c == 0:
                dv.e.wait_ge(dv.chain, dv.n)
            dv.e.wait_ge(*dv.taken(f"ru{c}")); dv.e.wait_ge(*dv.taken(f"ra{c}"))
            ts(w["LW"], w["LW"], -0.5 * EXP_NEG_HALF, -0.5 * EXP_NEG_HALF, ALU.mult, ALU.add).then_inc(dv.chained(), 1)
            ts(w["A"], w["A"], 0.5, 0.5, ALU.mult, ALU.add).then_inc(dv.chained(), 1)
            ts(w["KK"], k_, one("k_k"), None, ALU.mult).then_inc(dv.tells("kk0"), 1)
            dv.e.wait_ge(dv.chain, dv.n)
            V.tensor_tensor_scan(w["L"], cc("scan_keep"), w["LW"], 0.0, ALU.mult, ALU.add).then_inc(dv.tells("scan"), 1)
            dv.e.wait_ge(*dv.nth("scan", 2 * c + 1))
            tt(w["ELX"], w["L"], w["LW"], ALU.subtract).then_inc(dv.tells("scan"), 1)
            ts(w["B"], w["A"], -1.0, one("k_a"), ALU.add, ALU.mult).then_inc(dv.chained(), 1); dv.e.wait_ge(dv.chain, dv.n)
            stt(w["KP"], w["B"], 1.0, k_, ALU.add, ALU.mult).then_inc(dv.chained(), 1); dv.e.wait_ge(dv.chain, dv.n)
            stt(w["Y"], r_, one("r_k"), w["KP"], ALU.mult, ALU.mult).then_inc(dv.tells("rkr"), 1)
            dv.e.wait_ge(*dv.taken(f"rkk{c}"))
            V.reciprocal(w["RS"], w["RS"]).then_inc(dv.chained(), 1); dv.e.wait_ge(dv.chain, dv.n)
            tt(w["KK"], w["KK"], w["RS"], ALU.mult).then_inc(dv.chained(), 1); dv.e.wait_ge(dv.chain, dv.n)
            tt(w["B"], w["KK"], w["A"], ALU.mult).then_inc(dv.chained(), 1)
            dv.e.wait_ge(*dv.filled(f"rb{c}"))
            ps = bank_of(f"rb{c}")
            tt(w["BON"], ps[:, :], v_, ALU.mult).then_inc(dv.takes(f"rb{c}"), 1)
            dv.e.wait_ge(dv.chain, dv.n)
            dv.e.wait_ge(*dv.nth("explog", c + 1))
            stt(w["AT"], w["KK"], -1.0, w["ELX"], ALU.mult, ALU.mult).then_inc(dv.chained(), 1)
            tt(w["BT"], w["B"], w["ENL"], ALU.mult).then_inc(dv.chained(), 1)
            tt(w["KT"], w["KP"], w["ENL"], ALU.mult).then_inc(dv.chained(), 1)
            tt(w["RT"], r_, w["EL"], ALU.mult).then_inc(dv.chained(), 1); dv.e.wait_ge(dv.chain, dv.n)
            c64 = lambda a: a.rearrange("p (n w) -> p n w", n=NCH)
            dc = c64(w["EL"])[:, :, 63:64].to_broadcast([P, NCH, 64])
            tt(c64(w["BH"]), c64(w["BT"]), dc, ALU.mult).then_inc(dv.chained(), 1)
            tt(c64(w["KH"]), c64(w["KT"]), dc, ALU.mult).then_inc(dv.tells("hats"), 1)
            for hh in range(2):
                dv.e.wait_ge(*dv.filled(f"mabT{c}_{hh}"))
                ps = bank_of(f"mabT{c}_{hh}")
                tt(tiles4(w[f"MT{hh}"]), tiles4(ps[:, :]), over4(cc("lower")), ALU.mult).then_inc(dv.chained(), 1)
                tt(tiles4(w[f"TT{hh}"]), tiles4(ps[:, :]), over4(cc("lev1T")), ALU.mult).then_inc(dv.takes(f"mabT{c}_{hh}"), 1)
                dv.e.wait_ge(*dv.taken(f"mabT{c}_{hh}"))
                tt(tiles4(w[f"TT{hh}"]), tiles4(w[f"TT{hh}"]), over4(ident), ALU.add).then_inc(dv.chained(), 1)
                dv.e.wait_ge(*dv.filled(f"mab{c}_{hh}"))
                ps = bank_of(f"mab{c}_{hh}")
                tt(tiles4(w[f"TI{hh}"]), tiles4(ps[:, :]), over4(cc("lev1")), ALU.mult).then_inc(dv.takes(f"mab{c}_{hh}"), 1)
                dv.e.wait_ge(*dv.taken(f"mab{c}_{hh}"))
                tt(tiles4(w[f"TI{hh}"]), tiles4(w[f"TI{hh}"]), over4(ident), ALU.add).then_inc(dv.tells("tinv"), 1)
                for x, d, m in (("ak", "MK", "upper"), ("br", "MB", "upper_eq"), ("kr", "MR", "upper_eq")):
                    dv.e.wait_ge(*dv.filled(f"m{x}{c}_{hh}"))
                    ps = bank_of(f"m{x}{c}_{hh}")
                    tt(tiles4(w[f"{d}{hh}"]), tiles4(ps[:, :]), over4(cc(m)), ALU.mult).then_inc(dv.takes(f"m{x}{c}_{hh}"), 1)
            for n, lev in enumerate((2, 4, 8, 16, 32)):
                for hh in range(2):
                    dv.e.wait_ge(*dv.filled(f"ix{c}_{lev}_{hh}"))
                    ps = bank_of(f"ix{c}_{lev}_{hh}")
                    tt(tiles4(w[f"XX{hh}"]), tiles4(ps[:, :]), over4(cc(f"lev{lev}")), ALU.mult).then_inc(dv.takes(f"ix{c}_{lev}_{hh}"), 1)
                for hh in range(2):
                    dv.e.wait_ge(*dv.nth("tinv", 2 * c + hh + 1)) if lev == 2 else dv.e.wait_ge(*dv.taken(f"iy{c}_{lev // 2}_{hh}"))
                    if lev != 32:
                        dv.e.wait_ge(*dv.filled(f"iz{c}_{lev}_{hh}"))
                        ps2 = bank_of(f"iz{c}_{lev}_{hh}")
                        dv.e.wait_ge(*dv.filled(f"iy{c}_{lev}_{hh}"))
                        ps = bank_of(f"iy{c}_{lev}_{hh}")
                        tt(w[f"TT{hh}"], w[f"TT{hh}"], ps2[:, :], ALU.add).then_inc(dv.takes(f"iz{c}_{lev}_{hh}"), 1)
                    else:
                        dv.e.wait_ge(*dv.filled(f"iy{c}_{lev}_{hh}"))
                        ps = bank_of(f"iy{c}_{lev}_{hh}")
                    tt(w[f"TI{hh}"], w[f"TI{hh}"], ps[:, :], ALU.add).then_inc(dv.takes(f"iy{c}_{lev}_{hh}"), 1)
            dcol = c64(w["EL"])[:, :, 63]
            for x in ("ST", "US"):
                V.memset(w[x], 0.0).then_inc(dv.chained(), 1)
            dv.e.wait_ge(dv.chain, dv.n)
            for n in range(NCH):
                tp = slice(64 * (n % 2), 64 * (n % 2) + 64)
                dv.e.wait_ge(*dv.filled(f"cu{c}_{n}"))
                ps = bank_of(f"cu{c}_{n}")
                V.tensor_copy(w["US"][tp, :], ps[tp, 0:P]).then_inc(dv.takes(f"cu{c}_{n}"), 1)
                if n < NCH - 1:
                    dv.e.wait_ge(*dv.filled(f"cs{c}_{n}"))
                    ps = bank_of(f"cs{c}_{n}")
                    if n:
                        dv.e.wait_ge(*dv.taken(f"cs{c}_{n - 1}"))
                    else:
                        dv.e.wait_ge(dv.chain, dv.n)
                    for hh in range(2):
                        hp = slice(64 * hh, 64 * hh + 64)
                        i = stt(w["ST"][hp, hp], w["ST"][hp, hp], dcol[hp, n:n + 1], ps[hp, 0:64], ALU.mult, ALU.add)
                    i.then_inc(dv.takes(f"cs{c}_{n}"), 1)
            dv.e.wait_ge(*dv.filled(f"gm{c}"))
            ps = bank_of(f"gm{c}")
            stt(w["L"], ps[:, :], -1.0 / RN, w["Y"], ALU.mult, ALU.add).then_inc(dv.takes(f"gm{c}"), 1)
            dv.e.wait_ge(*dv.taken(f"gv{c}"))
            V.reciprocal(w["RS"], w["RS"]).then_inc(dv.chained(), 1); dv.e.wait_ge(dv.chain, dv.n)
            stt(w["L"], w["L"], one("lnx_g"), w["RS"], ALU.mult, ALU.mult).then_inc(dv.chained(), 1); dv.e.wait_ge(dv.chain, dv.n)
            dv.e.wait_ge(*dv.taken(f"rb{c}"))
            stt(w["L"], w["L"], one("lnx_b"), w["BON"], ALU.add, ALU.add).then_inc(dv.chained(), 1); dv.e.wait_ge(dv.chain, dv.n)
            dv.e.wait_ge(*dv.taken(f"rg{c}"))
            tt(H[:, 4 + c, :], w["L"], w["G"], ALU.mult).then_inc(dv.tells("rw_out"), 1)

        rt_cols = [("lg", 144), ("gmax", 4), ("geq", 16), ("gidx", 16), ("gmin", 4), ("goh", 16), ("gsub", 16),
                   ("gexp", 16), ("gsum", 4), ("pg", 4), ("gpen", 16), ("me", 128), ("v1", 4), ("eq", 128),
                   ("idx", 128), ("oh1", 128), ("oh2", 128), ("v2", 4), ("vdiff", 4), ("e21", 4), ("mask", 128),
                   ("comb", 128), ("expert", 8), ("weight", 8), ("place", 8), ("over", 8), ("row", 8), ("miss", 8),
                   ("over_weight", 8), ("to_row", 8), ("from_row", 8), ("busiest", 1), ("overflow", 1)]
        RTC, nRT = offsets(rt_cols)
        rt0 = m0 + 3072 + 8192 + 8192
        def RT(n):
            o, w = RTC[n]
            return arena[:, rt0 + o:rt0 + o + w]
        COMB = RT("comb").rearrange("p (n e) -> p n e", n=NT)
        CT = ch(15360, 1)
        MRING = arena[:, 0:RM * TPS * P].rearrange("p (r n) -> p r n", r=RM)
        XG = arena[:, 12288:12288 + D]
        SQ2 = ch(12800, 8)
        XF = arena[:, 14336:14336 + D].rearrange("p (c n) -> p c n", c=KD)
        TGM = arena[:, 16384:16640].rearrange("p (e n) -> p e n", e=2)
        HIDM = arena[:, 16640:16896].rearrange("p (e n) -> p e n", e=2)
        HT = ch(16896, NT, D)
        YO = arena[:, 20992:20992 + D]
        YG = [ch(16896, NT, D), ch(20992 + 0, NT, D)]
        BEFORE = arena[:, rt0 - P:rt0]
        assert rt0 + nRT <= ARENA

        def router(dv):
            t = lambda n, e: RT(n).rearrange("p (n e) -> p n e", n=NT)
            st = lambda ins: (ins.then_inc(dv.chained(), 1), dv.e.wait_ge(dv.chain, dv.n))
            dv.e.wait_ge(*dv.filled("route"))
            ps = bank_of("route")
            lg = t("lg", 36)
            br = par(p1, A1, "b_route", 0, 36).unsqueeze(1).to_broadcast([P, NT, 36])
            tt(lg, ps[:, 0:144].rearrange("p (n e) -> p n e", n=NT), br, ALU.add).then_inc(dv.takes("route"), 1)
            dv.e.wait_ge(*dv.taken("route"))
            g = lg[:, :, 0:NG]
            x = lg[:, :, NG:36]
            bc = lambda n, e: t(n, 1).to_broadcast([P, NT, e])

            def first_max(src, mx, eq, idx, imin, oh, e, iota, second=0):
                st(V.tensor_reduce(t(mx, 1)[:, :, 0], src, AX.X, ALU.max))
                st(tt(t(eq, e), src, bc(mx, e), ALU.is_equal))
                it = cc(iota).unsqueeze(1).to_broadcast([P, NT, e])
                st(stt(t(idx, e), t(eq, e), -100.0, it, ALU.mult, ALU.add))
                first = RT(imin)[:, 4 * second:4 * second + 4]
                st(V.tensor_reduce(first, t(idx, e), AX.X, ALU.min))
                st(tt(t(oh, e), t(idx, e), first.unsqueeze(2).to_broadcast([P, NT, e]), ALU.is_equal))

            first_max(g, "gmax", "geq", "gidx", "gmin", "goh", NG, "iota4")
            tt(t("gsub", NG), g, bc("gmax", NG), ALU.subtract).then_inc(dv.tells("gsub"), 1)
            st(ts(RT("gpen"), RT("goh"), -NEG, NEG, ALU.mult, ALU.add))
            me4 = RT("me").rearrange("p (n g e) -> p (n g) e", n=NT, g=NG)
            st(V.tensor_copy(t("me", 32), x))
            pen = RT("gpen").unsqueeze(2).to_broadcast([P, NT * NG, EG])
            st(tt(me4, me4, pen, ALU.add))
            first_max(t("me", 32), "v1", "eq", "idx", "expert", "oh1", NE, "iota32")
            st(stt(RT("me"), RT("oh1"), 3 * NEG, RT("me"), ALU.mult, ALU.add))
            first_max(t("me", 32), "v2", "eq", "idx", "expert", "oh2", NE, "iota32", 1)
            tt(RT("vdiff"), RT("v2"), RT("v1"), ALU.subtract).then_inc(dv.tells("vdiff"), 1)
            tt(RT("mask"), RT("oh1"), RT("oh2"), ALU.add).then_inc(dv.tells("mask"), 1)
            dv.e.wait_ge(*dv.nth("gexp", 1))
            st(V.tensor_reduce(RT("gsum"), t("gexp", NG), AX.X, ALU.add))
            st(V.reciprocal(RT("pg"), RT("gsum")))
            dv.e.wait_ge(*dv.nth("e21", 1))
            w1_, w2_ = RT("weight")[:, 0:4], RT("weight")[:, 4:8]
            st(ts(w1_, RT("e21"), 1.0, None, ALU.add))
            st(V.reciprocal(w1_, w1_))
            st(tt(w1_, w1_, RT("pg"), ALU.mult))
            st(tt(w2_, w1_, RT("e21"), ALU.mult))
            dv.e.wait_ge(*dv.filled("pos"))
            ps = bank_of("pos")
            pos = ps[:, 0:NT * NE].rearrange("p (n e) -> p n e", n=NT)
            tt(t("idx", NE), t("oh1", NE), pos, ALU.mult).then_inc(dv.chained(), 1)
            tt(t("eq", NE), t("oh2", NE), pos, ALU.mult).then_inc(dv.chained(), 1)
            V.tensor_reduce(RT("busiest"), ps[:, NT * NE:(NT + 1) * NE], AX.X, ALU.max).then_inc(dv.takes("pos"), 1)
            dv.e.wait_ge(dv.chain, dv.n)
            dv.e.wait_ge(*dv.taken("pos"))
            V.tensor_reduce(RT("place")[:, 0:4], t("idx", NE), AX.X, ALU.add).then_inc(dv.chained(), 1)
            V.tensor_reduce(RT("place")[:, 4:8], t("eq", NE), AX.X, ALU.add).then_inc(dv.chained(), 1)
            st(ts(OVERFLOW, RT("busiest"), float(CAP), None, ALU.is_gt))
            st(ts(RT("over"), RT("place"), float(CAP), None, ALU.is_ge))
            st(stt(RT("row"), RT("expert"), float(ROWS // NE), RT("place"), ALU.mult, ALU.add))
            st(ts(RT("row"), RT("row"), 100.0 * (ROWS // NE), None, ALU.add))
            st(tt(RT("miss"), cc("spare_row"), RT("row"), ALU.subtract))
            st(tt(RT("miss"), RT("miss"), RT("over"), ALU.mult))
            tt(RT("to_row").bitcast(I32), RT("row"), RT("miss"), ALU.add).then_inc(dv.tells("to_row"), 1)
            tt(RT("over_weight"), RT("weight"), RT("over"), ALU.mult).then_inc(dv.chained(), 1)
            st(ts(RT("over"), RT("over"), -1.0, 1.0, ALU.mult, ALU.add))
            tt(RT("from_row").bitcast(I32), RT("row"), RT("over"), ALU.mult).then_inc(dv.tells("from_row"), 1)
            st(stt(RT("weight"), RT("weight"), 0.5, RT("over"), ALU.mult, ALU.mult))
            ow = lambda j: RT("over_weight")[:, 4 * j:4 * j + 4].unsqueeze(2).to_broadcast([P, NT, NE])
            st(tt(t("oh1", NE), t("oh1", NE), ow(0), ALU.mult))
            st(tt(t("oh2", NE), t("oh2", NE), ow(1), ALU.mult))
            tt(RT("comb"), RT("oh1"), RT("oh2"), ALU.add).then_inc(dv.tells("comb"), 1)
            rows_turned(dv, "pxt")

        OVERFLOW = RT("overflow").bitcast(I32)

        def rows_turned(dv, job):
            for x in range(2):
                dv.e.wait_ge(*dv.filled(f"{job}{x}"))
                ps = bank_of(f"{job}{x}")
                V.tensor_copy(XF[:, 4 * x:4 * x + 4, :], tiles4(ps[:, :])).then_inc(dv.takes(f"{job}{x}"), 1)

        def pe_M(pe):
            pe.sec = "M"
            pe.e.wait_ge(*pe.taken("pxt0"))
            pe.e.wait_ge(*pe.taken("pxt1"))
            with pe.e.Fori(0, NPAIR) as l:
                pe.l = l
                pe.e.wait_ge(*pe.emptied("xt0"))
                pe.e.wait_ge(*pe.emptied("xt1"))
                for x in range(2):
                    pe.e.wait_ge(*pe.emptied(f"mg{x}"))
                    ps = bank_of(f"mg{x}")
                    for s, at_ in enumerate((0, 128, 64, 192)):
                        pe.e.wait_ge(expert_slot_full[6 * x + s], 16 + 16 * l)
                        w = MRING[:, 6 * x + s, :].rearrange("p (k n) -> p k n", k=TPS)
                        for c in range(KD):
                            i = mm(ps[:, at_:at_ + 64], w[:, c, :], XF[:, c, 64 * x:64 * x + 64], start=c == 0, stop=c == KD - 1)
                    i.then_inc(pe.fills(f"mg{x}"), 1)
                pe.e.wait_ge(ev("rows_in"), 32 + 16 * l)
                turn_rows(pe, "xt")
                for x in range(2):
                    pe.e.wait_ge(*pe.emptied(f"md{x}"))
                pss = [bank_of(f"md{x}") for x in range(2)]
                for x in range(2):
                    pe.e.wait_ge(*pe.taken(f"mg{x}"))
                    for k in range(2):
                        s = 6 * x + 4 + k
                        pe.e.wait_ge(expert_slot_full[s], 16 + 16 * l)
                        for n in range(2):
                            i = mm(pss[n][64 * x:64 * x + 64, :], HIDM[:, x, 64 * k:64 * k + 64], MRING[:, s, 512 * n:512 * n + 512],
                                   start=k == 0, stop=k == 1)
                            if x == 1 and k == 1:
                                i.then_inc(pe.fills(f"md{n}"), 1)

        def act_M(sc):
            sc.sec = "M"
            with sc.e.Fori(0, NPAIR) as l:
                sc.l = l
                for x in range(2):
                    sc.e.wait_ge(*sc.filled(f"mg{x}"))
                    ps = bank_of(f"mg{x}")
                    act_(TGM[:, x, :], ps[:, 0:128], ACT.Tanh, scale=0.5).then_inc(sc.tells("m_tanh"), 1)
                for n in range(2):
                    sc.e.wait_ge(*sc.filled(f"md{n}"))
                    ps = bank_of(f"md{n}")
                    act_(YO[:, 512 * n:512 * n + 512], ps[:, :], ACT.Copy).then_inc(sc.takes(f"md{n}"), 1)
                for n in range(2):
                    sc.e.wait_ge(*sc.taken(f"md{n}"))
                sc.e.dma_start(sorted_y[bass.ds(l * P, P), :], YO).then_inc(ev("y_stored"), 16)
                sc.e.wait_ge(ev("y_stored"), 16 + 16 * l)
            sc.l = 0

        def dve_M(dv):
            dv.sec = "M"
            dv.restart()
            with dv.e.Fori(0, NPAIR) as l:
                dv.l = l
                for x in range(2):
                    dv.e.wait_ge(*dv.nth("m_tanh", x + 1))
                    dv.e.wait_ge(*dv.filled(f"mg{x}"))
                    ps = bank_of(f"mg{x}")
                    stt(HIDM[:, x, :], TGM[:, x, :], 1.0, ps[:, 0:128], ALU.add, ALU.mult).then_inc(dv.tells("m_silu"), 1)
                    dv.e.wait_ge(*dv.nth("m_silu", x + 1))
                    tt(HIDM[:, x, :], HIDM[:, x, :], ps[:, 128:256], ALU.mult).then_inc(dv.takes(f"mg{x}"), 1)
                rows_turned(dv, "xt")
            dv.l = 0

        def pool_all(po):
            e = po.e
            e.wait_ge(ev("rows_cleared"), 16)
            po.e.wait_ge(*po.nth("to_row", 1))
            for i_ in range(NT):
                po.e.wait_ge(*po.taken(f"ht{i_}_1"))
                po.e.wait_ge(*po.taken(f"ht{i_}_0"))
                for j in range(2):
                    rows = RT("to_row")[:, 4 * j + i_:4 * j + i_ + 1].bitcast(I32)
                    nc.gpsimd.indirect_dma_start(sorted_x, bass.IndirectOffsetOnAxis(ap=rows, axis=0), HT[:, i_, :], None).then_inc(ev("sorted"), 16)
            po.e.wait_ge(*po.nth("from_row", 1))
            e.wait_ge(ev("y_stored"), 16 * NPAIR)
            for i_ in range(NT):
                for j in range(2):
                    rows = RT("from_row")[:, 4 * j + i_:4 * j + i_ + 1].bitcast(I32)
                    nc.gpsimd.indirect_dma_start(YG[j][:, i_, :], None, sorted_y, bass.IndirectOffsetOnAxis(ap=rows, axis=0)).then_inc(ev(f"y_back{i_}"), 16)

        def pool_L(po):
            po.sec = "L"
            with po.e.Fori(0, L2) as l:
                po.l = l
                po.e.wait_ge(*po.nth("x_ready", 1))
                uses_ = 0
                for n, s in enumerate(SPLIT):
                    g = slot0["L"] + s
                    high, slot = W_high[:, n % 2, :], g % R
                    po.e.wait_ge(slot_full[slot], 16 * (g // R + 1 + l * (n_slots["L"] // R)))
                    if n >= 2:
                        job = last_user["L"][SPLIT[n - 2]]
                        if job == last_user["L"][SPLIT[n - 1]]:
                            uses_ += 1
                            po.e.wait_ge(*po.nth("w_used", uses_))
                        else:
                            po.e.wait_ge(*po.filled(job))
                    G.tensor_tensor(high, ring[:, slot, :], cc("ones")[:, 0:1].to_broadcast([P, TPS * P]), ALU.mult).then_inc(po.tells("w_high"), 1)
                    po.e.wait_ge(*po.nth("w_high", n + 1))
                    G.tensor_tensor(ring_low[:, slot, :], ring[:, slot, :], high.bitcast(F32), ALU.subtract).then_inc(po.tells("w_split"), 1)
            po.l = 0

        def dve_combine(dv):
            dv.sec = "B"
            for i_ in range(NT):
                dv.e.wait_ge(ev(f"y_back{i_}"), 32)
                a_, b_ = YG[0][:, i_, :], YG[1][:, i_, :]
                ts(a_, a_, RT("weight")[:, i_:i_ + 1], None, ALU.mult).then_inc(dv.chained(), 1); dv.e.wait_ge(dv.chain, dv.n)
                stt(a_, b_, RT("weight")[:, 4 + i_:5 + i_], a_, ALU.mult, ALU.add).then_inc(dv.tells("y_mixed"), 1)
            for m in range(8):
                dv.e.wait_ge(*dv.filled(f"gt{m}"))
                ps = bank_of(f"gt{m}")
                tt(X[:, m, :], X[:, m, :], ps[:, :], ALU.add).then_inc(dv.takes(f"gt{m}"), 1)
            dv.e.wait_ge(*dv.taken("gt7"))

        def pe_combine(pe):
            pe.sec, pe.l = "B", 0
            for i_ in range(NT):
                for m in range(8):
                    if i_ == 0:
                        pe.e.wait_ge(*pe.emptied(f"gt{m}"))
                    if m == 0:
                        pe.e.wait_ge(*pe.nth("y_mixed", i_ + 1))
                    i = nc.tensor.transpose(bank_of(f"gt{m}")[:, i_ * P:(i_ + 1) * P], YG[0][:, i_, m * P:(m + 1) * P], ident)
                    if i_ == NT - 1:
                        i.then_inc(pe.fills(f"gt{m}"), 1)

        FRING = arena[:, 0:RF * TPS * P].rearrange("p (r k n) -> p r k n", r=RF, k=TPS)
        HIDF, TGF, CBF = ch(6144, 2), ch(7168, 2), ch(8192)

        def dense(engine, body):
            engine.e.wait_ge(*engine.nth("comb", 1))
            n = engine.e.value_load(OVERFLOW[0:1, 0:1], min_val=0, max_val=1)
            with engine.e.If(n > 0):
                engine.sec = "F"
                body(engine)
                engine.sec, engine.l = "B", 0

        def pe_F(pe):
            for m in range(8):
                pe.e.wait_ge(*pe.taken(f"gt{m}"))
            with pe.e.Fori(0, NE) as l:
                pe.l = l
                for s, (x, k) in enumerate((("g", 0), ("u", 0), ("g", 1), ("u", 1))):
                    pe.e.wait_ge(dense_slot_full[s], 16 + 16 * l)
                    pe.e.wait_ge(*pe.emptied(f"f{x}{k}"))
                    ps = bank_of(f"f{x}{k}")
                    for c in range(KD):
                        i = mm(ps[:, :], FRING[:, s, c, :], H[:, c, :], start=c == 0, stop=c == KD - 1)
                    i.then_inc(pe.fills(f"f{x}{k}"), 1)
                for k in range(2):
                    pe.e.wait_ge(*pe.taken(f"fu{k}"))
                    pe.e.wait_ge(dense_slot_full[4 + k], 16 + 16 * l)
                for m in range(8):
                    pe.e.wait_ge(*pe.emptied(f"fd{m}"))
                    ps = bank_of(f"fd{m}")
                    for k in range(2):
                        i = mm(ps[:, :], FRING[:, 4 + k, m, :], HIDF[:, k, :], start=k == 0, stop=k == 1)
                    i.then_inc(pe.fills(f"fd{m}"), 1)
            pe.l = NE - 1
            for m in range(8):
                pe.e.wait_ge(*pe.taken(f"fd{m}"))

        def act_F(sc):
            with sc.e.Fori(0, NE) as l:
                sc.l = l
                for k in range(2):
                    sc.e.wait_ge(*sc.filled(f"fg{k}"))
                    ps = bank_of(f"fg{k}")
                    act_(TGF[:, k, :], ps[:, :], ACT.Tanh, scale=0.5).then_inc(sc.tells("f_tanh"), 1)

        def dve_F(dv):
            for b in range(8):
                V.memset(arena[:, 8704 + b:8705 + b], 0.0).then_inc(dense_bank_free[b], 1)
            with dv.e.Fori(0, NE) as l:
                dv.l = l
                dv.e.wait_ge(*dv.landed("comb_row"))
                for k in range(2):
                    dv.e.wait_ge(*dv.nth("f_tanh", k + 1))
                    dv.e.wait_ge(*dv.filled(f"fg{k}"))
                    ps = bank_of(f"fg{k}")
                    stt(HIDF[:, k, :], TGF[:, k, :], 1.0, ps[:, :], ALU.add, ALU.mult).then_inc(dv.takes(f"fg{k}"), 1)
                    dv.e.wait_ge(*dv.taken(f"fg{k}"))
                    tt(HIDF[:, k, :], HIDF[:, k, :], CBF[:, 0, :], ALU.mult).then_inc(dv.tells("f_comb"), 1)
                    dv.e.wait_ge(*dv.nth("f_comb", k + 1))
                    dv.e.wait_ge(*dv.filled(f"fu{k}"))
                    ps = bank_of(f"fu{k}")
                    tt(HIDF[:, k, :], HIDF[:, k, :], ps[:, :], ALU.mult).then_inc(dv.takes(f"fu{k}"), 1)
                for m in range(8):
                    dv.e.wait_ge(*dv.filled(f"fd{m}"))
                    ps = bank_of(f"fd{m}")
                    stt(X[:, m, :], ps[:, :], 0.5, X[:, m, :], ALU.mult, ALU.add).then_inc(dv.takes(f"fd{m}"), 1)
                dv.e.wait_ge(*dv.taken("fd7"))

        def sp_F(sp):
            e = sp.e
            for m in range(8):
                sp.e.wait_ge(*sp.filled(f"gt{m}"))
            e.wait_ge(ev("comb_stored"), 16)
            e.wait_ge(ev("bias_in"), 16 * DH)
            for s in range(RF):
                e.dma_start(FRING[:, s, :, :], stream[at0["M"] + s].rearrange("p (k n) -> p k n", k=TPS)).then_inc(dense_slot_full[s], 16)
            e.dma_start(CBF[:, 0, :], scratch[0:1, :].to_broadcast([P, T])).then_inc(ev("comb_row"), 16)
            with e.Fori(0, NE - 1) as l:
                sp.l = l
                for s in range(RF):
                    sp.e.wait_ge(*sp.filled(last_user["F"][s]))
                    if s == 5:
                        sp.e.wait_ge(*sp.taken("fu1"))
                        e.dma_start(CBF[:, 0, :], scratch[bass.ds(l + 1, 1), :].to_broadcast([P, T])).then_inc(ev("comb_row"), 16)
                    src = stream[bass.ds((l + 1) * RF + (at0["M"] + s), 1)].rearrange("a p n -> (a p) n")
                    e.dma_start(FRING[:, s, :, :], src.rearrange("p (k n) -> p k n", k=TPS)).then_inc(dense_slot_full[s], 16)

        c_ = lambda i, n=1: ch(512 * i, n)
        QL, KL, DAV, RQL, RKL, RV, RG, SCB = c_(0, 4), c_(4, 4), c_(8, 4), c_(12, 2), c_(14, 2), c_(16, 2), c_(18, 2), c_(20, 2)
        RVt = arena[:, 512 * 16:512 * 18].rearrange("p (n w) -> p n w", n=NT)
        BIASB = c_(22, 4)
        SCX = arena[:, 512 * 26:512 * 26 + 1032].rearrange("p (n w) -> p n w", n=2)
        ODA, ORET, OSC = c_(29, 4), c_(33, 2), c_(35, 2)
        PTL = [c_(37, 4), c_(41, 4)]
        SQL = c_(37, 8)
        SE = c_(45, 4)
        TL = c_(49, 6)
        YL = c_(0, 8)
        HL = c_(0, 22)
        GP = arena[:, 512 * 37:512 * 37 + 1032].rearrange("p (n w) -> p n w", n=2)
        dunits = [(h, i) for h in range(DH) for i in range(NT)]
        q2 = lambda name, i=0, n=1: par(p2, A2, name, i, n)

        RELB, ONEH, REPB, RROW = c_(0), c_(1), c_(2), arena[:, 512 * 4:512 * 4 + 4 * 640].rearrange("p (n w) -> p n w", n=4)

        def pe_B(pe):
            pe.sec, pe.l = "B", 0
            for h in range(DH):
                pe.e.wait_ge(*pe.emptied(f"bias{h}"))
                ps = bank_of(f"bias{h}")
                pe.e.wait_ge(*pe.nth("rel_rep", h + 1))
                mm(ps[:, :], REPB[0:32, 0, h * P:(h + 1) * P], ONEH[0:32, 0, :], start=True, stop=True).then_inc(pe.fills(f"bias{h}"), 1)

        def dve_B(dv):
            dv.sec = "B"
            dv.e.wait_ge(ev("rel_in"), 32)
            for h in range(DH):
                ts(REPB[0:32, 0, h * P:(h + 1) * P], cc("ones", slice(0, 32)), RELB[0:32, 0, h:h + 1], None, ALU.mult).then_inc(dv.tells("rel_rep"), 1)
            for h in range(DH):
                V.memset(RROW[:, h, 512:640], NEG).then_inc(dv.tells("bias_pad"), 1)
            for h in range(DH):
                dv.e.wait_ge(*dv.filled(f"bias{h}"))
                ps = bank_of(f"bias{h}")
                V.tensor_copy(RROW[:, h, 0:512], ps[:, :]).then_inc(dv.takes(f"bias{h}"), 1)

        def act_B(sc):
            sc.sec = "B"
            e = sc.e
            sc.e.wait_ge(*sc.filled("md1"))
            e.dma_start(RELB[0:32, 0, 0:DH], ts_["rel_bias"]).then_inc(ev("rel_in"), 16)
            e.dma_start(ONEH[0:32, 0, :], ts_["onehot"]).then_inc(ev("rel_in"), 16)
            sc.e.wait_ge(*sc.nth("bias_pad", DH))
            for h in range(DH):
                sc.e.wait_ge(*sc.taken(f"bias{h}"))
                e.dma_start(bias_scratch[h].rearrange("(p w) -> p w", w=640), RROW[:, h, :]).then_inc(ev("bias_stored"), 16)
            e.wait_ge(ev("bias_stored"), 16 * DH)
            for h in range(DH):
                skew = bias_scratch[h, 127:127 + P * 639].rearrange("(p w) -> p w", w=639)[:, 0:512]
                e.dma_start(BIASB[:, h, :], skew).then_inc(ev("bias_in"), 16)

        def branch_rhs(b):
            return [[(k, ODA[:, k, :]) for k in range(4)], [(4 + k, ORET[:, k, :]) for k in range(2)],
                    [(6 + k, OSC[:, k, :]) for k in range(2)]][b]

        def pe_L(pe):
            pe.sec = "L"
            e = pe.e
            with e.Fori(0, L2) as l:
                pe.l = l
                slot = iter(range(n_slots["L"]))
                W_ = lambda: weights(pe, next(slot), "L")

                def split_weights(per):
                    s = next(slot)
                    n = SPLIT.index(s)
                    pe.e.wait_ge(*pe.nth("w_split", n + 1))
                    return (W_high[:, n % 2, :].rearrange("p (k n) -> p k n", k=per),
                            ring_low[:, (slot0["L"] + s) % R, :].rearrange("p (k n) -> p k n", k=per))

                pe.e.wait_ge(*pe.emptied("ssq3"))
                ps = bank_of("ssq3")
                for c in range(KD):
                    pe.e.wait_ge(*pe.nth("Lsq", c + 1))
                    i = mm(ps[:, :], cc("ones"), SQL[:, c, :], start=c == 0, stop=c == KD - 1)
                i.then_inc(pe.fills("ssq3"), 1)
                for x, w_, per in (("dav", 512, 2), ("rv", 256, 4)):
                    for i_ in range(NT):
                        pe.e.wait_ge(*pe.emptied(f"{x}{i_}"))
                    pss = [bank_of(f"{x}{i_}") for i_ in range(NT)]
                    for k in range(KD):
                        if k % per == 0:
                            wh, wl = split_weights(per)
                        if x == "dav":
                            pe.e.wait_ge(*pe.nth("Lh", k + 1))
                        for i_ in range(NT):
                            tk = slice(i_ * P, (i_ + 1) * P)
                            mm(pss[i_][:, 0:w_], H_high[:, k, tk], wh[:, k % per, :], start=k == 0, stop=False)
                            mm(pss[i_][:, 0:w_], H_high[:, k, tk], wl[:, k % per, :], start=False, stop=False)
                            i = mm(pss[i_][:, 0:w_], H_low[:, k, tk], wh[:, k % per, :], start=False, stop=k == KD - 1)
                            if k == KD - 1:
                                i.then_inc(pe.fills(f"{x}{i_}"), 1)
                        if k % per == per - 1 and k < KD - 1:
                            i.then_inc(pe.tells("w_used"), 1)

                def chunk(job, first=False):
                    wh, wl = split_weights(TPS)
                    pe.e.wait_ge(*pe.emptied(job))
                    steps(job, wh, wl, range(KD), first)

                def steps(job, wh, wl, ks, first=False):
                    ps = bank_of(job)
                    for k in ks:
                        if first:
                            pe.e.wait_ge(*pe.nth("Lh", KD + k + 1))
                        mm(ps[:, :], wh[:, k, :], H_high[:, k, :], start=k == 0, stop=False)
                        mm(ps[:, :], wh[:, k, :], H_low[:, k, :], start=False, stop=False)
                        i = mm(ps[:, :], wl[:, k, :], H_high[:, k, :], start=False, stop=k == KD - 1)
                    if ks[-1] == KD - 1:
                        i.then_inc(pe.fills(job), 1)

                for h in range(DH):
                    chunk(f"dq{h}")
                    chunk(f"dk{h}")
                for h in range(DH):
                    for j, x in enumerate("qk"):
                        pe.e.wait_ge(*pe.emptied(f"d{x}ss{h}"))
                        ps = bank_of(f"d{x}ss{h}")
                        pe.e.wait_ge(*pe.nth("Lqsq", 2 * h + j + 1))
                        mm(ps[:, :], cc("blk64"), SQL[:, 2 * h + j, :], start=True, stop=True).then_inc(pe.fills(f"d{x}ss{h}"), 1)
                def turned_halves(x, c):
                    pe.e.wait_ge(*pe.emptied(f"{x}p{c}"))
                    ps = bank_of(f"{x}p{c}")
                    pe.e.wait_ge(*pe.taken(f"{x}{c}"))
                    src = RQL if x == "rq" else RKL
                    mm(ps[:, :], cc("perm64"), src[:, c, :], start=True, stop=True).then_inc(pe.fills(f"{x}p{c}"), 1)

                for x in ("rq", "rk"):
                    for c in range(2):
                        chunk(f"{x}{c}")
                def turn(n):
                    h, i_ = dunits[n]
                    pe.e.wait_ge(*pe.emptied(f"dt{h}_{i_}"))
                    ps = bank_of(f"dt{h}_{i_}")
                    pe.e.wait_ge(*pe.nth("Lprob", n + 1))
                    for j in range(i_ + 1):
                        i = nc.tensor.transpose(ps[:, j * P:(j + 1) * P], SE[:, 2 * (n % 2), j * P:(j + 1) * P], ident)
                    i.then_inc(pe.fills(f"dt{h}_{i_}"), 1)
                    if i_ == NT - 1:
                        pe.e.wait_ge(*pe.emptied(f"do{h}"))
                        ps = bank_of(f"do{h}")
                        pe.e.wait_ge(*pe.taken(f"dt{h}_{i_}"))
                        for j in range(NT):
                            i = mm(ps[:, j * P:T], DAV[:, j, h * P:(h + 1) * P], PTL[h % 2][:, j, j * P:T], start=j == 0, stop=j == NT - 1)
                        i.then_inc(pe.fills(f"do{h}"), 1)

                for n, (h, i_) in enumerate(dunits):
                    for m in range(2):
                        pe.e.wait_ge(*pe.emptied(f"ds{h}_{i_}_{m}"))
                        ps = bank_of(f"ds{h}_{i_}_{m}")
                        if i_ == 0 and m == 0:
                            pe.e.wait_ge(*pe.nth("Lqkn", 2 * h + 2))
                        hp = slice(64 * m, 64 * m + 64)
                        i = mm(ps[:, 0:(i_ + 1) * P], QL[hp, h, i_ * P:(i_ + 1) * P], KL[hp, h, 0:(i_ + 1) * P], start=True, stop=True)
                        i.then_inc(pe.fills(f"ds{h}_{i_}_{m}"), 1)
                    job = HALVES[n // 2]
                    if n % 2 == 0:
                        wh, wl = split_weights(TPS)
                        pe.e.wait_ge(*pe.emptied(job))
                        steps(job, wh, wl, range(0, KD // 2))
                    else:
                        steps(job, wh, wl, range(KD // 2, KD))
                    if n:
                        turn(n - 1)
                    for job in AMID.get(n, []):
                        turned_halves(job[0:2], int(job[3]))
                turn(len(dunits) - 1)
                for h in range(RH):
                    hp, c = slice(64 * (h % 2), 64 * (h % 2) + 64), h // 2
                    for j in range(NT):
                        pe.e.wait_ge(*pe.emptied(f"rs{h}_{j}"))
                        ps = bank_of(f"rs{h}_{j}")
                        if h == 0 and j == 0:
                            pe.e.wait_ge(*pe.nth("Lrot", 4))
                        n = T - j * P
                        mm(ps[:, 0:n], RKL[hp, c, j * P:(j + 1) * P], RQL[hp, c, j * P:T], start=True, stop=True).then_inc(pe.fills(f"rs{h}_{j}"), 1)
                    if h % 2:
                        pe.e.wait_ge(*pe.emptied(f"ro{c}"))
                        ps = bank_of(f"ro{c}")
                        for hh in (h - 1, h):
                            for j in range(NT):
                                pe.e.wait_ge(*pe.taken(f"rs{hh}_{j}"))
                                sd = (SE if hh % 2 == 0 else TL)[:, j, 0:T - j * P]
                                i = mm(ps[64 * (hh % 2):64 * (hh % 2) + 64, j * P:T], RVt[:, j, hh * 64:hh * 64 + 64], sd,
                                       start=j == 0, stop=j == NT - 1)
                        i.then_inc(pe.fills(f"ro{c}"), 1)
                for c in range(2):
                    pe.e.wait_ge(*pe.emptied(f"ross{c}"))
                    ps = bank_of(f"ross{c}")
                    pe.e.wait_ge(*pe.nth("Lrsq", c + 1))
                    mm(ps[:, :], cc("blk64"), TL[:, 4 + c, :], start=True, stop=True).then_inc(pe.fills(f"ross{c}"), 1)

                for h in range(DH):
                    pe.e.wait_ge(*pe.emptied(f"doss{h}"))
                    ps = bank_of(f"doss{h}")
                    pe.e.wait_ge(*pe.nth("Losq", h + 1))
                    mm(ps[:, :], cc("ones"), TL[:, h, :], start=True, stop=True).then_inc(pe.fills(f"doss{h}"), 1)
                for b in range(3):
                    chunk(f"gate{b}_0")
                for m in range(8):
                    for b in range(3):
                        if m < 7:
                            chunk(f"gate{b}_{m + 1}")
                    w = W_()
                    for b in range(3):
                        pe.e.wait_ge(*pe.emptied(f"br{b}_{m}"))
                        ps = bank_of(f"br{b}_{m}")
                        if m == 0 and b == 0:
                            pe.e.wait_ge(*pe.nth("Loda", 4))
                        if m == 0 and b == 1:
                            pe.e.wait_ge(*pe.nth("Loret", 2))
                        if m == 0 and b == 2:
                            pe.e.wait_ge(*pe.nth("Losc", 2))
                        rs = branch_rhs(b)
                        for k, r in rs:
                            i = mm(ps[:, :], w[:, k, :], r, start=k == rs[0][0], stop=k == rs[-1][0])
                        i.then_inc(pe.fills(f"br{b}_{m}"), 1)
                for m in range(8):
                    w = W_()
                    pe.e.wait_ge(*pe.emptied(f"wout{m}"))
                    ps = bank_of(f"wout{m}")
                    for k in range(KD):
                        if m == 0:
                            pe.e.wait_ge(*pe.nth("Ly", k + 1))
                        i = mm(ps[:, :], w[:, k, :], YL[:, k, :], start=k == 0, stop=k == KD - 1)
                    i.then_inc(pe.fills(f"wout{m}"), 1)
                pe.e.wait_ge(*pe.emptied("ssq4"))
                ps = bank_of("ssq4")
                for c in range(KD):
                    pe.e.wait_ge(*pe.nth("Lsq", KD + c + 1))
                    i = mm(ps[:, :], cc("ones"), SQL[:, c, :], start=c == 0, stop=c == KD - 1)
                i.then_inc(pe.fills("ssq4"), 1)
                for k in range(KF):
                    chunk(f"ffg{k}", first=k == 0)
                    chunk(f"ffu{k}")
                w = None
                for m in range(8):
                    pe.e.wait_ge(*pe.emptied(f"fo{m}"))
                    ps = bank_of(f"fo{m}")
                    for k in range(KF):
                        t_ = m * KF + k
                        if t_ % 8 == 0:
                            w = W_()
                        if m == 0:
                            pe.e.wait_ge(*pe.taken(f"ffu{k}"))
                        i = mm(ps[:, :], w[:, t_ % 8, :], HL[:, k, :], start=k == 0, stop=k == KF - 1)
                    i.then_inc(pe.fills(f"fo{m}"), 1)

        def act_L(sc):
            sc.sec = "L"
            e = sc.e
            sc.restart()
            with e.Fori(0, L2) as l:
                sc.l = l
                sc.e.wait_ge(*sc.nth("x_ready", 1))
                e.dma_start(p2[:, :], ts_["p2"][bass.ds(l, 1)].rearrange("a p n -> (a p) n")).then_inc(ev("p2_in"), 16)
                for c in range(KD):
                    act_(SQL[:, c, :], X[:, c, :], ACT.Square).then_inc(sc.tells("Lsq"), 1)
                sc.e.wait_ge(*sc.filled("ssq3"))
                ps = bank_of("ssq3")
                act_(TL[:, 0, :], ps[:, :], ACT.Sqrt, EPS, 1.0 / D).then_inc(sc.takes("ssq3"), 1)
                for i_ in range(NT):
                    sc.e.wait_ge(*sc.filled(f"dav{i_}"))
                    ps = bank_of(f"dav{i_}")
                    act_(DAV[:, i_, :], ps[:, :], ACT.Copy).then_inc(sc.takes(f"dav{i_}"), 1)
                for i_ in range(NT):
                    sc.e.wait_ge(*sc.filled(f"rv{i_}"))
                    ps = bank_of(f"rv{i_}")
                    act_(RVt[:, i_, :], ps[:, 0:256], ACT.Copy).then_inc(sc.takes(f"rv{i_}"), 1)
                for h in range(DH):
                    for j, x in enumerate("qk"):
                        sc.e.wait_ge(*sc.taken(f"d{x}{h}"))
                        act_(SQL[:, 2 * h + j, :], (QL if x == "q" else KL)[:, h, :], ACT.Square).then_inc(sc.tells("Lqsq"), 1)
                for h in range(DH):
                    for j, x in enumerate("qk"):
                        sc.e.wait_ge(*sc.filled(f"d{x}ss{h}"))
                        ps = bank_of(f"d{x}ss{h}")
                        act_(SQL[:, 2 * h + j, :], ps[:, :], ACT.Sqrt, EPS, 1.0 / DQ).then_inc(sc.takes(f"d{x}ss{h}"), 1)
                sc.e.wait_ge(*sc.nth("Llam", 1))
                act_(small[:, 24:26], small[:, 22:24], ACT.Exp).then_inc(sc.tells("Llexp"), 1)

                def half_done(job):
                    c = int(job[3])
                    if job[0:3] == "rgt":
                        sc.e.wait_ge(*sc.filled(job))
                        act_(TL[:, 1 + c, :], bank_of(job)[:, :], ACT.Tanh, scale=0.5).then_inc(sc.tells("Lrgt"), 1)
                    if job[0:3] in ("scb", "scc"):
                        sc.e.wait_ge(*sc.filled(job))
                        o = SCB[:, c, :] if job[0:3] == "scb" else TL[:, 3 + c, :]
                        act_(o, bank_of(job)[:, :], ACT.Copy).then_inc(sc.takes(job), 1)

                for n, (h, i_) in enumerate(dunits):
                    for m in range(2):
                        sc.e.wait_ge(*sc.nth("Lmax", 2 * n + m + 1))
                        s = SE[:, 2 * (n % 2) + m, 0:(i_ + 1) * P]
                        c0 = 2 * (n % 2) + m
                        act_(s, s, ACT.Exp, bias=small[:, 36 + c0:37 + c0], accum=small[:, 40 + c0:41 + c0]).then_inc(sc.tells("Lexp"), 1)
                    if n:
                        turned_L(sc, n - 1)
                    if n % 2:
                        half_done(HALVES[n // 2])
                turned_L(sc, len(dunits) - 1)
                for c in range(2):
                    sc.e.wait_ge(*sc.taken(f"ro{c}"))
                    act_(TL[:, 4 + c, :], ORET[:, c, :], ACT.Square).then_inc(sc.tells("Lrsq"), 1)
                for c in range(2):
                    sc.e.wait_ge(*sc.filled(f"ross{c}"))
                    ps = bank_of(f"ross{c}")
                    act_(TL[:, 4 + c, :], ps[:, :], ACT.Sqrt, EPS, 1.0 / 64).then_inc(sc.takes(f"ross{c}"), 1)
                for h in range(DH):
                    sc.e.wait_ge(*sc.taken(f"do{h}"))
                    act_(TL[:, h, :], ODA[:, h, :], ACT.Square).then_inc(sc.tells("Losq"), 1)
                for h in range(DH):
                    sc.e.wait_ge(*sc.filled(f"doss{h}"))
                    ps = bank_of(f"doss{h}")
                    act_(TL[:, h, :], ps[:, :], ACT.Sqrt, EPS, 1.0 / DV).then_inc(sc.takes(f"doss{h}"), 1)
                for m in range(8):
                    for b in range(3):
                        sc.e.wait_ge(*sc.filled(f"gate{b}_{m}"))
                        ps = bank_of(f"gate{b}_{m}")
                        if m == 0 and b == 0:
                            sc.e.wait_ge(*sc.nth("Loda", 4))
                            sc.e.wait_ge(*sc.nth("Lbgate", 1))
                        if m >= 2:
                            sc.e.wait_ge(*sc.nth("Ly", m - 1))
                        act_(TL[:, b + 3 * (m % 2), :], ps[:, :], ACT.Tanh, bias=arena_small("bgh", b * 8 + m), scale=0.5).then_inc(sc.takes(f"gate{b}_{m}"), 1)
                for c in range(KD):
                    sc.e.wait_ge(*sc.taken(f"wout{c}"))
                    act_(SQL[:, c, :], X[:, c, :], ACT.Square).then_inc(sc.tells("Lsq"), 1)
                sc.e.wait_ge(*sc.filled("ssq4"))
                ps = bank_of("ssq4")
                act_(TL[:, 0, :], ps[:, :], ACT.Sqrt, EPS, 1.0 / D).then_inc(sc.takes("ssq4"), 1)
                for k in range(KF):
                    sc.e.wait_ge(*sc.filled(f"ffg{k}"))
                    ps = bank_of(f"ffg{k}")
                    if k == 0:
                        sc.e.wait_ge(*sc.nth("Lh", 2 * KD))
                        sc.e.wait_ge(*sc.nth("Lgpad", 1))
                    if k >= 2:
                        sc.e.wait_ge(*sc.taken(f"ffu{k - 2}"))
                    act_(GP[:, k % 2, 2:514], ps[:, :], ACT.Copy).then_inc(sc.takes(f"ffg{k}"), 1)
                    sc.e.wait_ge(*sc.taken(f"ffg{k}"))
                    act_(TL[:, k % 2, :], GP[:, k % 2, 2:514], ACT.Identity, bias=q2("fcb", k), scale=q2("fcw", 2 * KF + k)).then_inc(sc.tells("Lfc"), 1)
                    sc.e.wait_ge(*sc.nth("Lconv", k + 1))
                    act_(TL[:, 2 + k % 2, :], TL[:, k % 2, :], ACT.Tanh, scale=0.5).then_inc(sc.tells("Lft"), 1)
            sc.l = 0

        def arena_small(name, i, n=1):
            return arena[:, 55 * 512 + i:55 * 512 + i + n]

        def turned_L(sc, n):
            h, i_ = dunits[n]
            sc.e.wait_ge(*sc.filled(f"dt{h}_{i_}"))
            ps = bank_of(f"dt{h}_{i_}")
            if i_ == 0 and h >= 2:
                sc.e.wait_ge(*sc.filled(f"do{h - 2}"))
            act_(PTL[h % 2][:, 0:i_ + 1, i_ * P:(i_ + 1) * P],
                         ps[:, 0:(i_ + 1) * P].rearrange("p (n w) -> p n w", n=i_ + 1), ACT.Copy).then_inc(sc.takes(f"dt{h}_{i_}"), 1)

        def dve_L(dv):
            dv.sec = "L"
            e = dv.e
            dv.restart()
            e.wait_ge(ev("bias_in"), 16 * DH)
            with e.Fori(0, L2) as l:
                dv.l = l
                dv.e.wait_ge(*dv.landed("p2_in"))
                norm_split(dv, "ssq3", lambda c: q2("g_mix", c))
                st = lambda ins: (ins.then_inc(dv.chained(), 1), dv.e.wait_ge(dv.chain, dv.n))
                lm = q2("lam", 0, 256).rearrange("p (a b d) -> p a b d", a=2, b=2)
                dv.e.wait_ge(*dv.nth("Lh", KD))
                st(tt(TL[:, 5, 0:128].rearrange("p (a d) -> p a d", a=2), lm[:, :, 0, :], lm[:, :, 1, :], ALU.mult))
                V.tensor_reduce(small[:, 22:24], TL[:, 5, 0:128].rearrange("p (a d) -> p a d", a=2), AX.X, ALU.add).then_inc(dv.tells("Llam"), 1)
                ts(small[:, 26:27], q2("gq"), DQ ** -0.5, None, ALU.mult).then_inc(dv.chained(), 1)
                ts(small[:, 27:28], q2("retg"), 0.5, None, ALU.mult).then_inc(dv.chained(), 1)
                tt(small[:, 28:29], q2("subln"), q2("one_minus"), ALU.mult).then_inc(dv.chained(), 1)
                ts(arena_small("bgh", 0, 24), q2("b_gate", 0, 24), 0.5, None, ALU.mult).then_inc(dv.tells("Lbgate"), 1)
                V.memset(SCX[:, :, 0:2], 0.0).then_inc(dv.chained(), 1)
                for h in range(DH):
                    for x, o in (("q", QL), ("k", KL)):
                        dv.e.wait_ge(*dv.filled(f"d{x}{h}"))
                        ps = bank_of(f"d{x}{h}")
                        V.tensor_copy(o[:, h, :], ps[:, :]).then_inc(dv.takes(f"d{x}{h}"), 1)
                def qk_norm(h):
                    for j, (x, o, g) in enumerate((("q", QL, small[:, 26:27]), ("k", KL, q2("gk")))):
                        dv.e.wait_ge(*dv.taken(f"d{x}ss{h}"))
                        r = SQL[:, 2 * h + j, :]
                        st(V.reciprocal(r, r))
                        stt(o[:, h, :], o[:, h, :], g, r, ALU.mult, ALU.mult).then_inc(dv.tells("Lqkn"), 1)

                qk_norm(0)
                for x, o in (("rq", RQL), ("rk", RKL)):
                    for c in range(2):
                        dv.e.wait_ge(*dv.filled(f"{x}{c}"))
                        ps = bank_of(f"{x}{c}")
                        V.tensor_copy(o[:, c, :], ps[:, :]).then_inc(dv.takes(f"{x}{c}"), 1)
                qk_norm(1)

                def middle(job):
                    c = int(job[-1])
                    if job[2] == "p":
                        x, o, t = job[0:2], RQL if job[1] == "q" else RKL, TL[:, 5, :]
                        dv.e.wait_ge(*dv.filled(job))
                        dv.e.wait_ge(dv.chain, dv.n)
                        tt(t, bank_of(job)[:, :], cc("ret_sin"), ALU.mult).then_inc(dv.takes(job), 1)
                        st(tt(o[:, c, :], o[:, c, :], cc("ret_cos"), ALU.mult))
                        dv.e.wait_ge(*dv.taken(job))
                        tt(o[:, c, :], o[:, c, :], t, ALU.add).then_inc(dv.tells("Lrot"), 1)
                        dv.e.wait_ge(*dv.nth("Lrot", 2 * (x == "rk") + c + 1))
                    elif job[0:3] == "scx":
                        dv.e.wait_ge(*dv.taken(f"scc{c}"))
                        dv.e.wait_ge(*dv.filled(job))
                        tt(SCX[:, c, 2:514], TL[:, 3 + c, :], bank_of(job)[:, :], ALU.mult).then_inc(dv.takes(job), 1)
                        o = OSC[:, c, :]
                        dv.e.wait_ge(*dv.taken(job))
                        st(ts(o, SCX[:, c, 2:514], q2("scw", 4 + c), q2("scb", c), ALU.mult, ALU.add))
                        st(stt(o, SCX[:, c, 1:513], q2("scw", 2 + c), o, ALU.mult, ALU.add))
                        st(stt(o, SCX[:, c, 0:512], q2("scw", c), o, ALU.mult, ALU.add))
                        dv.e.wait_ge(*dv.taken(f"scb{c}"))
                        tt(o, o, SCB[:, c, :], ALU.mult).then_inc(dv.tells("Losc"), 1)
                    elif job[0:3] == "rgt":
                        dv.e.wait_ge(*dv.nth("Lrgt", c + 1))
                        dv.e.wait_ge(*dv.filled(job))
                        stt(RG[:, c, :], TL[:, 1 + c, :], 1.0, bank_of(job)[:, :], ALU.add, ALU.mult).then_inc(dv.takes(job), 1)

                dv.e.wait_ge(*dv.nth("Llexp", 1))
                st(tt(small[:, 29:30], small[:, 25:26], small[:, 24:25], ALU.subtract))
                st(tt(small[:, 29:30], small[:, 29:30], q2("lam_init"), ALU.subtract))
                def prob(n):
                    h, i_ = dunits[n]
                    w = (i_ + 1) * P
                    b0 = 2 * (n % 2)
                    dv.e.wait_ge(*dv.nth("Lexp", 2 * n + 2))
                    r = small[:, 44 + b0:46 + b0]
                    st(V.reciprocal(r, small[:, 40 + b0:42 + b0]))
                    tt(r[:, 1:2], r[:, 1:2], small[:, 29:30], ALU.mult).then_inc(dv.chained(), 1)
                    st(ts(SE[:, b0, 0:w], SE[:, b0, 0:w], r[:, 0:1], None, ALU.mult))
                    stt(SE[:, b0, 0:w], SE[:, b0 + 1, 0:w], r[:, 1:2], SE[:, b0, 0:w], ALU.mult, ALU.add).then_inc(dv.tells("Lprob"), 1)
                    if i_ == 1 and h:
                        dv.e.wait_ge(*dv.filled(f"do{h - 1}"))
                        ps = bank_of(f"do{h - 1}")
                        V.tensor_copy(ODA[:, h - 1, :], ps[:, :]).then_inc(dv.takes(f"do{h - 1}"), 1)

                for n, (h, i_) in enumerate(dunits):
                    w = (i_ + 1) * P
                    for m in range(2):
                        b0 = 2 * (n % 2) + m
                        dv.e.wait_ge(*dv.filled(f"ds{h}_{i_}_{m}"))
                        ps = bank_of(f"ds{h}_{i_}_{m}")
                        if n >= 2 and m == 0:
                            dv.e.wait_ge(*dv.filled("dt%d_%d" % dunits[n - 2]))
                            dv.e.wait_ge(*dv.nth("Lprob", n - 1))
                        if n < 2 and m == 0:
                            dv.e.wait_ge(*dv.nth("Llexp", 1))
                        mx = small[:, 32 + b0:33 + b0]
                        V.memset(small[0:1, 58:59], 0.0)
                        V.tensor_tensor_reduce(SE[:, b0, 0:w], ps[:, 0:w], BIASB[:, h, 512 - w:512], 1.0, 3 * NEG,
                                                       ALU.add, ALU.max, mx).then_inc(dv.takes(f"ds{h}_{i_}_{m}"), 1)
                        dv.e.wait_ge(*dv.taken(f"ds{h}_{i_}_{m}"))
                        ts(small[:, 36 + b0:37 + b0], mx, -1.0, None, ALU.mult).then_inc(dv.tells("Lmax"), 1)
                    if n:
                        prob(n - 1)
                        for job in AMID.get(n - 1, []):
                            middle(job)
                    if n % 2:
                        middle(HALVES[n // 2])
                    if n in (1, 2):
                        qk_norm(n + 1)
                prob(len(dunits) - 1)
                dv.e.wait_ge(*dv.filled(f"do{DH - 1}"))
                ps = bank_of(f"do{DH - 1}")
                V.tensor_copy(ODA[:, DH - 1, :], ps[:, :]).then_inc(dv.takes(f"do{DH - 1}"), 1)
                for h in range(RH):
                    for j in range(NT):
                        dv.e.wait_ge(*dv.filled(f"rs{h}_{j}"))
                        ps = bank_of(f"rs{h}_{j}")
                        if h == 0 and j == 0:
                            dv.e.wait_ge(*dv.filled(f"do{DH - 1}"))
                        if h >= 2 and j == 0:
                            dv.e.wait_ge(*dv.filled("ro0"))
                        n = T - j * P
                        dec = cc("ret_decay")[:, h * 512:h * 512 + n]
                        stt((SE if h % 2 == 0 else TL)[:, j, 0:n], ps[:, 0:n], RQ ** -0.5, dec, ALU.mult, ALU.mult).then_inc(dv.takes(f"rs{h}_{j}"), 1)
                    if h % 2:
                        dv.e.wait_ge(*dv.filled(f"ro{h // 2}"))
                        ps = bank_of(f"ro{h // 2}")
                        V.tensor_copy(ORET[:, h // 2, :], ps[:, :]).then_inc(dv.takes(f"ro{h // 2}"), 1)
                for c in range(2):
                    dv.e.wait_ge(*dv.taken(f"ross{c}"))
                    r = TL[:, 4 + c, :]
                    st(V.reciprocal(r, r))
                    st(stt(ORET[:, c, :], ORET[:, c, :], small[:, 27:28], r, ALU.mult, ALU.mult))
                    dv.e.wait_ge(*dv.taken(f"rgt{c}"))
                    tt(ORET[:, c, :], ORET[:, c, :], RG[:, c, :], ALU.mult).then_inc(dv.tells("Loret"), 1)

                for h in range(DH):
                    dv.e.wait_ge(*dv.taken(f"doss{h}"))
                    r = TL[:, h, :]
                    st(V.reciprocal(r, r))
                    stt(ODA[:, h, :], ODA[:, h, :], small[:, 28:29], r, ALU.mult, ALU.mult).then_inc(dv.tells("Loda"), 1)
                for m in range(8):
                    t = [TL[:, b + 3 * (m % 2), :] for b in range(3)]
                    for b in range(3):
                        dv.e.wait_ge(*dv.taken(f"gate{b}_{m}"))
                        dv.e.wait_ge(*dv.filled(f"br{b}_{m}"))
                        ps = bank_of(f"br{b}_{m}")
                        stt(t[b], t[b], 1.0, ps[:, :], ALU.add, ALU.mult).then_inc(dv.takes(f"br{b}_{m}"), 1)
                    dv.e.wait_ge(*dv.taken(f"br1_{m}"))
                    st(tt(t[0], t[0], t[1], ALU.add))
                    dv.e.wait_ge(*dv.taken(f"br2_{m}"))
                    tt(YL[:, m, :], t[0], t[2], ALU.add).then_inc(dv.tells("Ly"), 1)
                for m in range(8):
                    dv.e.wait_ge(*dv.filled(f"wout{m}"))
                    ps = bank_of(f"wout{m}")
                    stt(X[:, m, :], ps[:, :], 0.5, X[:, m, :], ALU.mult, ALU.add).then_inc(dv.takes(f"wout{m}"), 1)
                dv.e.wait_ge(*dv.taken("wout7"))
                norm_split(dv, "ssq4", lambda c: q2("g_ffn", c))
                V.memset(GP[:, :, 0:2], 0.0).then_inc(dv.tells("Lgpad"), 1)
                for k in range(KF):
                    c = TL[:, k % 2, :]
                    g = GP[:, k % 2, :]
                    dv.e.wait_ge(*dv.nth("Lfc", k + 1))
                    st(stt(c, g[:, 1:513], q2("fcw", KF + k), c, ALU.mult, ALU.add))
                    stt(c, g[:, 0:512], q2("fcw", k), c, ALU.mult, ALU.add).then_inc(dv.tells("Lconv"), 1)
                    dv.e.wait_ge(*dv.nth("Lft", k + 1))
                    dv.e.wait_ge(*dv.nth("Lconv", k + 1))
                    st(stt(HL[:, k, :], TL[:, 2 + k % 2, :], 1.0, c, ALU.add, ALU.mult))
                    dv.e.wait_ge(*dv.filled(f"ffu{k}"))
                    ps = bank_of(f"ffu{k}")
                    tt(HL[:, k, :], HL[:, k, :], ps[:, :], ALU.mult).then_inc(dv.takes(f"ffu{k}"), 1)
                for m in range(8):
                    dv.e.wait_ge(*dv.filled(f"fo{m}"))
                    ps = bank_of(f"fo{m}")
                    stt(X[:, m, :], ps[:, :], 0.5, X[:, m, :], ALU.mult, ALU.add).then_inc(dv.takes(f"fo{m}"), 1)
                dv.e.wait_ge(*dv.taken("fo7"))
                V.memset(small[:, 59:60], 0.0).then_inc(dv.tells("x_ready"), 1)
                dv.restart()
            dv.l = 0

        stream = ts_["stream"]
        EXPERT_SLOTS = (0, 1, 2, 3, 6, 7, 8, 9, 4, 5, 10, 11)

        def sp_all(sp):
            e = sp.e
            e.dma_start(X[:, :, :], ts_["x"]).then_inc(ev("x_in"), 16)
            e.dma_start(cst[:, :], ts_["consts"]).then_inc(ev("consts_in"), 16)
            e.dma_start(early[:, 0:nCE + nA1], ts_["p1"]).then_inc(ev("p1_in"), 16)

            def fill(s, sec, at_=None):
                r = (slot0[sec] + s) % R
                src = stream[at0[sec] + s] if at_ is None else \
                    stream[bass.ds(at_ + (at0[sec] + s), 1)].rearrange("a p n -> (a p) n")
                e.dma_start(ring[:, r, :], src).then_inc(slot_full[r], 16)

            def fill_expert(s, at_=None):
                src = stream[at0["M"] + s] if at_ is None else \
                    stream[bass.ds(at_ + (at0["M"] + s), 1)].rearrange("a p n -> (a p) n")
                e.dma_start(MRING[:, s, :], src).then_inc(expert_slot_full[s], 16)

            n_in = n_slots["A"] - 8
            for s in range(n_in + R):
                if s >= R:
                    sp.e.wait_ge(*sp.filled(last_user["A"][s - R]))
                fill(s, "A")
                if s == 0:
                    e.dma_start(w1, ts_["w1"]).then_inc(ev("w1_in"), 16)
            e.dma_start(sorted_x[0:ROWS + P, :], ts_["zero_row"].to_broadcast([ROWS + P, D])).then_inc(ev("rows_cleared"), 16)
            sp.e.wait_ge(*sp.nth("rw_out", 4))
            e.dma_start(BEFORE, ts_["before"]).then_inc(ev("before_in"), 16)
            for s in EXPERT_SLOTS:
                fill_expert(s)
            for s in range(n_in + R, n_slots["A"]):
                sp.e.wait_ge(*sp.filled(last_user["A"][s - R]))
                fill(s, "A")
            for s in range(R):
                sp.e.wait_ge(*sp.filled(last_user["A"][n_slots["A"] - R + s]))
                fill(s, "L")
            e.wait_ge(ev("sorted"), 16 * 2 * NT)
            sp.e.wait_ge(*sp.filled("ssq2"))
            e.dma_start(XG, sorted_x[0:P, :]).then_inc(ev("rows_in"), 16)
            sp.e.wait_ge(*sp.filled("pxt1"))
            e.dma_start(XG, sorted_x[P:2 * P, :]).then_inc(ev("rows_in"), 16)
            sp.sec = "M"
            with e.Fori(0, NPAIR - 1) as l:
                sp.l = l
                for s in EXPERT_SLOTS:
                    if s == 4:
                        sp.e.wait_ge(*sp.filled("xt1"))
                        e.dma_start(XG, sorted_x[bass.ds(l * P + 2 * P, P), :]).then_inc(ev("rows_in"), 16)
                    sp.e.wait_ge(*sp.filled(last_user["M"][s]))
                    fill_expert(s, (l + 1) * RM)
            sp.sec, sp.l = "B", 0
            dense(sp, sp_F)
            sp.sec = "L"
            nl = n_slots["L"]
            with e.Fori(0, L2 - 1) as l:
                sp.l = l
                for s in range(R, nl):
                    sp.e.wait_ge(*sp.filled(last_user["L"][s - R]))
                    fill(s, "L", l * nl)
                for s in range(R):
                    sp.e.wait_ge(*sp.filled(last_user["L"][nl - R + s]))
                    fill(s, "L", (l + 1) * nl)
            sp.l = L2 - 1
            for s in range(R, nl):
                sp.e.wait_ge(*sp.filled(last_user["L"][s - R]))
                fill(s, "L", (L2 - 1) * nl)

        block = ctx.enter_context(nc.Block())

        @block.sync
        def _(eng):
            sp = Engine(eng, "sp")
            sp_all(sp)

        @block.tensor
        def _(eng):
            pe = Engine(eng, "pe")
            pe_A(pe)
            pe_M(pe)
            pe_B(pe)
            pe_combine(pe)
            dense(pe, pe_F)
            pe_L(pe)

        @block.scalar
        def _(eng):
            sc = Engine(eng, "act")
            eng.dma_start(arena[0:QK, o_ + 2048:o_ + 2048 + 512].bitcast(I32), ts_["positions"].to_broadcast([QK, T])).then_inc(ev("pos_in"), 16)
            act_A(sc)
            act_M(sc)
            act_B(sc)
            dense(sc, act_F)
            act_L(sc)
            sc.e.wait_ge(*sc.nth("x_ready", 1 + L2))
            for c in range(KD):
                eng.dma_start(out[c], X[:, c, :]).then_inc(ev("out_stored"), 16)
            eng.wait_ge(ev("out_stored"), 16 * KD)

        @block.gpsimd
        def _(eng):
            po = Engine(eng, "pool")
            pool_all(po)
            pool_L(po)

        @block.vector
        def _(eng):
            dv = Engine(eng, "dve")
            dve_A(dv)
            dve_M(dv)
            dve_B(dv)
            dve_combine(dv)
            dense(dv, dve_F)
            V.memset(small[:, 59:60], 0.0).then_inc(dv.tells("x_ready"), 1)
            dve_L(dv)
        assert sorted(ended) == sorted((j, x) for j in JOB for x in ("free", "full")), \
            (set((j, x) for j in JOB for x in ("free", "full")) ^ set(ended), len(ended))
        for n, per in PER.items():
            assert posts.get(n, 0) == per or n in ("x_ready",), (n, posts.get(n), per)


PER = {"w_used": 4, "w_high": 94, "w_split": 94, "m_tanh": 2, "m_silu": 2, "f_tanh": 2, "f_comb": 2, "x_ready": 1, "Lsq": 16, "Lh": 16, "Lqsq": 8, "Lqkn": 8, "Lrot": 4, "Lrgt": 2, "Llam": 1,
       "Llexp": 1, "Lrsq": 2, "Lmax": 32, "Lexp": 32, "Lprob": 16, "Losq": 4, "Loda": 4, "Loret": 2, "Losc": 2, "Ly": 8,
       "Lfc": 22, "Lconv": 22, "Lft": 22, "Lgpad": 1, "Lbgate": 1}


def shape_constants(cols):
    f = np.float32
    i = np.arange(P)
    a, b = i[:, None], i[None, :]
    same64 = (a // 64) == (b // 64)
    c = {"ident": a == b, "ones": np.ones((P, P)), "blk64": same64,
         "upper": same64 & (a < b), "upper_eq": same64 & (a <= b), "lower": same64 & (b < a)}
    for lev in (1, 2, 4, 8, 16, 32):
        m = ((a // (2 * lev)) == (b // (2 * lev))) & (a % (2 * lev) < lev) & (b % (2 * lev) >= lev)
        c[f"lev{lev}"] = m
    c["lev1T"] = c["lev1"].T
    p = np.zeros((P, P))
    for m in range(P):
        if m % 64 < 32:
            p[m + 32, m] = -1
        else:
            p[m - 32, m] = 1
    c["perm64"] = p
    p = np.zeros((P, P))
    for m in range(64, 80):
        p[m + 16, m] = -1
        p[m, m + 16] = 1
    c["perm96"] = p
    u = np.arange(512)
    c["causal"] = np.where(u[None, :] - 384 > a, NEG, 0.0)
    lg = np.log(1.0 - 2.0 ** (-5.0 - np.arange(4, dtype=f)))
    d = u[None, :] - a
    c["ret_decay"] = np.concatenate([np.where(d >= 0, np.exp(lg[h] * np.maximum(d, 0)), 0.0) for h in range(4)], 1)
    inv = (10000.0 ** (-np.arange(32, dtype=f) / f(32))).astype(f)
    ang = (u.astype(f)[None, :] * inv[i % 32][:, None]).astype(f)
    c["ret_cos"], c["ret_sin"] = np.cos(ang.astype(np.float64)), np.sin(ang.astype(np.float64))
    c["scan_keep"] = np.broadcast_to(u % CH != 0, (P, 512))
    inv1 = (f(1.0) / (f(10000.0) ** (np.arange(16, dtype=f) / f(16)))).astype(f)
    q = np.zeros((P, 1), f)
    q[64:96, 0] = inv1[np.arange(32) % 16]
    c["inv_freq"] = q
    c["iota32"] = np.broadcast_to(np.arange(32), (P, 32))
    c["iota4"] = np.broadcast_to(np.arange(4), (P, 4))
    c["spare_row"] = ROWS + np.arange(8)[None, :] * P + a
    return np.ascontiguousarray(np.concatenate([np.broadcast_to(c[n], (P, w)).astype(f) for n, w in cols], 1))


def bucket_onehot():
    f = np.float32
    n = 511 - np.arange(512)
    large = 16 + (np.log(np.maximum(n, 1).astype(f) / f(16)) / f(np.log(8.0)) * f(16)).astype(np.int32)
    b = np.where(n < 16, n, np.minimum(large, 31))
    return np.ascontiguousarray((b[None, :] == np.arange(32)[:, None]).astype(f))


def kernel(**a):
    import concourse.bacc as _bacc
    from concourse.bass_utils import run_bass_kernel_spmd as _run

    a = {k: np.asarray(v) for k, v in a.items()}

    def cols(v):
        return v.reshape(-1, P).T

    def tiled(w):
        k, n = w.shape
        return w.reshape(k // P, P, n // P, P).transpose(2, 1, 0, 3).reshape(n // P, P, k)

    def by_tile(w):
        k, n = w.shape
        return w.reshape(k // P, P, n // P, P).transpose(2, 0, 1, 3).reshape(-1, P, P)

    def slots(t):
        return t.reshape(-1, TPS, P, P).transpose(0, 2, 1, 3).reshape(-1, P, TPS * P)

    def moving(w, per):
        k, n = w.shape
        return w.reshape(k // P // per, per, P, n).transpose(0, 2, 1, 3).reshape(-1, P, per * n)

    w = a["w_in"][0]
    n1 = QR + KVR + ROPE
    kr = np.zeros((D, P), np.float32)
    kr[:, 0:ROPE] = w[:, QR + KVR:n1]
    feat = w[:, n1:]
    win = np.concatenate([w[:, 0:QR + KVR], kr, feat[:, 3 * RW:3 * RW + P], feat[:, 3 * RW + P:], feat[:, 0:3 * RW]], 1)
    stream = [tiled(win), tiled(a["w_o"][0])]
    for e in range(NE):
        g, u = tiled(a["w_gate"][0, e]), tiled(a["w_up"][0, e])
        stream += [g[0:1], u[0:1], g[1:2], u[1:2], moving(a["w_down"][0, e], 1)]
    for l in range(L2):
        w = a["w_in_2"][l]
        o = np.cumsum([0, 512, 512, 512, 256, 256, 256, 256, 256, 256, 256, 3072])
        dq, dk, dv, rq, rk, rv, rg, sb_, sc_, sx, gt = (w[:, o[i]:o[i + 1]] for i in range(11))
        stream += [moving(dv, 2), moving(rv, 4)]
        tq, tk = tiled(dq), tiled(dk)
        for h in range(DH):
            stream += [tq[h:h + 1], tk[h:h + 1]]
        stream += [tiled(rq), tiled(rk), tiled(rg), tiled(sb_), tiled(sc_), tiled(sx)]
        gt = tiled(gt)
        br = [by_tile(a[n][l]).reshape(8, -1, P, P) for n in ("w_branch_da_2", "w_branch_ret_2", "w_branch_sc_2")]
        br = slots(np.concatenate(br, 1).reshape(-1, P, P))
        for m in range(8):
            stream += [gt[m:m + 1], gt[8 + m:9 + m], gt[16 + m:17 + m]] + ([br[m - 1:m]] if m else [])
        stream += [br[7:8]]
        stream += [tiled(a["w_out_2"][l])]
        f = tiled(a["w_ffn_in_2"][l])
        for k in range(KF):
            stream += [f[k:k + 1], f[KF + k:KF + k + 1]]
        stream += [slots(by_tile(a["w_ffn_out_2"][l]))]
    stream = np.ascontiguousarray(np.concatenate(stream, 0))

    rep = lambda v: np.broadcast_to(v.reshape(1, -1), (P, v.size))

    def pad(v):
        out = np.zeros((P, 1), np.float32)
        out[0:v.size, 0] = v
        return out

    p1 = {"g_mix": cols(a["g_mix"][0]), "g_cq": cols(a["g_cq"][0]), "g_ckv": cols(a["g_ckv"][0]),
          "g_qn": pad(a["g_qn"][0]), "g_kn": pad(a["g_kn"][0]), "g_mla_out": cols(a["g_mla_out"][0]),
          "mu": cols(a["rw_mu"][0]), "w0": cols(a["rw_w0"][0]), "a0": cols(a["rw_a0"][0]),
          "k_k": cols(a["rw_k_k"][0]), "k_a": cols(a["rw_k_a"][0]), "r_k": cols(a["rw_r_k"][0].reshape(-1)),
          "lnx_g": cols(a["rw_lnx_g"][0]), "lnx_b": cols(a["rw_lnx_b"][0]), "g_ffn": cols(a["g_ffn"][0]),
          "b_route": rep(np.concatenate([a["b_group"][0], a["b_expert"][0]])),
          "w_route": np.concatenate([a["w_group"][0], a["w_expert"][0]], 1).reshape(KD, P, 36).transpose(1, 0, 2).reshape(P, -1)}
    w1 = {"uq": a["w_uq"][0].reshape(2, P, 768).transpose(1, 0, 2).reshape(P, -1), "uk": a["w_uk"][0].reshape(P, -1),
          "uv": a["w_uv"][0].reshape(P, -1), "w2a2": np.concatenate([a["rw_w2"][0], a["rw_a2"][0]], 0), "g2": a["rw_g2"][0]}
    p2 = []
    for l in range(L2):
        li = 0.8 - 0.6 * np.exp(-0.3 * l)
        twice = lambda v: np.concatenate([v, v]).reshape(P, 1)
        d = {"g_mix": cols(a["norm_mix_g_2"][l]), "b_gate": cols(a["b_gate_2"][l]), "gq": twice(a["da_q_norm_g_2"][l]),
             "gk": twice(a["da_k_norm_g_2"][l]), "subln": a["da_subln_g_2"][l].reshape(P, 1), "retg": twice(a["ret_norm_g_2"][l]),
             "scw": cols(a["sc_conv_w_2"][l].reshape(-1)), "scb": cols(a["sc_conv_b_2"][l]), "g_ffn": cols(a["norm_ffn_g_2"][l]),
             "fcw": cols(a["ffn_conv_w_2"][l].reshape(-1)), "fcb": cols(a["ffn_conv_b_2"][l]),
             "lam_init": np.full((P, 1), li, np.float32), "one_minus": np.full((P, 1), 1.0 - li, np.float32),
             "lam": rep(a["da_lambda_2"][l])}
        p2.append(np.concatenate([d[n] for n, _ in P2_COLS], 1))
    arrays = {"x": np.ascontiguousarray(a["x"][0].T.reshape(KD, P, T).transpose(1, 0, 2)),
              "positions": np.ascontiguousarray(a["positions"]),
              "consts": shape_constants(CONST_COLS),
              "p1": np.ascontiguousarray(np.concatenate([shape_constants(EARLY_COLS)] + [p1[n] for n, _ in P1_COLS], 1)),
              "w1": np.ascontiguousarray(np.concatenate([w1[n] for n, _ in W1_COLS], 1)),
              "p2": np.ascontiguousarray(np.stack(p2)),
              "zero_row": np.zeros((1, D), np.float32),
              "before": (np.arange(P)[:, None] < np.arange(P)[None, :]).astype(np.float32),
              "rel_bias": np.ascontiguousarray(a["rel_bias_2"]), "onehot": bucket_onehot(), "stream": stream}
    nc = _bacc.Bacc("TRN2", target_bir_lowering=False, num_devices=1)
    aps = {n: nc.dram_tensor(f"in_{n}", v.shape, mybir.dt.from_np(v.dtype), kind="ExternalInput").ap() for n, v in arrays.items()}
    out = nc.dram_tensor("out", (KD, P, T), F32, kind="ExternalOutput").ap()
    build(nc, aps, out)
    r = _run(nc, [{f"in_{n}": v for n, v in arrays.items()}], core_ids=[0])
    y = r.results[0]["out"]
    return np.ascontiguousarray(y.reshape(D, T).T).reshape(1, T, D)
```
